# Optimizing a Trainium2 kernel written in Bass

```python
import jax
import jax.numpy as jnp
from jax import lax
import numpy as np
import jax, jax.numpy as jnp

D_MODEL = 2048
BATCH = 1
SEQ = 256
DEPTH = 1

HEAD_DIM = 128
A_GROUPS = 4
A_WIDTH = A_GROUPS * HEAD_DIM
CHUNK = 128
B_HEADS = 4
DILATED_PAIRS = ((128, 1), (512, 4), (2048, 16))
C_HEADS = 8
C_KV_HEADS = 2
C_GROUP = C_HEADS // C_KV_HEADS
CMP_LEN = 32
CMP_STRIDE = 16
SEL_LEN = 64
SEL_TOP = 16
WIN_LEN = 512
NSA_QBLOCK = 64
BAND_BLOCK = 128
MIX_WIDTH = A_WIDTH + (B_HEADS + C_HEADS) * HEAD_DIM
IN_SPLITS = (2 * A_WIDTH,
             3 * B_HEADS * HEAD_DIM,
             C_HEADS * HEAD_DIM,
             2 * C_KV_HEADS * HEAD_DIM,
             2 * C_KV_HEADS * HEAD_DIM,
             2 * C_KV_HEADS * HEAD_DIM,
             3 * C_HEADS)
IN_WIDTH = sum(IN_SPLITS)
N_MEM = 256
X_HEADS = 4
X_WIDTH = X_HEADS * HEAD_DIM
D_FF = 4 * D_MODEL
EPS = 1e-6
NEG_INF = -1e30


def rms_norm(x, g):
    xf = x.astype(jnp.float32)
    y = xf * lax.rsqrt(jnp.mean(xf * xf, axis=-1, keepdims=True) + EPS)
    return (y * g.astype(jnp.float32)).astype(x.dtype)

def layer_norm(x, g, b):
    xf = x.astype(jnp.float32)
    xc = xf - jnp.mean(xf, axis=-1, keepdims=True)
    y = xc * lax.rsqrt(jnp.mean(xc * xc, axis=-1, keepdims=True) + EPS)
    return (y * g.astype(jnp.float32) + b.astype(jnp.float32)).astype(x.dtype)

def banded_attention(q, k, v, max_dist):
    bsz, ng, nr, L, hd = q.shape
    blk = BAND_BLOCK
    nprev = -(-max_dist // blk)
    nb = -(-L // blk)
    pad = nb * blk - L
    qb = jnp.pad(q, ((0, 0), (0, 0), (0, 0), (0, pad), (0, 0))).reshape(bsz, ng, nr, nb, blk, hd)

    def windows(t):
        tb = jnp.pad(t, ((0, 0), (0, 0), (nprev * blk, pad), (0, 0))).reshape(bsz, ng, nb + nprev, blk, hd)
        return jnp.concatenate([tb[:, :, i:i + nb] for i in range(nprev + 1)], axis=3)

    kw, vw = windows(k), windows(v)
    s = jnp.einsum('bgrnqd,bgnkd->bgrnqk', qb, kw).astype(jnp.float32) * (hd ** -0.5)
    qpos = jnp.arange(nb)[:, None] * blk + jnp.arange(blk)[None, :]
    kpos = (jnp.arange(nb)[:, None] - nprev) * blk + jnp.arange((nprev + 1) * blk)[None, :]
    dist = qpos[:, :, None] - kpos[:, None, :]
    mask = (dist >= 0) & (dist <= max_dist) & (kpos[:, None, :] >= 0)
    s = jnp.where(mask, s, NEG_INF)
    m = jnp.max(s, axis=-1, keepdims=True)
    e = jnp.exp(s - m)
    den = jnp.sum(e, axis=-1, keepdims=True)
    o = jnp.einsum('bgrnqk,bgnkd->bgrnqd', (e / den).astype(v.dtype), vw)
    lse = (m + jnp.log(den))[..., 0]
    o = o.reshape(bsz, ng, nr, nb * blk, hd)[:, :, :, :L]
    lse = lse.reshape(bsz, ng, nr, nb * blk)[:, :, :, :L]
    return o, lse

def spatial_gating(uv, ln_g, ln_b, w_s, b_s):
    bsz, S, _ = uv.shape
    u, v = jnp.split(jax.nn.gelu(uv), 2, axis=-1)
    v = layer_norm(v, ln_g, ln_b).reshape(bsz, S // CHUNK, CHUNK, A_GROUPS, HEAD_DIM)
    w = w_s * jnp.tril(jnp.ones((CHUNK, CHUNK), w_s.dtype))
    sv = jnp.einsum('gts,bcsgh->bctgh', w, v) + b_s.T[:, :, None]
    return u * sv.reshape(bsz, S, A_WIDTH)

def dilated_attention(q, k, v):
    bsz, nh, S, hd = q.shape
    outs, lses = [], []
    for window, d in DILATED_PAIRS:
        def fold(t):
            return t.reshape(bsz, nh, S // d, d, hd).transpose(0, 1, 3, 2, 4).reshape(bsz, nh * d, S // d, hd)
        o, l = banded_attention(fold(q)[:, :, None], fold(k), fold(v), window // d)
        outs.append(o[:, :, 0].reshape(bsz, nh, d, S // d, hd).transpose(0, 1, 3, 2, 4).reshape(bsz, nh, S, hd))
        lses.append(l[:, :, 0].reshape(bsz, nh, d, S // d).transpose(0, 1, 3, 2).reshape(bsz, nh, S))
    w = jax.nn.softmax(jnp.stack(lses), axis=0)
    o = jnp.einsum('pbhs,pbhsd->bhsd', w.astype(q.dtype), jnp.stack(outs))
    return o.transpose(0, 2, 1, 3).reshape(bsz, S, nh * hd)

def compress_blocks(kraw, pos, w1, w2):
    bsz, ng, S, hd = kraw.shape
    sub = kraw.reshape(bsz, ng, S // CMP_STRIDE, CMP_STRIDE, hd)
    blocks = jnp.concatenate([sub[:, :, :-1], sub[:, :, 1:]], axis=3) + pos
    n_c = blocks.shape[2]
    h = jax.nn.gelu(blocks.reshape(bsz, ng, n_c, CMP_LEN * hd) @ w1)
    return h @ w2

def nsa_attention(q, kv_cmp, kv_slc, kv_win, gates, cmp_pos, ck_w1, ck_w2, cv_w1, cv_w2):
    bsz, ng, nr, S, hd = q.shape
    scale = hd ** -0.5
    k_c = compress_blocks(kv_cmp[0], cmp_pos, ck_w1, ck_w2)
    v_c = compress_blocks(kv_cmp[1], cmp_pos, cv_w1, cv_w2)
    n_c = k_c.shape[2]
    n_sel = S // SEL_LEN
    n_top = min(SEL_TOP, n_sel)
    k_s = kv_slc[0].reshape(bsz, ng, n_sel, SEL_LEN, hd)
    v_s = kv_slc[1].reshape(bsz, ng, n_sel, SEL_LEN, hd)
    c_start = np.arange(n_c) * CMP_STRIDE
    s_start = np.arange(n_sel) * SEL_LEN
    overlap = jnp.asarray(((c_start[:, None] <= s_start[None, :] + SEL_LEN - 1)
                           & (c_start[:, None] + CMP_LEN - 1 >= s_start[None, :])).astype(np.float32))
    c_end = jnp.arange(n_c) * CMP_STRIDE + CMP_LEN - 1
    sel_idx = jnp.arange(n_sel)
    b_idx = jnp.arange(bsz)[:, None, None, None]
    g_idx = jnp.arange(ng)[None, :, None, None]
    nqb = S // NSA_QBLOCK
    q_blocks = q.reshape(bsz, ng, nr, nqb, NSA_QBLOCK, hd).transpose(3, 0, 1, 2, 4, 5)

    def block_step(args):
        qb, bi = args
        t = bi * NSA_QBLOCK + jnp.arange(NSA_QBLOCK)
        valid_c = c_end[None, :] <= t[:, None]
        s_c = jnp.einsum('bgrqd,bgnd->bgrqn', qb, k_c).astype(jnp.float32) * scale
        p_c = jax.nn.softmax(jnp.where(valid_c, s_c, NEG_INF), axis=-1) * valid_c
        o_c = jnp.einsum('bgrqn,bgnd->bgrqd', p_c.astype(v_c.dtype), v_c)
        imp = jnp.einsum('bgrqn,nj->bgqj', p_c, overlap)
        jt = t // SEL_LEN
        forced = (sel_idx[None] == 0) | (sel_idx[None] == jt[:, None]) | (sel_idx[None] == jt[:, None] - 1)
        valid_s = sel_idx[None] * SEL_LEN <= t[:, None]
        score = jnp.where(forced, 1e4, jnp.where(valid_s, imp, -1.0))
        _, idx = lax.top_k(score, n_top)
        ks = k_s[b_idx, g_idx, idx]
        vs = v_s[b_idx, g_idx, idx]
        kpos = idx[..., None] * SEL_LEN + jnp.arange(SEL_LEN)
        mask_s = (kpos <= t[None, None, :, None, None])[:, :, None]
        s_s = jnp.einsum('bgrqd,bgqnkd->bgrqnk', qb, ks).astype(jnp.float32) * scale
        s_s = jnp.where(mask_s, s_s, NEG_INF).reshape(bsz, ng, nr, NSA_QBLOCK, n_top * SEL_LEN)
        p_s = jax.nn.softmax(s_s, axis=-1).reshape(bsz, ng, nr, NSA_QBLOCK, n_top, SEL_LEN)
        o_s = jnp.einsum('bgrqnk,bgqnkd->bgrqd', p_s.astype(vs.dtype), vs)
        return o_c, o_s

    o_c, o_s = lax.map(block_step, (q_blocks, jnp.arange(nqb)))
    o_c = o_c.transpose(1, 2, 3, 0, 4, 5).reshape(bsz, ng, nr, S, hd)
    o_s = o_s.transpose(1, 2, 3, 0, 4, 5).reshape(bsz, ng, nr, S, hd)
    o_w, _ = banded_attention(q, kv_win[0], kv_win[1], WIN_LEN - 1)
    g = jax.nn.sigmoid(gates.astype(jnp.float32)).reshape(bsz, S, ng, nr, 3)
    g = g.transpose(4, 0, 2, 3, 1)[..., None].astype(q.dtype)
    o = g[0] * o_c + g[1] * o_s + g[2] * o_w
    return o.transpose(0, 3, 1, 2, 4).reshape(bsz, S, ng * nr * hd)

def first_inputs(seed: int = 0) -> dict:
    key = jax.random.key(seed)
    ks = jax.random.split(key, 24)
    f32 = jnp.float32

    def normal(k, shape, scale):
        return jax.random.normal(k, shape, f32) * scale

    def gain(k, shape):
        return 1.0 + normal(k, shape, 0.02)

    L = DEPTH
    return {
        'x': normal(ks[0], (BATCH, SEQ, D_MODEL), 1.0),
        'mem': normal(ks[1], (BATCH, N_MEM, D_MODEL), 1.0),
        'norm_mix': gain(ks[2], (L, D_MODEL)),
        'w_in': normal(ks[3], (L, D_MODEL, IN_WIDTH), D_MODEL ** -0.5),
        'gmlp_ln_g': gain(ks[4], (L, A_WIDTH)),
        'gmlp_ln_b': normal(ks[5], (L, A_WIDTH), 0.02),
        'gmlp_w_s': normal(ks[6], (L, A_GROUPS, CHUNK, CHUNK), CHUNK ** -0.5),
        'gmlp_b_s': gain(ks[7], (L, A_GROUPS, CHUNK)),
        'cmp_pos': normal(ks[8], (L, CMP_LEN, HEAD_DIM), 0.02),
        'cmp_k_w1': normal(ks[9], (L, CMP_LEN * HEAD_DIM, HEAD_DIM), (CMP_LEN * HEAD_DIM) ** -0.5),
        'cmp_k_w2': normal(ks[10], (L, HEAD_DIM, HEAD_DIM), HEAD_DIM ** -0.5),
        'cmp_v_w1': normal(ks[11], (L, CMP_LEN * HEAD_DIM, HEAD_DIM), (CMP_LEN * HEAD_DIM) ** -0.5),
        'cmp_v_w2': normal(ks[12], (L, HEAD_DIM, HEAD_DIM), HEAD_DIM ** -0.5),
        'w_out': normal(ks[13], (L, MIX_WIDTH, D_MODEL), 0.5 * MIX_WIDTH ** -0.5),
        'norm_xattn': gain(ks[14], (L, D_MODEL)),
        'norm_mem': gain(ks[15], (L, D_MODEL)),
        'xattn_wq': normal(ks[16], (L, D_MODEL, X_WIDTH), D_MODEL ** -0.5),
        'xattn_wkv': normal(ks[17], (L, D_MODEL, 2 * X_WIDTH), D_MODEL ** -0.5),
        'xattn_wo': normal(ks[18], (L, X_WIDTH, D_MODEL), 0.5 * X_WIDTH ** -0.5),
        'norm_mlp': gain(ks[19], (L, D_MODEL)),
        'w_up': normal(ks[20], (L, D_MODEL, D_FF), D_MODEL ** -0.5),
        'w_down': normal(ks[21], (L, D_FF, D_MODEL), 0.5 * D_FF ** -0.5),
        'final_norm': gain(ks[22], (D_MODEL,)),
    }

def first_block(x, mem, norm_mix, w_in, gmlp_ln_g, gmlp_ln_b, gmlp_w_s, gmlp_b_s, cmp_pos,
              cmp_k_w1, cmp_k_w2, cmp_v_w1, cmp_v_w2, w_out, norm_xattn, norm_mem,
              xattn_wq, xattn_wkv, xattn_wo, norm_mlp, w_up, w_down, final_norm):
    bsz, S, _ = x.shape
    n_mem = mem.shape[1]
    split_at = [int(i) for i in np.cumsum(IN_SPLITS)[:-1]]
    x_scale = HEAD_DIM ** -0.5
    for l in range(DEPTH):
        h = rms_norm(x, norm_mix[l])
        z = h @ w_in[l]
        z_a, z_b, z_cq, z_ckv_c, z_ckv_s, z_ckv_w, z_cg = jnp.split(z, split_at, axis=-1)
        out_a = spatial_gating(z_a, gmlp_ln_g[l], gmlp_ln_b[l], gmlp_w_s[l], gmlp_b_s[l])
        qkv_b = z_b.reshape(bsz, S, 3, B_HEADS, HEAD_DIM).transpose(2, 0, 3, 1, 4)
        out_b = dilated_attention(qkv_b[0], qkv_b[1], qkv_b[2])
        q_c = z_cq.reshape(bsz, S, C_KV_HEADS, C_GROUP, HEAD_DIM).transpose(0, 2, 3, 1, 4)

        def kv_heads(t):
            return t.reshape(bsz, S, 2, C_KV_HEADS, HEAD_DIM).transpose(2, 0, 3, 1, 4)

        out_c = nsa_attention(q_c, kv_heads(z_ckv_c), kv_heads(z_ckv_s), kv_heads(z_ckv_w), z_cg,
                              cmp_pos[l], cmp_k_w1[l], cmp_k_w2[l], cmp_v_w1[l], cmp_v_w2[l])
        x = x + jnp.concatenate([out_a, out_b, out_c], axis=-1) @ w_out[l]
        h = rms_norm(x, norm_xattn[l])
        m = rms_norm(mem, norm_mem[l])
        q = (h @ xattn_wq[l]).reshape(bsz, S, X_HEADS, HEAD_DIM)
        kv = (m @ xattn_wkv[l]).reshape(bsz, n_mem, 2, X_HEADS, HEAD_DIM)
        s = jnp.einsum('bshd,bmhd->bhsm', q, kv[:, :, 0]).astype(jnp.float32) * x_scale
        p = jax.nn.softmax(s, axis=-1).astype(x.dtype)
        o = jnp.einsum('bhsm,bmhd->bshd', p, kv[:, :, 1]).reshape(bsz, S, X_WIDTH)
        x = x + o @ xattn_wo[l]
        h = rms_norm(x, norm_mlp[l])
        x = x + jnp.square(jax.nn.relu(h @ w_up[l])) @ w_down[l]
    return rms_norm(x, final_norm)


GRID_W = 64
CTX_LEN = 256

N_HEADS = 4
D_KEY = D_MODEL // 2
D_VAL = D_MODEL
HEAD_K = D_KEY // N_HEADS
HEAD_V = D_VAL // N_HEADS
GATE_RANK = 16
GATE_NORM = 16.0
CHUNK_2 = 64

POOL_WINDOWS = (2, 4, 8, 16)
D_POOL = D_MODEL // 2
POOL_GROUP = D_POOL // len(POOL_WINDOWS)

D_FF_2 = ((8 * D_MODEL + 3 * 256 - 1) // (3 * 256)) * 256

N_BRANCH = 2
N_MOD = 6
DEEPNORM_ALPHA = (2.0 * DEPTH) ** 0.25
DEEPNORM_BETA = (8.0 * DEPTH) ** -0.25
LN_EPS = 1e-5
RMS_EPS = 1e-6

PROJ_WIDTHS = (D_KEY, D_KEY, D_VAL, D_VAL, 2 * GATE_RANK, D_POOL, N_BRANCH * D_MODEL)
D_PROJ = sum(PROJ_WIDTHS)
SPLIT_POINTS = tuple(int(s) for s in np.cumsum(PROJ_WIDTHS)[:-1])


def _layer_norm(x, gain, bias):
    xf = x.astype(jnp.float32)
    mu = jnp.mean(xf, axis=-1, keepdims=True)
    var = jnp.mean(jnp.square(xf - mu), axis=-1, keepdims=True)
    y = (xf - mu) * lax.rsqrt(var + LN_EPS)
    return (y * gain + bias).astype(x.dtype)

def _modulation(cond, w_ada, b_ada):
    return jnp.split(jax.nn.silu(cond) @ w_ada + b_ada, N_MOD, axis=-1)

def _heads(t, head_dim):
    b, l, _ = t.shape
    return t.reshape(b, l, -1, head_dim).transpose(0, 2, 1, 3)

def _split_proj(proj, w_decay_up, b_decay_up):
    q, k, v, g, a_lr, p, bg = jnp.split(proj, SPLIT_POINTS, axis=-1)
    q = _heads(q * HEAD_K ** -0.5, HEAD_K)
    k = _heads(k, HEAD_K)
    v = _heads(v, HEAD_V)
    log_decay = []
    for d in range(2):
        z = a_lr[..., d * GATE_RANK:(d + 1) * GATE_RANK] @ w_decay_up[d] + b_decay_up[d]
        log_decay.append(_heads(jax.nn.log_sigmoid(z.astype(jnp.float32)) / GATE_NORM, HEAD_K))
    return q, k, v, log_decay[0], log_decay[1], g, p, bg

def _gla_chunked(q, k, v, log_a, s0):
    b_, h_, l_, _ = q.shape
    n = l_ // CHUNK_2

    def chunks(t):
        return t.reshape(b_, h_, n, CHUNK_2, t.shape[-1]).astype(jnp.float32)

    q, k, v, log_a = chunks(q), chunks(k), chunks(v), chunks(log_a)
    cum = jnp.cumsum(log_a, axis=3)
    ref = cum[:, :, :, CHUNK_2 // 2 - 1:CHUNK_2 // 2]
    q_in = q * jnp.exp(cum - ref)
    k_in = k * jnp.exp(ref - cum)
    scores = jnp.einsum('bhnid,bhnjd->bhnij', q_in, k_in)
    mask = jnp.tril(jnp.ones((CHUNK_2, CHUNK_2), dtype=bool))
    scores = jnp.where(mask, scores, 0.0)
    o_intra = jnp.einsum('bhnij,bhnjv->bhniv', scores, v)
    last = cum[:, :, :, -1:]
    q_inter = q * jnp.exp(cum)
    k_state = k * jnp.exp(last - cum)
    decay_chunk = jnp.exp(last[:, :, :, 0, :])
    xs = (jnp.moveaxis(q_inter, 2, 0), jnp.moveaxis(k_state, 2, 0),
          jnp.moveaxis(v, 2, 0), jnp.moveaxis(decay_chunk, 2, 0))

    def step(state, inp):
        qc, kc, vc, dc = inp
        o = jnp.einsum('bhid,bhdv->bhiv', qc, state)
        state = dc[..., None] * state + jnp.einsum('bhjd,bhjv->bhdv', kc, vc)
        return state, o

    s_final, o_inter = lax.scan(step, s0.astype(jnp.float32), xs)
    o = o_intra + jnp.moveaxis(o_inter, 0, 2)
    return o.reshape(b_, h_, l_, HEAD_V), s_final

def _gla_two_way(q, k, v, la_fwd, la_bwd, s0_fwd, s0_bwd):
    flip = lambda t: jnp.flip(t, axis=2)
    o_f, s_f = _gla_chunked(q, k, v, la_fwd, s0_fwd)
    o_b, s_b = _gla_chunked(flip(q), flip(k), flip(v), flip(la_bwd), s0_bwd)
    return o_f + flip(o_b), s_f, s_b

def _box_mean(t, axis, window):
    n = t.shape[axis]
    lo = window // 2
    hi = window - lo - 1
    cs = jnp.cumsum(t.astype(jnp.float32), axis=axis)
    zero = jnp.zeros_like(lax.slice_in_dim(cs, 0, 1, axis=axis))
    cs = jnp.concatenate([zero, cs], axis=axis)
    idx = jnp.arange(n)
    upper = jnp.minimum(idx + hi + 1, n)
    lower = jnp.maximum(idx - lo, 0)
    total = jnp.take(cs, upper, axis=axis) - jnp.take(cs, lower, axis=axis)
    shape = [1] * t.ndim
    shape[axis] = n
    count = (upper - lower).astype(jnp.float32).reshape(shape)
    return (total / count).astype(t.dtype)

def _pool_branch(p, rows, w_pool_group, pool_scale, w_pool_out):
    outs = []
    for i, w in enumerate(POOL_WINDOWS):
        pg = p[..., i * POOL_GROUP:(i + 1) * POOL_GROUP]
        if rows is None:
            mean = _box_mean(pg, 1, w)
        else:
            b, l, ch = pg.shape
            img = pg.reshape(b, rows, GRID_W, ch)
            mean = _box_mean(_box_mean(img, 2, w), 1, w).reshape(b, l, ch)
        outs.append((mean - pg) @ w_pool_group[i])
    return (jnp.concatenate(outs, axis=-1) * pool_scale) @ w_pool_out

def _gla_output(o, g, gain, w_gla_out):
    of = o.transpose(0, 2, 1, 3)
    of = of * lax.rsqrt(jnp.mean(of * of, axis=-1, keepdims=True) + RMS_EPS)
    b, l = of.shape[:2]
    of = of.reshape(b, l, D_VAL).astype(g.dtype) * gain
    return (of * jax.nn.silu(g)) @ w_gla_out

def _merge(o, g, p, bg, rows, gla_norm_gain, w_gla_out, w_pool_group, pool_scale, w_pool_out, w_out):
    y_gla = _gla_output(o, g, gla_norm_gain, w_gla_out)
    y_pool = _pool_branch(p, rows, w_pool_group, pool_scale, w_pool_out)
    gate_gla, gate_pool = jnp.split(jax.nn.sigmoid(bg), N_BRANCH, axis=-1)
    return (gate_gla * y_gla + gate_pool * y_pool) @ w_out

def _token_mixer(h_lat, h_ctx, rows, ctx_out, w_in, w_decay_up, b_decay_up, gla_norm_gain,
                 w_pool_group, pool_scale, w_gla_out, w_pool_out, w_out):
    q_c, k_c, v_c, laf_c, lab_c, g_c, p_c, bg_c = _split_proj(h_ctx @ w_in, w_decay_up, b_decay_up)
    q_l, k_l, v_l, laf_l, lab_l, g_l, p_l, bg_l = _split_proj(h_lat @ w_in, w_decay_up, b_decay_up)
    s0 = jnp.zeros((h_lat.shape[0], N_HEADS, HEAD_K, HEAD_V), jnp.float32)
    o_c, s_fwd, s_bwd = _gla_two_way(q_c, k_c, v_c, laf_c, lab_c, s0, s0)
    o_l, _, _ = _gla_two_way(q_l, k_l, v_l, laf_l, lab_l, s_fwd, s_bwd)
    y_lat = _merge(o_l, g_l, p_l, bg_l, rows, gla_norm_gain, w_gla_out, w_pool_group,
                   pool_scale, w_pool_out, w_out)
    y_ctx = None
    if ctx_out:
        y_ctx = _merge(o_c, g_c, p_c, bg_c, None, gla_norm_gain, w_gla_out, w_pool_group,
                       pool_scale, w_pool_out, w_out)
    return y_lat, y_ctx

def _swiglu(h, w_ffn_in, w_ffn_out):
    gate, up = jnp.split(h @ w_ffn_in, 2, axis=-1)
    return (jax.nn.silu(gate) * up) @ w_ffn_out

def second_inputs(seed: int = 0) -> dict:
    key = jax.random.key(seed)
    ks = jax.random.split(key, 24)
    f32 = jnp.float32
    nrm = lambda k, shape, s: jax.random.normal(k, shape, f32) * s
    L = DEPTH
    return {
        "x": nrm(ks[0], (BATCH, SEQ, D_MODEL), 1.0),
        "c": nrm(ks[1], (BATCH, D_MODEL), 1.0),
        "ctx": nrm(ks[2], (BATCH, CTX_LEN, D_MODEL), 1.0),
        "c_ctx": nrm(ks[3], (D_MODEL,), 1.0),
        "w_ada": nrm(ks[4], (L, D_MODEL, N_MOD * D_MODEL), 0.5 * D_MODEL ** -0.5),
        "b_ada": nrm(ks[5], (L, N_MOD * D_MODEL), 0.02),
        "w_in": nrm(ks[6], (L, D_MODEL, D_PROJ), D_MODEL ** -0.5),
        "w_decay_up": nrm(ks[7], (L, 2, GATE_RANK, D_KEY), GATE_RANK ** -0.5),
        "b_decay_up": nrm(ks[8], (L, 2, D_KEY), 0.1),
        "gla_norm_gain": 1.0 + nrm(ks[9], (L, D_VAL), 0.1),
        "w_pool_group": nrm(ks[10], (L, len(POOL_WINDOWS), POOL_GROUP, POOL_GROUP), POOL_GROUP ** -0.5),
        "pool_scale": 1.0 + nrm(ks[11], (L, D_POOL), 0.1),
        "w_gla_out": nrm(ks[12], (L, D_VAL, D_MODEL), D_VAL ** -0.5),
        "w_pool_out": nrm(ks[13], (L, D_POOL, D_MODEL), D_POOL ** -0.5),
        "w_out": nrm(ks[14], (L, D_MODEL, D_MODEL), DEEPNORM_BETA * D_MODEL ** -0.5),
        "ln_mix_gain": 1.0 + nrm(ks[15], (L, D_MODEL), 0.1),
        "ln_mix_bias": nrm(ks[16], (L, D_MODEL), 0.02),
        "w_ffn_in": nrm(ks[17], (L, D_MODEL, 2 * D_FF_2), D_MODEL ** -0.5),
        "w_ffn_out": nrm(ks[18], (L, D_FF_2, D_MODEL), DEEPNORM_BETA * D_FF_2 ** -0.5),
        "ln_ffn_gain": 1.0 + nrm(ks[19], (L, D_MODEL), 0.1),
        "ln_ffn_bias": nrm(ks[20], (L, D_MODEL), 0.02),
    }

def second_block(x, c, ctx, c_ctx, w_ada, b_ada, w_in, w_decay_up, b_decay_up, gla_norm_gain,
              w_pool_group, pool_scale, w_gla_out, w_pool_out, w_out, ln_mix_gain, ln_mix_bias,
              w_ffn_in, w_ffn_out, ln_ffn_gain, ln_ffn_bias):
    rows = x.shape[1] // GRID_W
    for layer in range(DEPTH):
        ctx_out = layer < DEPTH - 1
        sh_m, sc_m, gt_m, sh_f, sc_f, gt_f = _modulation(c[:, None, :], w_ada[layer], b_ada[layer])
        csh_m, csc_m, cgt_m, csh_f, csc_f, cgt_f = _modulation(c_ctx, w_ada[layer], b_ada[layer])
        h_lat = x * (1.0 + sc_m) + sh_m
        h_ctx = ctx * (1.0 + csc_m) + csh_m
        mix_lat, mix_ctx = _token_mixer(h_lat, h_ctx, rows, ctx_out, w_in[layer], w_decay_up[layer],
                                        b_decay_up[layer], gla_norm_gain[layer], w_pool_group[layer],
                                        pool_scale[layer], w_gla_out[layer], w_pool_out[layer], w_out[layer])
        x = _layer_norm(DEEPNORM_ALPHA * x + gt_m * mix_lat, ln_mix_gain[layer], ln_mix_bias[layer])
        ffn_lat = _swiglu(x * (1.0 + sc_f) + sh_f, w_ffn_in[layer], w_ffn_out[layer])
        x = _layer_norm(DEEPNORM_ALPHA * x + gt_f * ffn_lat, ln_ffn_gain[layer], ln_ffn_bias[layer])
        if ctx_out:
            ctx = _layer_norm(DEEPNORM_ALPHA * ctx + cgt_m * mix_ctx, ln_mix_gain[layer], ln_mix_bias[layer])
            ffn_ctx = _swiglu(ctx * (1.0 + csc_f) + csh_f, w_ffn_in[layer], w_ffn_out[layer])
            ctx = _layer_norm(DEEPNORM_ALPHA * ctx + cgt_f * ffn_ctx, ln_ffn_gain[layer], ln_ffn_bias[layer])
    return x


def setup_inputs(seed=0):
    out = dict(first_inputs(seed))
    for name, value in second_inputs(seed + 1).items():
        if name != "x":
            out[name + "_2"] = value
    return out


def reference(
    x, mem, norm_mix, w_in, gmlp_ln_g, gmlp_ln_b, gmlp_w_s, gmlp_b_s, cmp_pos, cmp_k_w1,
    cmp_k_w2, cmp_v_w1, cmp_v_w2, w_out, norm_xattn, norm_mem, xattn_wq, xattn_wkv, xattn_wo,
    norm_mlp, w_up, w_down, final_norm, c_2, ctx_2, c_ctx_2, w_ada_2, b_ada_2, w_in_2,
    w_decay_up_2, b_decay_up_2, gla_norm_gain_2, w_pool_group_2, pool_scale_2, w_gla_out_2,
    w_pool_out_2, w_out_2, ln_mix_gain_2, ln_mix_bias_2, w_ffn_in_2, w_ffn_out_2, ln_ffn_gain_2,
    ln_ffn_bias_2,
):
    x = first_block(
        x, mem, norm_mix, w_in, gmlp_ln_g, gmlp_ln_b, gmlp_w_s, gmlp_b_s, cmp_pos, cmp_k_w1,
        cmp_k_w2, cmp_v_w1, cmp_v_w2, w_out, norm_xattn, norm_mem, xattn_wq, xattn_wkv,
        xattn_wo, norm_mlp, w_up, w_down, final_norm,
    )
    return second_block(
        x, c_2, ctx_2, c_ctx_2, w_ada_2, b_ada_2, w_in_2, w_decay_up_2, b_decay_up_2,
        gla_norm_gain_2, w_pool_group_2, pool_scale_2, w_gla_out_2, w_pool_out_2, w_out_2,
        ln_mix_gain_2, ln_mix_bias_2, w_ffn_in_2, w_ffn_out_2, ln_ffn_gain_2, ln_ffn_bias_2,
    )


_drawn_inputs = setup_inputs


def setup_inputs(seed=0):
    import zlib

    import numpy as np

    out = dict(_drawn_inputs(seed))
    spreads = {}
    factors = {'norm_mix': 8.0,
     'gmlp_ln_g': 8.0,
     'gmlp_ln_b': 8.0,
     'gmlp_b_s': 8.0,
     'cmp_pos': 22.137,
     'norm_xattn': 8.0,
     'norm_mem': 8.0,
     'norm_mlp': 4.872,
     'final_norm': 2.823,
     'ctx_2': 6.215,
     'c_ctx_2': 8.0,
     'b_ada_2': 5.082,
     'w_decay_up_2': 5.117,
     'b_decay_up_2': 8.0,
     'gla_norm_gain_2': 8.0,
     'pool_scale_2': 6.535,
     'ln_mix_bias_2': 2.759,
     'ln_ffn_bias_2': 2.81}
    for name, (base, spread) in spreads.items():
        noise = np.random.default_rng([zlib.crc32(name.encode()), seed]).standard_normal(out[name].shape)
        drawn = base * np.exp(spread * noise) if base else spread * noise
        out[name] = jnp.asarray(drawn.astype(out[name].dtype))
    for name, factor in factors.items():
        out[name] = (out[name] * factor).astype(out[name].dtype)
    return out
```

```python
from contextlib import ExitStack

import numpy as np

import concourse.bass as bass
from concourse import mybir

F32 = mybir.dt.float32
F32R = mybir.dt.float32r
U32 = mybir.dt.uint32
ALU = mybir.AluOpType
ACT = mybir.ActivationFunctionType
AX = mybir.AxisListType.X

P = 128
S = 256
D = 2048
KT = D // P
CH = 2048
SCALE = 128 ** -0.5
ALPHA = 2.0 ** 0.25
NEG = -1e30
FFT = 44

PLAIN = ("ck", "cv")
NW, NR = 5, 2

PAR = {}
_at = 0
for _n, _w in (("norm_mix", 16), ("norm_xattn", 16), ("norm_mem", 16), ("norm_mlp", 16), ("final_norm", 16),
               ("b_ada", 96), ("gla_gain", 16), ("pool_scale", 8), ("lnm_g", 16), ("lnm_b", 16),
               ("lnf_g", 16), ("lnf_b", 16), ("b_decay", 16), ("c", 16), ("c_ctx", 16)):
    PAR[_n] = (_at, _at + _w)
    _at += _w
NPAR = _at

CA = {}
_at = 0
for _n, _w in (("dil", 512), ("cau", 512), ("bcmp", 32), ("vcmp", 32), ("ln_g", 512), ("ln_b", 512),
               ("b_s", 512), ("w_s", 512), ("tri", 128), ("pos", 32), ("ckw2", 128), ("cvw2", 128)):
    CA[_n] = (_at, _at + _w)
    _at += _w
NCA = _at

CG = {}
_at = 0
for _n, _w in (("scan", 512), ("scan_all", 512), ("decay", 1024)):
    CG[_n] = (_at, _at + _w)
    _at += _w
NCG = _at
CP = {"mean": (0, 2048), "group": (2048, 4096)}
NCP = 4096


class Queue:

    def __init__(self, engine, sem):
        self.engine, self.sem, self.n, self.seen = engine, sem, 0, {}

    def wait(self, waits):
        most = {}
        for w in flat(waits):
            key = w[0].name
            if w[1] > self.seen.get(key, 0) and w[1] > most.get(key, (0, 0))[1]:
                most[key] = w
        for key, (sem, value) in most.items():
            self.seen[key] = value
            self.engine.wait_ge(sem, value)

    def __call__(self, make, *waits, mark=True):
        self.wait(waits)
        ins = make(self.engine)
        if not mark:
            return None
        self.n += 1
        ins.then_inc(self.sem, 1)
        return (self.sem, self.n)

    def dma(self, out, in_, load, *waits):
        self.wait(waits)
        load.n += 16
        self.engine.dma_start(out, in_).then_inc(load.sem, 16)
        return (load.sem, load.n)


def flat(x):
    if x is None:
        return []
    if isinstance(x, tuple) and len(x) == 2 and isinstance(x[1], int):
        return [x]
    return [w for y in x for w in flat(y)]


class Load:

    def __init__(self, sem):
        self.sem, self.n = sem, 0

    def all(self):
        return (self.sem, self.n)


class Place:

    def __init__(self, ap):
        self.ap, self.free = ap, []


class Ring:
    def __init__(self, places):
        self.places, self.i = places, 0

    def next(self):
        self.i += 1
        return self.places[(self.i - 1) % len(self.places)]


def program(nc, io, order):
    st = ExitStack()
    found = []
    with st:
        def sem(name):
            return st.enter_context(nc.semaphore(name))

        def sb(name, width, dt=F32):
            return st.enter_context(nc.sbuf_tensor(name, [P, width], dt))

        PE, DV, AC, PO, SP = (Queue(e, sem(n)) for e, n in (
            (nc.tensor, "s_pe"), (nc.vector, "s_dve"), (nc.scalar, "s_act"), (nc.gpsimd, "s_pool"), (nc.sync, "s_sp")))
        everyone = (PE, DV, AC, PO)

        def now():
            return [(q.sem, q.n) for q in everyone if q.n]

        RW = sb("RW", NW * CH)
        RH = sb("RH", NR * CH, F32R)
        RL = sb("RL", NR * CH, F32R)
        X = sb("X", KT * S)
        AH = sb("AH", KT * S, F32R)
        AL = sb("AL", KT * S, F32R)
        C = sb("C", 256 + NPAR)
        MODT = sb("MODT", 96 + 32)
        RS = sb("RS", 3 * 256)
        SM = sb("SM", 128)
        over = ExitStack()
        HH = over.enter_context(nc.sbuf_tensor("HH", [P, 24 * S], F32R))
        HL = over.enter_context(nc.sbuf_tensor("HL", [P, 24 * S], F32R))
        over.close()
        NE = 8000
        G = sb("G", 48 * S + NE)
        E0 = 48 * S
        banks = [Place(st.enter_context(nc.psum_tensor(f"b{i}", [P, 512], F32))) for i in range(8)]
        pairs = Ring([Place((banks[0], banks[1])), Place((banks[2], banks[3]))])
        misc = Ring(banks[4:8])

        def g(at, n, **split):
            ap = G[:, at:at + n]
            if split:
                (keys, sizes), = [(k, v) for k, v in split.items()]
            return ap

        ident, ones = C[:, 0:128], C[:, 128:256]

        def par(name, i=None):
            a, b = PAR[name]
            return C[:, 256 + a:256 + b] if i is None else C[:, 256 + a + i:256 + a + i + 1]

        def mod(i, kt):
            return MODT[:, 16 * i + kt:16 * i + kt + 1]

        def cmod(i, kt):
            return MODT[:, 96 + 16 * i + kt:96 + 16 * i + kt + 1]

        w_sems = [Load(sem(f"s_w{i}")) for i in range(NW)]
        loaded, ready_at, prepared = {}, {}, [0]
        gem_used = []
        split_of = {}
        state = {"gemm": 0, "dma": 0}
        side = {}

        def send(j, waits):
            if order is None or j >= len(order):
                return
            name, i = order[j]
            k = j % NW
            SP.dma(RW[:, k * CH:(k + 1) * CH], io["w_" + name][i], w_sems[k], waits)
            loaded[j] = w_sems[k].all()

        def prepare():
            j = prepared[0]
            prepared[0] += 1
            name, i = order[j]
            k = j % NW
            w = RW[:, k * CH:(k + 1) * CH]
            if name in side:
                done = side[name](i, w, loaded[j])
            else:
                n = state["gemm"]
                state["gemm"] += 1
                s = n % NR
                split_of[j] = n
                free = gem_used[n - NR] if n >= NR else None
                hi, lo = RH[:, s * CH:(s + 1) * CH], RL[:, s * CH:(s + 1) * CH]
                h = AC(lambda e: e.activation(hi, w, ACT.Copy), loaded[j], free)
                lo_t = DV(lambda e: e.tensor_tensor(lo, w, hi.bitcast(F32), ALU.subtract), h, free)
                ready_at[j] = (n, h, lo_t)
                done = lo_t
            send(j + NW, done)

        def take(name, i):
            j = len(found)
            found.append((name, i))
            if order is None:
                return 0, None, None
            assert order[j] == (name, i), (order[j], name, i)
            while j not in ready_at:
                prepare()
            n, h, lo_t = ready_at[j]
            while prepared[0] < len(order) and (order[prepared[0]][0] in side or state["gemm"] < n + NR):
                if order[prepared[0]][0] in PLAIN or (order[prepared[0]][0] not in side and state["gemm"] - NR >= len(gem_used)):
                    break
                prepare()
            return n % NR, h, lo_t

        def take_side(name, i):
            j = len(found)
            found.append((name, i))
            if order is None:
                side[name](i, RW[:, 0:CH], None)
                return
            assert order[j] == (name, i)
            while prepared[0] <= j:
                prepare()

        def used(mark):
            gem_used.append(mark)

        def gemm(name, first, n_blocks, kc, hi, lo, ready, form, evac, dirs=2):
            for b in range(n_blocks):
                pair = pairs.next()
                bb = pair.ap
                for c in range(kc):
                    s, wh_t, wl_t = take(name, (first + b) * kc + c)
                    wh = RH[:, s * CH:(s + 1) * CH].rearrange("p (k n) -> p k n", k=4)
                    wl = RL[:, s * CH:(s + 1) * CH].rearrange("p (k n) -> p k n", k=4)
                    PE.wait([wh_t, wl_t, ready[c], bb[0].free, bb[1].free])
                    t = None
                    if form == "T":
                        for m in range(4):
                            out = bb[m // 2].ap[:, (m % 2) * 256:(m % 2) * 256 + 256]
                            for k in range(4):
                                cols = slice(m * 128, m * 128 + 128)
                                start = c == 0 and k == 0 and m % 2 == 0
                                stop = c == kc - 1 and k == 3
                                for q, (l, r) in enumerate(((wh, hi), (wh, lo), (wl, hi))):
                                    lhs, rhs = l[:, k, cols], r(4 * c + k)
                                    a, z = start and q == 0, stop and q == 2
                                    last = m == 3 and k == 3 and q == 2
                                    t = PE(lambda e, o=out, l=lhs, r=rhs, a=a, z=z: e.matmul(
                                        o, l, r, start=a, stop=z, skip_group_check=True), mark=last) or t
                    else:
                        for m in range(2):
                            out = bb[m].ap[:, :]
                            for k in range(4):
                                start, stop = c == 0 and k == 0, c == kc - 1 and k == 3
                                for q, (l, r) in enumerate(((hi, wh), (lo, wh), (hi, wl))):
                                    lhs, rhs = l(4 * c + k)[:, m * 128:m * 128 + 128], r[:, k, :]
                                    a, z = start and q == 0, stop and q == 2
                                    last = m == 1 and k == 3 and q == 2
                                    t = PE(lambda e, o=out, l=lhs, r=rhs, a=a, z=z: e.matmul(
                                        o, l, r, start=a, stop=z, skip_group_check=True), mark=last) or t
                    used(t)
                    yield
                evac(b, bb, t)
                yield

        def small(name, hi, lo, ready, out):
            s, wh_t, wl_t = take(name, 0)
            wh = RH[:, s * CH:(s + 1) * CH].rearrange("p (k n) -> p k n", k=16)
            wl = RL[:, s * CH:(s + 1) * CH].rearrange("p (k n) -> p k n", k=16)
            PE.wait([wh_t, wl_t, ready, out.free])
            t = None
            for k in range(16):
                for q, (l, r) in enumerate(((wh, hi), (wh, lo), (wl, hi))):
                    t = PE(lambda e, l=l[:, k, :], r=r(k), a=k == 0 and q == 0, z=k == 15 and q == 2: e.matmul(
                        out.ap[:, 0:256], l, r, start=a, stop=z), mark=k == 15 and q == 2) or t
            used(t)
            return t

        def ap_of(t, base=0):
            return lambda kt: t[:, (base + kt) * S:(base + kt + 1) * S]

        def split(hi, lo, src, *waits, on=None):
            h = AC(lambda e: e.activation(hi, src, ACT.Copy), *waits)
            return (on or DV)(lambda e: e.tensor_tensor(lo, src, hi.bitcast(F32), ALU.subtract), h, *waits)

        def stats(src, sq, ready, mean=False):
            bk = misc.next()
            t = None
            for i in range(4):
                s = sq[i % 2]
                a = AC(lambda e, i=i, s=s: e.activation(s.ap, src[:, 1024 * i:1024 * i + 1024], ACT.Square),
                       ready[i], s.free)
                for k in range(4):
                    t = PE(lambda e, s=s, i=i, k=k: e.matmul(
                        bk.ap[:, 0:256], ones, s.ap[:, k * 256:k * 256 + 256], start=(i == 0 and k == 0),
                        stop=(i == 3 and k == 3)), a, bk.free, mark=k == 3) or t
                s.free = [t]
            return bk, t

        def rms_stats(src, sq, ready, eps=1e-6):
            bk, t = stats(src, sq, ready)
            free = state.get("rs")
            a = DV(lambda e: e.tensor_scalar(RS[:, 256:512], bk.ap[:, 0:256], 1.0 / D, eps, ALU.mult, ALU.add), t, free)
            bk.free = [a]
            b = AC(lambda e: e.activation(RS[:, 512:768], RS[:, 256:512], ACT.Sqrt), a)
            return DV(lambda e: e.reciprocal(RS[:, 0:256], RS[:, 512:768]), b, free)

        def rms_split(src, gain, sq, ready, hi, lo, free):
            r = rms_stats(src, sq, ready)
            out = []
            for i in range(4):
                s = sq[i % 2]
                t = None
                for k in range(4):
                    kt = 4 * i + k
                    t = DV(lambda e, s=s, k=k, kt=kt: e.scalar_tensor_tensor(
                        s.ap[:, k * 256:k * 256 + 256], src[:, kt * S:kt * S + S], par(gain, kt), RS[:, 0:256],
                        ALU.mult, ALU.mult), r, s.free)
                d = slice(1024 * i, 1024 * i + 1024)
                t2 = split(hi[:, d], lo[:, d], s.ap, t, free)
                s.free = [t2]
                out.append(t2)
            state["rs"] = [out[-1]]
            return out

        def load(name, out, in_, waits=()):
            ld = Load(sem("s_l_" + name))
            PO.dma(out, in_, ld, *waits)
            return ld.all()

        for j in range(NW):
            send(j, None)
        l_c = load("c", C[:, :], io["c_base"])
        l_x = load("x", X[:, :], io["x_t"])
        l_ca = load("ca", G[:, E0:E0 + NCA], io["c_attn"])
        debug = io.get("debug", {})
        dbg_load = Load(sem("s_dbg")) if debug else None

        def dbg(name, ap):
            if name in debug:
                w = PO.dma(debug[name], ap, dbg_load, now())
                for q in everyone:
                    q.wait([w])

        def ca(name):
            a, b = CA[name]
            return G[:, E0 + a:E0 + b]

        sq = [Place(G[:, E0 + NCA + 1024 * i:E0 + NCA + 1024 * i + 1024]) for i in range(2)]
        ra = rms_split(X, "norm_mix", sq, [[l_x, l_c]] * 4, AH, AL, None)
        hA, lA = ap_of(AH), ap_of(AL)

        UA, VA, QKB, VB, QC, CKV, KSW, VSW = (G[:, a:b] for a, b in (
            (0, 1024), (1024, 2048), (2048, 4096), (4096, 5120), (5120, 7168), (7168, 8192), (8192, 9216), (9216, 10240)))
        GT = G[:, 10240:10496]
        GN = G[:, 10496:10560]
        got = {}

        def to(dst, key, func=None):
            def evac(b, bb, t):
                for i in range(2):
                    o = dst[:, b * 1024 + i * 512:b * 1024 + i * 512 + 512]
                    if func is None and i == 0:
                        r = DV(lambda e, o=o, s=bb[i]: e.tensor_copy(o, s.ap[:, :]), t)
                    else:
                        r = AC(lambda e, o=o, s=bb[i]: e.activation(o, s.ap[:, :], func or ACT.Copy), t)
                    bb[i].free = [r]
                    got.setdefault(key, []).append(r)
            return evac

        def to_n(dst, width, key):
            def evac(b, bb, t):
                for i in range(2):
                    o = dst[:, i * width + b * 512:i * width + b * 512 + 512]
                    if i == 0:
                        r = DV(lambda e, o=o, s=bb[i]: e.tensor_copy(o, s.ap[:, :]), t)
                    else:
                        r = AC(lambda e, o=o, s=bb[i]: e.activation(o, s.ap[:, :], ACT.Copy), t)
                    bb[i].free = [r]
                    got.setdefault(key, []).append(r)
            return evac

        def run(*gens):
            gens = list(gens)
            while gens:
                for x in list(gens):
                    if next(x, "end") == "end":
                        gens.remove(x)

        def emit_w_in():
            yield from gemm("in", 0, 1, 4, hA, lA, ra, "T", to(UA, "ua", ACT.Gelu_apprx_tanh))

            def va(b, bb, t):
                for i in range(2):
                    r = AC(lambda e, i=i: e.activation(VA[:, i * 512:i * 512 + 512], bb[i].ap[:, :], ACT.Gelu_apprx_tanh), t)
                    bb[i].free = [r]
                    got.setdefault("va", []).append(r)
            yield from gemm("in", 1, 1, 4, hA, lA, ra, "N", va)
            yield from gemm("in", 2, 1, 4, hA, lA, ra, "T", to(CKV, "ckv"))
            yield from gemm("in", 3, 2, 4, hA, lA, ra, "T", to(QKB, "qkb"))
            yield from gemm("in", 5, 1, 4, hA, lA, ra, "N", to_n(VB, 512, "vb"))
            yield from gemm("in", 6, 2, 4, hA, lA, ra, "T", to(QC, "qc"))
            yield from gemm("in", 8, 1, 4, hA, lA, ra, "T", to(KSW, "ksw"))
            yield from gemm("in", 9, 1, 4, hA, lA, ra, "N", to_n(VSW, 512, "vsw"))
            bk = misc.next()
            t = small("gates", hA, lA, ra, bk)
            r = AC(lambda e: e.activation(GT[0:32, :], bk.ap[0:32, 0:256], ACT.Sigmoid), t)
            bk.free = [r]
            bk = misc.next()
            for i in range(2):
                t = PE(lambda e, i=i: e.transpose(bk.ap[:, i * 32:i * 32 + 32], GT[0:32, i * 128:i * 128 + 128],
                                                  ident[0:32, 0:32]), r, bk.free)
            r = DV(lambda e: e.tensor_copy(GN, bk.ap[:, 0:64]), t)
            bk.free = [r]
            got["gates"] = [r]

        run(emit_w_in())
        in_done = [(PE.sem, PE.n)]
        dbg("ua", UA)
        dbg("va", VA)
        dbg("ckv", CKV)
        dbg("qkb", QKB)
        dbg("gn", GN)

        F0 = E0 + NCA
        scr = Ring([Place(G[:, F0 + 512 * i:F0 + 512 * i + 512]) for i in range(3)])
        pts = Ring([Place(G[:, F0 + 1536 + 512 * i:F0 + 2048 + 512 * i]) for i in range(3)])
        sms = Ring([Place(SM[:, 8 * i:8 * i + 8]) for i in range(8)])
        first_scr = [t for s in sq for t in flat(s.free)]
        for s in scr.places + pts.places:
            s.free = list(first_scr)

        def gmlp():
            sm = sms.next()
            W = scr.next()
            w_m = pts.next()
            mk = DV(lambda e: e.tensor_tensor(
                w_m.ap.rearrange("p (g t) -> p g t", g=4), ca("w_s").rearrange("p (g t) -> p g t", g=4),
                ca("tri").unsqueeze(1).to_broadcast([P, 4, 128]), ALU.mult), l_ca, w_m.free)
            outs = []
            for i in range(2):
                v = VA[:, i * 512:i * 512 + 512]
                a = AC(lambda e, v=v, i=i: e.activation(W.ap, v, ACT.Copy, accum_out=sm.ap[:, i:i + 1]), got["va"], W.free, sm.free)
                b = DV(lambda e, i=i: e.tensor_scalar(sm.ap[:, i:i + 1], sm.ap[:, i:i + 1], -1.0 / 512, None, ALU.mult), a)
                c = DV(lambda e, v=v, i=i: e.tensor_scalar(v, v, sm.ap[:, i:i + 1], None, ALU.add), b)
                d = AC(lambda e, v=v, i=i: e.activation(W.ap, v, ACT.Square, accum_out=sm.ap[:, 2 + i:3 + i]), c)
                W.free = [d]
                f = DV(lambda e, i=i: e.tensor_scalar(sm.ap[:, 2 + i:3 + i], sm.ap[:, 2 + i:3 + i], 1.0 / 512, 1e-6, ALU.mult, ALU.add), d)
                h = AC(lambda e, i=i: e.activation(sm.ap[:, 4 + i:5 + i], sm.ap[:, 2 + i:3 + i], ACT.Sqrt), f)
                k = DV(lambda e, i=i: e.reciprocal(sm.ap[:, 6 + i:7 + i], sm.ap[:, 4 + i:5 + i]), h)
                m = DV(lambda e, v=v, i=i: e.scalar_tensor_tensor(v, v, sm.ap[:, 6 + i:7 + i], ca("ln_g"), ALU.mult, ALU.mult), k)
                o = DV(lambda e, v=v: e.tensor_tensor(v, v, ca("ln_b"), ALU.add), m)
                outs.append(o)
            sm.free = [outs[-1]]
            yield
            bk = [misc.next(), misc.next()]
            ts = []
            for i in range(2):
                for q in range(4):
                    t = PE(lambda e, i=i, q=q: e.matmul(
                        bk[q // 2].ap[:, (q % 2) * 256 + i * 128:(q % 2) * 256 + i * 128 + 128],
                        VA[:, i * 512 + q * 128:i * 512 + q * 128 + 128], w_m.ap[:, q * 128:q * 128 + 128],
                        start=True, stop=True), outs[i], mk, bk[0].free, bk[1].free)
            w_m.free = [t]
            yield
            for j in range(2):
                W = scr.next()
                bs = ca("b_s")[:, j * 256:j * 256 + 256].rearrange("p (g t) -> p g t", g=2).unsqueeze(2).to_broadcast([P, 2, 2, 128])
                a = DV(lambda e, j=j, W=W, bs=bs: e.tensor_tensor(
                    W.ap.rearrange("p (g i t) -> p g i t", g=2, i=2), bk[j].ap[:, :].rearrange("p (g i t) -> p g i t", g=2, i=2),
                    bs, ALU.add), t, W.free)
                bk[j].free = [a]
                b = DV(lambda e, j=j, W=W: e.tensor_tensor(W.ap, W.ap, UA[:, j * 512:j * 512 + 512], ALU.mult), a, got["ua"])
                d = slice(j * 512, j * 512 + 512)
                W.free = [split(AH[:, d], AL[:, d], W.ap, b, in_done)]
                got.setdefault("mix", []).append(W.free[0])
                yield

        def scores(qT, kT, bias, gate, ready, n=256):
            bk, sc, sm = misc.next(), scr.next(), sms.next()
            for i in range(2):
                t = PE(lambda e, i=i: e.matmul(bk.ap[:, i * n:i * n + n], qT[:, i * 128:i * 128 + 128], kT,
                                               start=True, stop=True), ready, bk.free)
            sv = sc.ap[:, 0:2 * n].rearrange("p (i k) -> p i k", i=2)
            if bias is not None:
                a = DV(lambda e: e.scalar_tensor_tensor(sc.ap[:, 0:2 * n], bk.ap[:, 0:2 * n], SCALE, bias, ALU.mult, ALU.add),
                       t, sc.free, l_ca)
                bk.free = [a]
                m = DV(lambda e: e.tensor_reduce(sm.ap[:, 0:2], sv, AX, ALU.max, negate=True), a, sm.free)
                src, scale = sc.ap, 1.0
            else:
                a = DV(lambda e: e.tensor_reduce(sm.ap[:, 6:8], bk.ap[:, 0:2 * n].rearrange("p (i k) -> p i k", i=2), AX, ALU.max,
                                                 negate=True), t, sm.free)
                m = DV(lambda e: e.tensor_scalar(sm.ap[:, 0:2], sm.ap[:, 6:8], SCALE, None, ALU.mult), a)
                src, scale = bk.ap, SCALE
            for i in range(2):
                b = AC(lambda e, i=i: e.activation(sc.ap[:, i * n:i * n + n], src[:, i * n:i * n + n], ACT.Exp,
                                                   bias=sm.ap[:, i:i + 1], scale=scale, accum_out=sm.ap[:, 2 + i:3 + i]), m, sc.free)
            if bias is None:
                bk.free = [b]
            r = DV(lambda e: e.reciprocal(sm.ap[:, 4:6], sm.ap[:, 2:4]), b)
            if gate is not None:
                r = DV(lambda e: e.tensor_tensor(sm.ap[:, 4:6], sm.ap[:, 4:6], gate, ALU.mult), r, got["gates"])
            p = DV(lambda e: e.tensor_tensor(sv, sv, sm.ap[:, 4:6].unsqueeze(2).to_broadcast([P, 2, n]), ALU.mult), r)
            sm.free = [p]
            return sc, p

        def turned(sc, p, n=256, causal=True):
            bk, pt = misc.next(), pts.next()
            if n < 128:
                for i in range(2):
                    t = PE(lambda e, i=i: e.transpose(bk.ap[0:n, i * 128:i * 128 + 128], sc.ap[:, i * n:i * n + n], ident), p, bk.free)
                c = AC(lambda e: e.activation(pt.ap[0:n, 0:256], bk.ap[0:n, 0:256], ACT.Copy), t, pt.free)
                blocks = [(0, 0), (1, 0)]
            else:
                blocks = [(0, 0), (1, 0), (1, 1)] if causal else [(0, 0), (0, 1), (1, 0), (1, 1)]
                for j, (i, k) in enumerate(blocks):
                    t = PE(lambda e, i=i, k=k, j=j: e.transpose(
                        bk.ap[:, j * 128:j * 128 + 128], sc.ap[:, i * 256 + k * 128:i * 256 + k * 128 + 128], ident), p, bk.free)
                w = len(blocks) * 128
                c = AC(lambda e: e.activation(pt.ap[:, 0:w], bk.ap[:, 0:w], ACT.Copy), t, pt.free)
            sc.free = [t]
            bk.free = [c]
            return pt, c, blocks

        def attend(units, out_hi, out_lo, extra):
            bk = misc.next()
            for i in range(2):
                ops = [(pt, j, n, v(k), c) for (pt, c, blocks), v, n in units for j, (ii, k) in enumerate(blocks) if ii == i]
                for a, (pt, j, n, v, c) in enumerate(ops):
                    t = PE(lambda e, i=i, j=j, n=n, v=v, pt=pt, a=a, z=len(ops) - 1: e.matmul(
                        bk.ap[:, i * 128:i * 128 + 128], v, pt.ap[0:n, j * 128:j * 128 + 128], start=a == 0, stop=a == z),
                        c, bk.free, extra)
            for (pt, _, _), _, _ in units:
                pt.free = [t]
            h = AC(lambda e: e.activation(out_hi, bk.ap[:, 0:256], ACT.Copy), t, in_done)
            r = DV(lambda e: e.tensor_tensor(out_lo, bk.ap[:, 0:256], out_hi.bitcast(F32), ALU.subtract), h, t, in_done)
            bk.free = [r]
            got.setdefault("mix", []).append(r)

        def dilated():
            held = None
            for h in range(5):
                new = None
                if h < 4:
                    new = scores(QKB[:, h * 256:h * 256 + 256], QKB[:, 1024 + h * 256:1024 + h * 256 + 256], ca("dil"), None, got["qkb"])
                    yield
                if held is not None:
                    tr = turned(*held)
                    o = (4 + h - 1) * S
                    attend([(tr, lambda k, h=h: VB[:, k * 512 + (h - 1) * 128:k * 512 + h * 128], 128)],
                           AH[:, o:o + S], AL[:, o:o + S], got["vb"])
                    yield
                held = new

        B1 = G[:, F0 + 3072:F0 + 3072 + 960]
        KC = RS[:, 256:512]

        def compress():
            for kv in range(2):
                w_name = ("ck", "cv")[kv]
                hid = misc.next()
                vb = B1.rearrange("p (g n j) -> p g n j", g=2, n=15)
                ov = CKV[:, kv * 512:kv * 512 + 512].rearrange("p (g n j) -> p g n j", g=2, n=16)
                po = ca("pos").rearrange("p (h j) -> p h j", h=2)
                for h in range(2):
                    a = DV(lambda e, h=h: e.tensor_tensor(
                        vb[:, :, :, h * 16:h * 16 + 16], ov[:, :, h:h + 15, :],
                        po[:, h, :].unsqueeze(1).unsqueeze(1).to_broadcast([P, 2, 15, 16]), ALU.add),
                        got["ckv"], l_ca, got.get("b1free"))
                t = None
                for c in range(2):
                    w, wt, rel = take_plain(w_name, c)
                    for j in range(16):
                        jj = 16 * c + j
                        t = PE(lambda e, w=w, j=j, jj=jj: e.matmul(
                            hid.ap[:, 0:30], w[:, j * 128:j * 128 + 128], vb[:, :, :, jj], start=jj == 0, stop=jj == 31),
                            wt, a, hid.free, mark=j == 15) or t
                    rel(t)
                    yield
                got["b1free"] = [t]
                h_sb = sms8.next()
                b = AC(lambda e: e.activation(h_sb.ap[:, 0:30], hid.ap[:, 0:30], ACT.Gelu_apprx_tanh), t, h_sb.free)
                hid.free = [b]
                o = misc.next()
                if kv == 0:
                    t = PE(lambda e: e.matmul(o.ap[:, 0:30], ca("ckw2"), h_sb.ap[:, 0:30], start=True, stop=True), b, o.free)
                    r = DV(lambda e: e.tensor_copy(KC[:, 0:30], o.ap[:, 0:30]), t)
                    got["kc"] = [r]
                else:
                    for q in range(2):
                        t = PE(lambda e, q=q: e.matmul(o.ap[0:15, q * 128:q * 128 + 128], h_sb.ap[:, q * 15:q * 15 + 15],
                                                       ca("cvw2"), start=True, stop=True), b, o.free)
                    r = DV(lambda e: e.tensor_copy(RS[0:15, 512:768], o.ap[0:15, 0:256]), t)
                    got["vc"] = [r]
                o.free = [r]
                h_sb.free = [t]
                yield

        sms8 = Ring([Place(SM[:, 64 + 32 * i:64 + 32 * i + 32]) for i in range(2)])
        plain = {}

        def plain_side(i_w_t):
            pass

        def take_plain(name, i):
            j = len(found)
            found.append((name, i))
            if order is None:
                return RW[:, 0:CH], None, lambda t: None
            assert order[j] == (name, i)
            while prepared[0] < j:
                prepare()
            assert prepared[0] == j
            prepared[0] += 1
            k = j % NW
            return RW[:, k * CH:(k + 1) * CH], loaded[j], lambda t: send(j + NW, t)

        def nsa():
            held = None
            for h in range(9):
                new = None
                if h < 8:
                    q, gq = QC[:, h * 256:h * 256 + 256], h // 4
                    gate = lambda i, h=h: GN.rearrange("p (i c) -> p i c", i=2)[:, :, h * 3 + i]
                    new = []
                    sc, p = scores(q, KC[:, gq * 15:gq * 15 + 15], ca("bcmp")[:, 0:30], gate(0), [got["qc"], got["kc"]], n=15)
                    p = DV(lambda e, sc=sc: e.tensor_tensor(sc.ap[:, 0:30], sc.ap[:, 0:30], ca("vcmp")[:, 0:30], ALU.mult), p)
                    new.append((sc, p))
                    yield
                    tc = turned(sc, p, n=15)
                    s1 = scores(q, KSW[:, gq * 256:gq * 256 + 256], ca("cau"), gate(1), [got["qc"], got["ksw"]])
                    yield
                    s2 = scores(q, KSW[:, 512 + gq * 256:512 + gq * 256 + 256], ca("cau"), gate(2), [got["qc"], got["ksw"]])
                    yield
                    t1 = turned(*s1)
                    yield
                    t2 = turned(*s2)
                    o = (8 + h) * S
                    attend([(tc, lambda k, gq=gq: RS[0:15, 512 + gq * 128:512 + gq * 128 + 128], 15),
                            (t1, lambda k, gq=gq: VSW[:, k * 512 + gq * 128:k * 512 + gq * 128 + 128], 128),
                            (t2, lambda k, gq=gq: VSW[:, k * 512 + 256 + gq * 128:k * 512 + 256 + gq * 128 + 128], 128)],
                           AH[:, o:o + S], AL[:, o:o + S], [got["vsw"], got["vc"]])
                    yield

        run(gmlp())
        run(compress())
        run(dilated())
        run(nsa())
        dbg("mixh", AH[:, :].bitcast(F32))
        dbg("mixl", AL[:, :].bitcast(F32))

        got["x"] = []

        def add_x(b, bb, t):
            for i in range(2):
                x = X[:, b * 1024 + i * 512:b * 1024 + i * 512 + 512]
                r = DV(lambda e, x=x, s=bb[i]: e.tensor_tensor(x, s.ap[:, :], x, ALU.add), t, got["x"])
                bb[i].free = [r]
            got["x"] = [r]

        mix = [got["mix"]] * 4
        run(gemm("out", 0, 4, 4, hA, lA, mix, "T", add_x))
        dbg("x1", X[:, :])

        e_free = now()
        state["rs"] = e_free
        MEM = G[:, E0:E0 + 4096]
        l_mem = load("mem", MEM, io["mem_t"], [e_free])
        sq = [Place(G[:, E0 + 4096 + 1024 * i:E0 + 5120 + 1024 * i]) for i in range(2)]
        for s in sq:
            s.free = e_free
        rm = rms_split(MEM, "norm_mem", sq, [l_mem] * 4, HH, HL, e_free)
        hM, lM = ap_of(HH), ap_of(HL)
        XK, XV = G[:, E0 + 6144:E0 + 7168], G[:, E0 + 7168 - 1024 * 0:E0 + 7168]
        XV = G[:, E0:E0 + 1024]
        XQ = G[:, E0 + 1024:E0 + 2048]
        got["xk"], got["xv"], got["xq"] = [], [], []
        run(gemm("xkv", 0, 1, 4, hM, lM, rm, "T", to(XK, "xk")))
        run(gemm("xkv", 1, 1, 4, hM, lM, rm, "N", to_n(XV, 512, "xv")))
        rx = rms_split(X, "norm_xattn", sq, [got["x"]] * 4, AH, AL, now())
        run(gemm("xq", 0, 1, 4, hA, lA, rx, "T", to(XQ, "xq")))
        base = now()
        scr = Ring([Place(G[:, E0 + 2048 + 512 * i:E0 + 2560 + 512 * i]) for i in range(3)])
        pts = Ring([Place(G[:, E0 + 4096 + 512 * i:E0 + 4608 + 512 * i]) for i in range(3)])
        for s in scr.places + pts.places:
            s.free = list(base)
        in_done = base
        got["mix"] = []

        def cross():
            held = None
            for h in range(5):
                new = None
                if h < 4:
                    new = scores(XQ[:, h * 256:h * 256 + 256], XK[:, h * 256:h * 256 + 256], None, None, [got["xq"], got["xk"]])
                    yield
                if held is not None:
                    tr = turned(*held, causal=False)
                    o = (16 + h - 1) * S
                    attend([(tr, lambda k, h=h: XV[:, k * 512 + (h - 1) * 128:k * 512 + h * 128], 128)],
                           HH[:, o:o + S], HL[:, o:o + S], got["xv"])
                    yield
                held = new

        run(cross())
        run(gemm("xo", 0, 4, 1, ap_of(HH, 16), ap_of(HL, 16), [got["mix"]], "T", add_x))
        dbg("x2", X[:, :])

        ACC = [G[:, E0:E0 + 2048], G[:, E0 + 2048:E0 + 4096]]
        SIL = SM[:, 0:32]
        tmps = Ring([Place(G[:, E0 + 6144 + 512 * i:E0 + 6656 + 512 * i]) for i in range(3)])
        sq = [Place(G[:, E0 + 4096 + 1024 * i:E0 + 5120 + 1024 * i]) for i in range(2)]
        base = now()
        for s in tmps.places + sq:
            s.free = list(base)
        sil = AC(lambda e: e.activation(SIL, C[:, 256 + PAR["c"][0]:256 + PAR["c_ctx"][1]], ACT.Silu), base)
        rm = rms_split(X, "norm_mlp", sq, [got["x"]] * 4, AH, AL, base)
        acc_t = {"a": base, "b": base}

        def ada(i, w, ld):
            cb, kt = divmod(i, 16)
            done = []
            for which in range(2 if cb < 2 else 1):
                key = "ab"[which]
                a = ACC[which]
                s = SIL[:, which * 16 + kt:which * 16 + kt + 1]
                if kt == 0:
                    t = DV(lambda e, a=a, s=s: e.tensor_scalar(a, w, s, None, ALU.mult), ld, sil, acc_t[key])
                else:
                    t = DV(lambda e, a=a, s=s: e.scalar_tensor_tensor(a, w, s, a, ALU.mult, ALU.add), ld, acc_t[key])
                acc_t[key] = t
                done.append(t)
                if kt == 15:
                    bk = misc.next()
                    for m in range(16):
                        p = PE(lambda e, a=a, m=m, bk=bk: e.matmul(bk.ap[:, m:m + 1], a[:, m * 128:m * 128 + 128], ones[:, 0:1],
                                                                   start=True, stop=True), t, bk.free)
                    acc_t[key] = p
                    o = cb * 16 if which == 0 else 96 + cb * 16
                    r = DV(lambda e, o=o, bk=bk: e.tensor_tensor(MODT[:, o:o + 16], bk.ap[:, 0:16], par("b_ada")[:, cb * 16:cb * 16 + 16], ALU.add), p)
                    bk.free = [r]
                    got["mod"] = [r]
            return done

        side["ada"] = ada
        hid_free = [base] * 24
        hid_ready = [None] * 24

        def up(qn, b0, nb):
            def evac(b, bb, t):
                for i in range(2):
                    kt = (16 * qn + 4 * (b0 + b) + 2 * i) % 24
                    tm = tmps.next()
                    r = DV(lambda e, s=bb[i], tm=tm: e.tensor_scalar(tm.ap, s.ap[:, :], 0.0, None, ALU.max), t, tm.free)
                    bb[i].free = [r]
                    r2 = AC(lambda e, tm=tm: e.activation(tm.ap, tm.ap, ACT.Square), r)
                    d = slice(kt * S, kt * S + 512)
                    z = split(HH[:, d], HL[:, d], tm.ap, r2, hid_free[kt], on=PO)
                    tm.free = [z]
                    hid_ready[kt] = hid_ready[kt + 1] = z
            yield from gemm("up", 4 * qn + b0, nb, 4, hA, lA, rm, "T", evac)

        def ring24(t, qn):
            return lambda kt: t[:, ((16 * qn + kt) % 24) * S:((16 * qn + kt) % 24 + 1) * S]

        def down(qn):
            ready = [[hid_ready[(16 * qn + 4 * c + k) % 24] for k in range(4)] for c in range(4)]
            yield from gemm("down", 4 * qn, 4, 4, ring24(HH, qn), ring24(HL, qn), ready, "T", add_x)
            for k in range(16):
                hid_free[(16 * qn + k) % 24] = [(PE.sem, PE.n)]

        def mlp():
            yield from up(0, 0, 4)
            for qn in range(4):
                if qn < 3:
                    yield from up(qn + 1, 0, 2)
                yield from down(qn)
                if qn < 3:
                    yield from up(qn + 1, 2, 2)

        def ada_all():
            for i in range(96):
                take_side("ada", i)
                yield
                yield

        run(mlp(), ada_all())
        dbg("x3", X[:, :])
        dbg("mod", MODT[:, :])

        r = rms_stats(X, sq, [got["x"]] * 4)
        for kt in range(16):
            t = DV(lambda e, kt=kt: e.scalar_tensor_tensor(X[:, kt * S:kt * S + S], X[:, kt * S:kt * S + S], par("final_norm", kt),
                                                           RS[:, 0:256], ALU.mult, ALU.mult), r)
        got["x"] = [t]
        state["rs"] = [t]
        one = []
        for a in (16, 64, 96 + 16):
            one.append(DV(lambda e, a=a: e.tensor_scalar(MODT[:, a:a + 16], MODT[:, a:a + 16], 1.0, None, ALU.add), got["mod"]))
        dbg("x4", X[:, :])

        def modulate(src, sh, sc, sqs, ready, free, out=None):
            outs = []
            for i in range(4):
                s = sqs[i % 2]
                for k in range(4):
                    kt = 4 * i + k
                    t = DV(lambda e, s=s, k=k, kt=kt: e.tensor_scalar(
                        s.ap[:, k * 256:k * 256 + 256], src[:, kt * S:kt * S + S], sc(kt), sh(kt), ALU.mult, ALU.add),
                        ready, one, s.free)
                d = slice(1024 * i, 1024 * i + 1024)
                t2 = split(AH[:, d], AL[:, d], s.ap, t, free)
                s.free = [t2]
                outs.append(t2)
            return outs

        base = now()
        l_cg = load("cg", G[:, E0:E0 + NCG], io["c_gla"], [base])

        def cg(name):
            a, b = CG[name]
            return G[:, E0 + a:E0 + b]

        T0 = E0 + NCG
        CTX = G[:, 4096:8192]
        l_ctx = load("ctx", CTX, io["ctx_t"], [base])
        sq = [Place(G[:, T0 + 1024 * i:T0 + 1024 + 1024 * i]) for i in range(2)]
        for s in sq:
            s.free = list(base)
        rc = modulate(CTX, lambda kt: cmod(0, kt), lambda kt: cmod(1, kt), sq, l_ctx, base)
        ctx_split = [rc[-1]]
        K = G[:, 0:2048]
        V = [Place(G[:, 2048:3072]), Place(G[:, 3072:4096])]
        Vr = Ring(V)
        Q = G[:, 4096:6144]
        SS = [Place(G[:, 6144 + 2048 * i:8192 + 2048 * i]) for i in range(1)]
        SSr = Ring(SS)
        OT = G[:, T0:T0 + 4096]
        ALR = RS[:, 256:512]
        Z = G[:, 8192:8704]
        CU = G[:, 8704:9216]
        TM = [Place(G[:, 9216:9728]), Place(G[:, 9728:10240])]
        QN = G[:, 10240:10752]
        KN = G[:, 10752:11264]
        KS = G[:, 11264:11776]
        KSN = G[:, 11776:12288]
        QI = G[:, T0 + 4096:T0 + 5120]
        ATs = [G[:, T0 + 5120 + 256 * i:T0 + 5376 + 256 * i] for i in range(2)]
        assert T0 + 5120 + 512 <= E0 + NE, (T0 + 5632, E0 + NE)
        for pl in V + SS + TM:
            pl.free = list(base) + ctx_split
        gla = {"z": base + ctx_split, "first": base + ctx_split}
        MSK = C[:, 0:0]
        spill = Load(sem("s_spill"))
        s_back = {}

        def decay(d, h, alr_t, mask):
            bk = misc.next()
            for k in range(2):
                f = (2 * h + k) * 128
                t = PE(lambda e, k=k, f=f: e.matmul(bk.ap[:, k * 256:k * 256 + 256], cg("decay")[32 * d:32 * d + 32, f:f + 128],
                                                    ALR[32 * d:32 * d + 32, :], start=True, stop=True, tile_position=(32 * d, 0)),
                       alr_t, bk.free, l_cg)
            for k in range(2):
                a = AC(lambda e, k=k: e.activation(Z[:, k * 256:k * 256 + 256], bk.ap[:, k * 256:k * 256 + 256], ACT.Identity,
                                                   bias=par("b_decay", 8 * d + 2 * h + k)), t, gla["z"])
            bk.free = [a]
            tm = TM[0]
            b = DV(lambda e: e.scalar_tensor_tensor(tm.ap, Z, -1.0, Z, ALU.mult, ALU.min), a, tm.free)
            c = AC(lambda e: e.activation(tm.ap, tm.ap, ACT.Exp), b)
            c = AC(lambda e: e.activation(tm.ap, tm.ap, ACT.Ln, bias=1.0), c)
            a = DV(lambda e: e.scalar_tensor_tensor(Z, Z, 0.0, tm.ap, ALU.min, ALU.subtract), c)
            tm.free = [a]
            rev = (lambda ap: ap) if d == 0 else (lambda ap: ap[:, ::-1])
            t = DV(lambda e: e.tensor_tensor_scan(rev(CU), cg(mask), rev(Z), 0.0, ALU.mult, ALU.add), a, gla.get("cu"))
            gla["z"] = [t]
            return t

        def scaled(src, diff, sign, out, waits, free):
            tm = TM[1]
            a = DV(lambda e: diff(e, tm.ap), waits, tm.free)
            b = AC(lambda e: e.activation(tm.ap, tm.ap, ACT.Exp, scale=sign / 16.0), a)
            c = DV(lambda e: out(e, src, tm.ap), b, waits, free)
            tm.free = [c]
            return c

        def c_scores_free():
            return None

        alr_bk = misc.next()
        t = small("alr", hA, lA, rc, alr_bk)
        alr_t = DV(lambda e: e.tensor_copy(ALR, alr_bk.ap[:, 0:256]), t, got["x"], state["rs"])
        alr_bk.free = [alr_t]
        got["k"] = []

        def to_k(dst, key, scale=1.0):
            def evac(b, bb, t):
                for i in range(2):
                    o = dst[:, b * 1024 + i * 512:b * 1024 + i * 512 + 512]
                    r = AC(lambda e, o=o, s=bb[i]: e.activation(o, s.ap[:, :], ACT.Copy, scale=scale), t, gla.get(key))
                    bb[i].free = [r]
                    got.setdefault(key, []).append(r)
            return evac

        def v_block(name, h):
            v = Vr.next()

            def evac(b, bb, t):
                rs = []
                for i in range(2):
                    o = v.ap[:, i * 512:i * 512 + 512]
                    rs.append(AC(lambda e, o=o, s=bb[i]: e.activation(o, s.ap[:, :], ACT.Copy), t, v.free))
                    bb[i].free = [rs[-1]]
                v.ready = rs
            return v, gemm(name, h, 1, 4, hA, lA, rc, "N", evac)

        gla["k"] = base + ctx_split
        run(gemm("k2", 0, 2, 4, hA, lA, rc, "T", to_k(K, "k")))

        def turn_k(ready):
            bk = misc.next()
            for i in range(2):
                for k in range(2):
                    t = PE(lambda e, i=i, k=k: e.transpose(bk.ap[:, i * 256 + k * 128:i * 256 + k * 128 + 128],
                                                           KS[:, k * 256 + i * 128:k * 256 + i * 128 + 128], ident), ready, bk.free)
            gla["ks"] = [t]
            c = DV(lambda e: e.tensor_copy(KSN, bk.ap[:, :]), t, gla.get("ksn"))
            bk.free = [c]
            return c

        def ctx_head(h, v):
            for d in range(2):
                cu = decay(d, h, alr_t, "scan_all")
                yield
                cv = CU.rearrange("p (k t) -> p k t", k=2)
                last = cv[:, :, 255:256] if d == 0 else cv[:, :, 0:1]
                ks = scaled(K[:, h * 512:h * 512 + 512],
                            lambda e, o: e.tensor_tensor(o.rearrange("p (k t) -> p k t", k=2), last.to_broadcast([P, 2, 256]), cv, ALU.subtract),
                            1.0, lambda e, s, x: e.tensor_tensor(KS, s, x, ALU.mult), [cu, got["k"]], [gla.get("ks"), gla["first"]])
                gla["cu"] = [ks]
                yield
                kn = turn_k(ks)
                sv = SSr.next()
                for k in range(2):
                    bk = misc.next()
                    for i in range(2):
                        t = PE(lambda e, i=i, k=k, bk=bk: e.matmul(bk.ap[:, :], KSN[:, i * 256 + k * 128:i * 256 + k * 128 + 128],
                                                                   v.ap[:, i * 512:i * 512 + 512], start=i == 0, stop=i == 1),
                               kn, v.ready, bk.free)
                    c = AC(lambda e, k=k, bk=bk, sv=sv: e.activation(sv.ap[:, (k * 512):(k * 512) + 512], bk.ap[:, :], ACT.Copy), t, sv.free)
                    bk.free = [c]
                gla["ksn"] = [t]
                z = PO.dma(io["state"][h, d], sv.ap[:, 0:1024], spill, c)
                sv.free = [z]
                yield
            v.free = [t]

        v, gen = v_block("v2", 0)
        run(gen)
        for h in range(4):
            nxt = None
            if h < 3:
                nxt, gen = v_block("v2", h + 1)
                run(ctx_head(h, v), gen)
            else:
                run(ctx_head(h, v))
            v = nxt

        base = now()
        rl = modulate(X, lambda kt: mod(0, kt), lambda kt: mod(1, kt), sq, got["x"], base)
        rc = rl
        alr_bk = misc.next()
        t = small("alr", hA, lA, rc, alr_bk)
        alr_t = DV(lambda e: e.tensor_copy(ALR, alr_bk.ap[:, 0:256]), t, base)
        alr_bk.free = [alr_t]
        got["k"], got["q"] = [], []
        gla["k"] = gla["q"] = base
        run(gemm("k2", 0, 2, 4, hA, lA, rc, "T", to_k(K, "k")))
        run(gemm("q2", 0, 2, 4, hA, lA, rc, "T", to_k(Q, "q", 1.0 / 16.0)))
        base2 = now()
        z1 = PO(lambda e: e.memset(QI, 0.0), base2)
        z2 = PO(lambda e: e.memset(G[:, T0 + 5120:T0 + 5632], 0.0), base2)
        MK = [st.enter_context(nc.sbuf_tensor(f"MK{d}", [P, 64], U32)) for d in range(2)]
        l_mk = [load(f"mk{d}", MK[d][:, :], io["masks"][d]) for d in range(2)]
        back = Load(sem("s_back"))
        ob = [banks[4], banks[5]]
        misc2 = Ring([banks[6], banks[7]])
        misc = misc2
        gla["qi"] = [z1]
        gla["at"] = [z2]

        def lat_head(h, v):
            sv = SSr.next()
            PO.wait([spill.all(), sv.free])
            for d in range(2):
                lt = PO.dma(sv.ap[:, d * 1024:d * 1024 + 1024], io["state"][h, d], back)
            PE.wait([ob[0].free, ob[1].free])
            t_at = []
            for d in range(2):
                cu = decay(d, h, alr_t, "scan")
                yield
                cv = CU.rearrange("p (c t) -> p c t", c=8)
                ref = cv[:, :, 31:32] if d == 0 else cv[:, :, 32:33]
                last = cv[:, :, 63:64] if d == 0 else cv[:, :, 0:1]
                q, kk = Q[:, h * 512:h * 512 + 512], K[:, h * 512:h * 512 + 512]
                v8 = lambda ap: ap.rearrange("p (c t) -> p c t", c=8)
                tm = TM[1]
                a = DV(lambda e: e.tensor_tensor(v8(TM[0].ap), cv, ref.to_broadcast([P, 8, 64]), ALU.subtract), cu, TM[0].free)
                b = AC(lambda e: e.activation(tm.ap, TM[0].ap, ACT.Exp, scale=1 / 16.0), a, tm.free)
                qn = DV(lambda e: e.tensor_tensor(QN, q, tm.ap, ALU.mult), b, got["q"], gla.get("qn"))
                b = AC(lambda e: e.activation(TM[0].ap, TM[0].ap, ACT.Exp, scale=-1 / 16.0), b)
                tm.free = [qn]
                kn = DV(lambda e: e.tensor_tensor(KN, kk, TM[0].ap, ALU.mult), b, got["k"], gla.get("qn"))
                TM[0].free = [kn]
                yield
                sb_ = misc.next()
                parts = ((0, 0, 64), (32, 32, 32)) if d == 0 else ((32, 0, 64), (0, 0, 32))
                for c in range(4):
                    half = 64 * (c % 2)
                    for j0, i0, ni in parts:
                        for k in range(2):
                            o = k * 256 + c * 64
                            t = PE(lambda e: e.matmul(
                                sb_.ap[half + j0:half + j0 + 32, c * 64 + i0:c * 64 + i0 + ni], KN[:, o + j0:o + j0 + 32],
                                QN[:, o + i0:o + i0 + ni], start=k == 0, stop=k == 1, tile_position=(0, half + j0)),
                                qn, kn, sb_.free)
                gla["qn"] = [t]
                at = ATs[d].rearrange("p (i t) -> p i t", i=2)
                sv2 = sb_.ap[:, 0:256].rearrange("p (i t) -> p i t", i=2)
                for half in (0, 64):
                    for j0, i0, ni in parts:
                        r, q_ = slice(half + j0, half + j0 + 32), slice(half + i0, half + i0 + ni)
                        c = DV(lambda e: e.copy_predicated(
                            at[r, :, q_], MK[d][r, i0:i0 + ni].unsqueeze(1).to_broadcast([32, 2, ni]), sv2[r, :, q_]),
                            t, l_mk, gla["at"])
                sb_.free = [c]
                yield
                for i in range(2):
                    t = PE(lambda e, i=i, d=d: e.matmul(ob[i].ap[:, :], ATs[d][:, i * 128:i * 128 + 128], v.ap[:, i * 512:i * 512 + 512],
                                                        start=d == 0, stop=False, skip_group_check=True), c, v.ready)
                t_at.append(t)
                a = AC(lambda e: e.activation(tm.ap, CU, ACT.Exp, scale=1 / 16.0), cu, tm.free)
                qv = QI.rearrange("p (k c t) -> p k c t", k=2, c=4)
                ws = []
                for cpar in range(2):
                    ws.append(DV(lambda e, cpar=cpar: e.tensor_tensor(
                        qv[:, :, cpar::2, 64 * cpar:64 * cpar + 64] if False else QI.rearrange("p (k i c t) -> p k i c t", k=2, i=2, c=2)[:, :, :, cpar, 64 * cpar:64 * cpar + 64],
                        q.rearrange("p (k i c t) -> p k i c t", k=2, i=2, c=2)[:, :, :, cpar, :],
                        tm.ap.rearrange("p (k i c t) -> p k i c t", k=2, i=2, c=2)[:, :, :, cpar, :], ALU.mult), a, gla["qi"]))
                sm = SM[:, 8 * d:8 * d + 8]
                dc = AC(lambda e, sm=sm: e.activation(sm, last.rearrange("p c t -> p (c t)"), ACT.Exp, scale=1 / 16.0), cu, gla.get("sm"))
                tm.free = [ws[-1]]
                ks = scaled(kk, lambda e, o: e.tensor_tensor(v8(o), last.to_broadcast([P, 8, 64]), cv, ALU.subtract),
                            1.0, lambda e, s, x: e.tensor_tensor(KS, s, x, ALU.mult), [cu, got["k"], ws], gla.get("ks"))
                gla["cu"] = [ks, dc]
                yield
                ksn = turn_k(ks)
                yield
                chunks = range(4) if d == 0 else range(3, -1, -1)
                up_t = [lt, lt]
                for n, c in enumerate(chunks):
                    for k in range(2):
                        s_ap = sv.ap[:, d * 1024 + k * 512:d * 1024 + k * 512 + 512]
                        t = PE(lambda e, c=c, k=k, s_ap=s_ap, z=(d == 1 and n == 3 and k == 1): e.matmul(
                            ob[c // 2].ap[:, :], QI[:, k * 512 + c * 128:k * 512 + c * 128 + 128], s_ap,
                            start=False, stop=z, skip_group_check=True), ws, up_t[k])
                    ti = t
                    if n < 3:
                        r = slice(64 * (c % 2), 64 * (c % 2) + 64)
                        for k in range(2):
                            bk = misc.next()
                            s_ap = sv.ap[:, d * 1024 + k * 512:d * 1024 + k * 512 + 512]
                            t = PE(lambda e, c=c, k=k, r=r, bk=bk: e.matmul(
                                bk.ap[:, :], KSN[r, (c // 2) * 256 + k * 128:(c // 2) * 256 + k * 128 + 128],
                                v.ap[r, (c // 2) * 512:(c // 2) * 512 + 512], start=True, stop=True,
                                tile_position=(64 * (c % 2), 0)), ksn, v.ready, bk.free)
                            up_t[k] = DV(lambda e, c=c, k=k, bk=bk, s_ap=s_ap, sm=sm: e.scalar_tensor_tensor(
                                s_ap, s_ap, sm[:, 4 * k + c:4 * k + c + 1], bk.ap[:, :], ALU.mult, ALU.add), t, ti, dc)
                            bk.free = [up_t[k]]
                    yield
                gla["qi"] = [ti]
                gla["ksn"] = [t]
                gla["sm"] = [up_t[0], up_t[1]]
            gla["at"] = [t_at[0], t_at[1]]
            sv.free = [ti, up_t]
            v.free = [ti, t]
            sq2 = [TM[0], TM[1]]
            ready = []
            for i in range(2):
                a = AC(lambda e, i=i: e.activation(sq2[i].ap, ob[i].ap[:, :], ACT.Square, accum_out=SM[:, 16 + i:17 + i]), ti, sq2[i].free, gla.get("sm2"))
                b = DV(lambda e, i=i: e.tensor_scalar(SM[:, 18 + i:19 + i], SM[:, 16 + i:17 + i], 1.0 / 512, 1e-6, ALU.mult, ALU.add), a)
                b = AC(lambda e, i=i: e.activation(SM[:, 20 + i:21 + i], SM[:, 18 + i:19 + i], ACT.Sqrt), b)
                b = DV(lambda e, i=i: e.reciprocal(SM[:, 22 + i:23 + i], SM[:, 20 + i:21 + i]), b)
                c = DV(lambda e, i=i: e.tensor_scalar(sq2[i].ap, ob[i].ap[:, :], SM[:, 22 + i:23 + i], None, ALU.mult), b)
                ob[i].free = [c]
                ready.append(c)
            gla["sm2"] = [c]
            yield
            for j in range(2):
                bk = misc.next()
                for k in range(2):
                    for i in range(2):
                        f = (2 * j + k) * 128
                        t = PE(lambda e, i=i, k=k, f=f, bk=bk: e.transpose(bk.ap[:, k * 256 + i * 128:k * 256 + i * 128 + 128],
                                                                           sq2[i].ap[:, f:f + 128], ident), ready[i], bk.free)
                for k in range(2):
                    ft = 4 * h + 2 * j + k
                    c = DV(lambda e, k=k, ft=ft, bk=bk: e.tensor_scalar(OT[:, ft * 256:ft * 256 + 256], bk.ap[:, k * 256:k * 256 + 256],
                                                                        par("gla_gain", ft), None, ALU.mult), t, gla["ot"])
                bk.free = [c]
                yield
            TM[0].free = [t]
            TM[1].free = [t]
            got["ot"] = [c]

        gla["ot"] = base2
        v, gen = v_block("v2", 0)
        run(gen)
        for h in range(4):
            nxt = None
            if h < 3:
                nxt, gen = v_block("v2", h + 1)
                run(lat_head(h, v), gen)
            else:
                run(lat_head(h, v))
            v = nxt
        dbg("ot", OT)
        misc = Ring(banks[4:8])

        base = now()

        def half_tiles(lo_base, hi_base):
            def at(i, n):
                b = (lo_base if i < 8 else hi_base) + (i % 8) * S
                return G[:, b:b + n * S]
            return at

        BG = half_tiles(16 * S, (24 + 16) * S)
        tm2 = Ring([Place(G[:, E0 + 512 * i:E0 + 512 + 512 * i]) for i in range(3)])
        for s in tm2.places:
            s.free = list(base)

        def gate_evac(dst, key):
            def evac(b, bb, t):
                for i in range(2):
                    o = dst(4 * b + 2 * i, 2)
                    r = AC(lambda e, o=o, s=bb[i]: e.activation(o, s.ap[:, :], ACT.Sigmoid), t, base)
                    bb[i].free = [r]
                    got.setdefault(key, []).append(r)
            return evac

        got["y"] = []

        def g_evac(b, bb, t):
            for i in range(2):
                tm = tm2.next()
                a = AC(lambda e, tm=tm, s=bb[i]: e.activation(tm.ap, s.ap[:, :], ACT.Silu), t, tm.free)
                bb[i].free = [a]
                d = slice(b * 1024 + i * 512, b * 1024 + i * 512 + 512)
                m = DV(lambda e, tm=tm, d=d: e.tensor_tensor(tm.ap, tm.ap, OT[:, d], ALU.mult), a, got["ot"])
                z = split(HH[:, d], HL[:, d], tm.ap, m, base, on=PO)
                tm.free = [z]
                got["y"].append(z)

        run(gemm("g2", 0, 4, 4, hA, lA, rc, "T", g_evac))
        run(gemm("bg2", 0, 4, 4, hA, lA, rc, "T", gate_evac(BG, "bg")))
        base = now()
        l_cp = load("cp", G[:, E0 + 512 * 3:E0 + 512 * 3 + NCP], io["c_pool"], [base])
        PM = G[:, E0 + 1536:E0 + 1536 + 2048].rearrange("p (w i t) -> p w i t", w=4, i=2)
        PG = G[:, E0 + 3584:E0 + 3584 + 2048].rearrange("p (k w n) -> p k w n", k=2, w=4)
        PN = G[:, E0 + 5632:E0 + 5632 + 2048]

        def y_evac(b, bb, t):
            for i in range(2):
                o = BG(4 * b + 2 * i, 2)
                r = DV(lambda e, o=o, s=bb[i]: e.tensor_tensor(o, s.ap[:, :], o, ALU.mult), t, got["bg"])
                bb[i].free = [r]
            got["yg"] = [r]

        run(gemm("gout", 0, 4, 4, ap_of(HH), ap_of(HL), [got["y"]] * 4, "T", y_evac))
        got["pn"] = []
        y_done = now()

        def pn_evac(b, bb, t):
            for i in range(2):
                o = PN[:, i * 1024 + b * 512:i * 1024 + b * 512 + 512]
                r = DV(lambda e, o=o, s=bb[i]: e.tensor_copy(o, s.ap[:, :]), t)
                bb[i].free = [r]
                got["pn"].append(r)

        run(gemm("p2", 0, 2, 4, hA, lA, rc, "N", pn_evac))
        BP = half_tiles(8 * S, (24 + 8) * S)
        base = y_done
        run(gemm("bg2", 4, 4, 4, hA, lA, rc, "T", gate_evac(BP, "bp")))
        got["pp"] = []
        for w in range(4):
            bk = misc.next()
            for k in range(2):
                for i in range(2):
                    t = PE(lambda e, w=w, k=k, i=i, bk=bk: e.matmul(
                        bk.ap[:, k * 256:k * 256 + 256], PN[:, i * 1024 + (2 * w + k) * 128:i * 1024 + (2 * w + k) * 128 + 128],
                        PM[:, w, i, :], start=i == 0, stop=i == 1), got["pn"], l_cp, bk.free)
            tm = tm2.next()
            a = AC(lambda e, tm=tm, bk=bk: e.activation(tm.ap, bk.ap[:, :], ACT.Copy), t, tm.free)
            bk.free = [a]
            bk = misc.next()
            for m in range(2):
                for k in range(2):
                    t = PE(lambda e, w=w, k=k, m=m, bk=bk, tm=tm: e.matmul(
                        bk.ap[:, m * 256:m * 256 + 256], PG[:, k, w, m * 128:m * 128 + 128], tm.ap[:, k * 256:k * 256 + 256],
                        start=k == 0, stop=k == 1), a, bk.free)
            tm.free = [t]
            tm = tm2.next()
            for m in range(2):
                b = DV(lambda e, m=m, w=w, tm=tm, bk=bk: e.tensor_scalar(tm.ap[:, m * 256:m * 256 + 256], bk.ap[:, m * 256:m * 256 + 256],
                                                                        par("pool_scale", 2 * w + m), None, ALU.mult), t, tm.free)
            bk.free = [b]
            d = slice(w * 512, w * 512 + 512)
            z = split(HH[:, d], HL[:, d], tm.ap, b, y_done, on=PO)
            tm.free = [z]
            got["pp"].append(z)

        a_done = now()
        got["m"] = []

        def merge_evac(b, bb, t):
            for i in range(2):
                tm = tm2.next()
                r = DV(lambda e, tm=tm, s=bb[i], o=BP(4 * b + 2 * i, 2): e.tensor_tensor(tm.ap, s.ap[:, :], o, ALU.mult), t, got["bp"], tm.free)
                bb[i].free = [r]
                r = DV(lambda e, tm=tm, o=BG(4 * b + 2 * i, 2): e.tensor_tensor(tm.ap, tm.ap, o, ALU.add), r, got["yg"])
                d = slice(b * 1024 + i * 512, b * 1024 + i * 512 + 512)
                z = split(AH[:, d], AL[:, d], tm.ap, r, a_done, on=PO)
                tm.free = [z]
                got["m"].append(z)

        run(gemm("pout", 0, 4, 2, ap_of(HH), ap_of(HL), [got["pp"]] * 2, "T", merge_evac))

        def gated_x(which):
            def evac(b, bb, t):
                for i in range(2):
                    for m in range(2):
                        kt = 4 * b + 2 * i + m
                        x = X[:, kt * S:kt * S + S]
                        a = DV(lambda e, x=x: e.tensor_scalar(x, x, ALPHA, None, ALU.mult), got["x"])
                        r = DV(lambda e, x=x, kt=kt, m=m, s=bb[i]: e.scalar_tensor_tensor(
                            x, s.ap[:, m * 256:m * 256 + 256], mod(which, kt), x, ALU.mult, ALU.add), t, a)
                    bb[i].free = [r]
                got["xn"] = [r]
            return evac

        run(gemm("out2", 0, 4, 4, hA, lA, [got["m"]] * 4, "T", gated_x(2)))
        got["x"] = got["xn"]
        dbg("x5", X[:, :])

        def layer_norm(gain, bias):
            bk = misc.next()
            for k in range(16):
                t = PE(lambda e, k=k, bk=bk: e.matmul(bk.ap[:, 0:256], ones, X[:, k * S:k * S + S], start=k == 0, stop=k == 15),
                       got["x"], bk.free)
            a = AC(lambda e: e.activation(RS[:, 0:256], bk.ap[:, 0:256], ACT.Copy, scale=1.0 / D), t, state["rs"])
            bk.free = [a]
            cs = []
            for i in range(4):
                xv = X[:, 1024 * i:1024 * i + 1024].rearrange("p (k t) -> p k t", k=4)
                cs.append(DV(lambda e, xv=xv: e.tensor_tensor(xv, xv, RS[:, 0:256].unsqueeze(1).to_broadcast([P, 4, 256]), ALU.subtract), a))
            state["rs"] = [cs[-1]]
            r = rms_stats(X, sq, cs, eps=1e-5)
            for kt in range(16):
                x = X[:, kt * S:kt * S + S]
                t = DV(lambda e, x=x: e.tensor_tensor(x, x, RS[:, 0:256], ALU.mult), r)
                t = DV(lambda e, x=x, kt=kt: e.tensor_scalar(x, x, par(gain, kt), par(bias, kt), ALU.mult, ALU.add), t)
            got["x"] = [t]
            state["rs"] = [t]

        base = now()
        state["rs"] = base
        sq = [Place(G[:, E0 + 1536 + 1024 * i:E0 + 2560 + 1024 * i]) for i in range(2)]
        for s in sq:
            s.free = list(base)
        layer_norm("lnm_g", "lnm_b")
        dbg("x6", X[:, :])

        base = now()
        rf = modulate(X, lambda kt: mod(3, kt), lambda kt: mod(4, kt), sq, got["x"], base)
        hid_free = [base] * 24
        silu_tm = Ring([Place(G[:, E0 + 3584 + 512 * i:E0 + 4096 + 512 * i]) for i in range(3)])
        for s in silu_tm.places:
            s.free = list(base)

        def ffn_up(b0, nb):
            def evac(b, bb, t):
                kt = (2 * (b0 + b)) % 24
                tm = silu_tm.next()
                a = AC(lambda e, tm=tm: e.activation(tm.ap, bb[0].ap[:, :], ACT.Silu), t, tm.free)
                bb[0].free = [a]
                m = DV(lambda e, tm=tm: e.tensor_tensor(tm.ap, bb[1].ap[:, :], tm.ap, ALU.mult), a, t)
                bb[1].free = [m]
                d = slice(kt * S, kt * S + 512)
                z = split(HH[:, d], HL[:, d], tm.ap, m, hid_free[kt], on=PO)
                tm.free = [z]
                hid_ready[kt] = hid_ready[kt + 1] = z
            yield from gemm("fin", b0, nb, 4, hA, lA, rf, "T", evac)

        PARTS = [(0, 16), (16, 16), (32, 12)]
        first_part = [True]

        def ffn_down(part):
            a, n = PARTS[part]

            def evac(b, bb, t):
                for i in range(2):
                    for m in range(2):
                        kt = 4 * b + 2 * i + m
                        x = X[:, kt * S:kt * S + S]
                        w = got["x"]
                        if part == 0:
                            w = DV(lambda e, x=x: e.tensor_scalar(x, x, ALPHA, None, ALU.mult), got["x"], rf)
                        r = DV(lambda e, x=x, kt=kt, m=m, s=bb[i]: e.scalar_tensor_tensor(
                            x, s.ap[:, m * 256:m * 256 + 256], mod(5, kt), x, ALU.mult, ALU.add), t, w)
                    bb[i].free = [r]
                got["xn"] = [r]
            ready = [[hid_ready[(a + 4 * c + k) % 24] for k in range(4)] for c in range(n // 4)]
            yield from gemm(f"fout{part}", 0, 4, n // 4, lambda kt: HH[:, ((a + kt) % 24) * S:((a + kt) % 24 + 1) * S],
                            lambda kt: HL[:, ((a + kt) % 24) * S:((a + kt) % 24 + 1) * S], ready, "T", evac)
            got["x"] = got["xn"]
            for k in range(n):
                hid_free[(a + k) % 24] = [(PE.sem, PE.n)]

        def ffn():
            yield from ffn_up(0, 8)
            yield from ffn_up(8, 4)
            yield from ffn_down(0)
            yield from ffn_up(12, 4)
            yield from ffn_up(16, 4)
            yield from ffn_down(1)
            yield from ffn_up(20, 2)
            yield from ffn_down(2)

        run(ffn())
        dbg("x7", X[:, :])
        layer_norm("lnf_g", "lnf_b")
        o = Load(sem("s_out"))
        SP.dma(io["out"], X[:, :], o, got["x"])
        SP.wait([o.all(), spill.all()])
        if debug:
            PO.wait([dbg_load.all()])

        if order is None:
            return found
        assert found == order
    return found


def blocks(w, kt=4, width=512):
    k, n = w.shape
    v = w.reshape(k // (P * kt), kt, P, n // width, width)
    return np.ascontiguousarray(v.transpose(3, 0, 2, 1, 4)).reshape(-1, P, kt * width)


def padded(w, width):
    out = np.zeros((w.shape[0], width), w.dtype)
    return out, w


def columns(v):
    return v.reshape(-1, P).T


def tokens(x):
    return np.ascontiguousarray(x.reshape(S, -1, P).transpose(2, 1, 0)).reshape(P, -1)


def constants():
    t = np.arange(S)
    dist = t[:, None] - t[None, :]
    count = (((dist >= 0) & (dist <= 128)).astype(np.float64) + ((dist >= 0) & (dist % 4 == 0) & (dist // 4 <= 128))
             + ((dist >= 0) & (dist % 16 == 0) & (dist // 16 <= 128)))
    dil = np.where(count > 0, np.log(np.maximum(count, 1)), NEG).astype(np.float32)
    cau = np.where(dist >= 0, 0.0, NEG).astype(np.float32)
    end = np.arange(15) * 16 + 31
    valid = end[None, :] <= t[:, None]
    bcmp = np.where(valid, 0.0, NEG).astype(np.float32)
    rows = lambda a: a.reshape(2, P, -1).transpose(1, 0, 2).reshape(P, -1)
    pad = lambda a: np.pad(a, ((0, 0), (0, 32 - a.shape[1])))
    tri = (np.arange(P)[:, None] <= np.arange(P)[None, :]).astype(np.float32)
    mean = np.zeros((4, S, S))
    for i, w in enumerate((2, 4, 8, 16)):
        def axis(n):
            m = np.zeros((n, n))
            for a in range(n):
                lo, hi = max(a - w // 2, 0), min(a + w - w // 2, n)
                m[a, lo:hi] = 1.0 / (hi - lo)
            return m
        mean[i] = np.kron(axis(4), axis(64)) - np.eye(S)
    pm = mean.transpose(2, 0, 1).reshape(2, P, 4, S).transpose(1, 2, 0, 3).reshape(P, -1).astype(np.float32)
    scan = np.ones(512, np.float32)
    scan[::64] = 0
    scan_all = np.ones(512, np.float32)
    scan_all[::256] = 0
    j, i = np.arange(64)[:, None], np.arange(64)[None, :]
    masks = np.stack([np.tile((j <= i).astype(np.uint32), (2, 1)), np.tile((j >= i).astype(np.uint32), (2, 1))])
    return dict(dil=rows(dil), cau=rows(cau), bcmp=pad(rows(bcmp)), vcmp=pad(rows(valid.astype(np.float32))), tri=tri,
                pm=pm, scan=np.tile(scan, (P, 1)), scan_all=np.tile(scan_all, (P, 1)), masks=masks)


def layout(a):
    k = constants()
    wi, w2 = a["w_in"][0], a["w_in_2"][0]
    cat = np.concatenate
    cols = cat([wi[:, 0:1024], wi[:, 3584:4096], wi[:, 1024:2048], wi[:, 2048:2560], wi[:, 2560:3584],
                wi[:, 4096:4352], wi[:, 4608:4864], wi[:, 4352:4608], wi[:, 4864:5120]], axis=1)
    gates = np.zeros((D, 128), np.float32)
    gates[:, 0:24] = wi[:, 5120:5144]
    alr = np.zeros((D, 128), np.float32)
    alr[:, 0:16] = w2[:, 6144:6160]
    alr[:, 32:48] = w2[:, 6160:6176]
    dn = a["w_down"][0]
    fi, fo = a["w_ffn_in_2"][0], a["w_ffn_out_2"][0]
    pair = cat([x for b in range(22) for x in (fi[:, 256 * b:256 * b + 256], fi[:, 5632 + 256 * b:5632 + 256 * b + 256])], axis=1)
    ada = a["w_ada_2"][0].reshape(16, P, 6, CH).transpose(2, 0, 1, 3).reshape(96, P, CH)
    out = {
        "w_in": blocks(cols), "w_gates": blocks(gates, 16, 128), "w_alr": blocks(alr, 16, 128),
        "w_ck": blocks(a["cmp_k_w1"][0], 16, 128), "w_cv": blocks(a["cmp_v_w1"][0], 16, 128),
        "w_out": blocks(a["w_out"][0]), "w_xkv": blocks(a["xattn_wkv"][0]), "w_xq": blocks(a["xattn_wq"][0]),
        "w_xo": blocks(a["xattn_wo"][0]), "w_up": blocks(a["w_up"][0]),
        "w_down": cat([blocks(dn[2048 * q:2048 * q + 2048]) for q in range(4)]),
        "w_ada": np.ascontiguousarray(ada),
        "w_q2": blocks(w2[:, 0:1024]), "w_k2": blocks(w2[:, 1024:2048]), "w_v2": blocks(w2[:, 2048:4096]),
        "w_g2": blocks(w2[:, 4096:6144]), "w_p2": blocks(w2[:, 6176:7200]), "w_bg2": blocks(w2[:, 7200:11296]),
        "w_gout": blocks(a["w_gla_out_2"][0]), "w_pout": blocks(a["w_pool_out_2"][0]), "w_out2": blocks(a["w_out_2"][0]),
        "w_fin": blocks(pair), "w_fout0": blocks(fo[0:2048]), "w_fout1": blocks(fo[2048:4096]), "w_fout2": blocks(fo[4096:5632]),
    }
    small = cat([columns(np.asarray(x).reshape(-1)) for x in (
        a["norm_mix"], a["norm_xattn"], a["norm_mem"], a["norm_mlp"], a["final_norm"], a["b_ada_2"], a["gla_norm_gain_2"],
        a["pool_scale_2"], a["ln_mix_gain_2"], a["ln_mix_bias_2"], a["ln_ffn_gain_2"], a["ln_ffn_bias_2"], a["b_decay_up_2"],
        a["c_2"], a["c_ctx_2"])], axis=1)
    out["c_base"] = cat([np.eye(P, dtype=np.float32), np.ones((P, P), np.float32), small], axis=1)
    row = lambda v: np.tile(np.asarray(v).reshape(1, -1), (P, 1))
    ws = a["gmlp_w_s"][0].transpose(2, 0, 1).reshape(P, -1)
    out["c_attn"] = cat([k["dil"], k["cau"], k["bcmp"], k["vcmp"], row(a["gmlp_ln_g"]), row(a["gmlp_ln_b"]), row(a["gmlp_b_s"]), ws,
                         k["tri"], a["cmp_pos"][0].T, a["cmp_k_w2"][0], a["cmp_v_w2"][0]], axis=1)
    dec = np.zeros((P, 1024), np.float32)
    dec[0:16] = a["w_decay_up_2"][0, 0]
    dec[32:48] = a["w_decay_up_2"][0, 1]
    out["c_gla"] = cat([k["scan"], k["scan_all"], dec], axis=1)
    pg = a["w_pool_group_2"][0].reshape(4, 2, P, 256).transpose(2, 1, 0, 3).reshape(P, -1)
    out["c_pool"] = cat([k["pm"], pg], axis=1)
    out["masks"] = k["masks"]
    out["x_t"], out["mem_t"], out["ctx_t"] = tokens(a["x"][0]), tokens(a["mem"][0]), tokens(a["ctx_2"][0])
    return {n: np.ascontiguousarray(v) for n, v in out.items()}


def build(nc, shapes, debug=()):
    dts = {"float32": F32, "uint32": U32}
    io = {n: nc.dram_tensor(f"in_{n}", list(s), dts[d], kind="ExternalInput").ap() for n, (s, d) in shapes.items()}
    io["out"] = nc.dram_tensor("out_0", [P, KT * S], F32, kind="ExternalOutput").ap()
    io["state"] = nc.dram_tensor("state", [4, 2, P, 1024], F32).ap()
    dbg = {n: nc.dram_tensor("dbg_" + n, [P, w], F32, kind="ExternalOutput").ap() for n, w in debug}
    return io, dbg


def kernel(**inputs):
    from concourse import bacc
    from concourse.bass_utils import run_bass_kernel_spmd

    arrays = layout({n: np.asarray(v) for n, v in inputs.items()})
    shapes = {n: (v.shape, v.dtype.name) for n, v in arrays.items()}
    dry = bacc.Bacc("TRN2", target_bir_lowering=False, num_devices=1)
    order = program(dry, build(dry, shapes)[0], None)
    nc = bacc.Bacc("TRN2", target_bir_lowering=False, num_devices=1)
    program(nc, build(nc, shapes)[0], order)
    r = run_bass_kernel_spmd(nc, [{f"in_{n}": v for n, v in arrays.items()}], core_ids=[0])
    got = r.results[0]["out_0"]
    return np.ascontiguousarray(got.reshape(P, KT, S).transpose(2, 1, 0)).reshape(1, S, D)
```

```python
from contextlib import ExitStack

import numpy as np

import concourse.bass as bass
from concourse import mybir

F32 = mybir.dt.float32
F32R = mybir.dt.float32r
U32 = mybir.dt.uint32
ALU = mybir.AluOpType
ACT = mybir.ActivationFunctionType
AX = mybir.AxisListType.X

P = 128
S = 256
D = 2048
KT = D // P
CH = 2048
SCALE = 128 ** -0.5
ALPHA = 2.0 ** 0.25
NEG = -1e30
FFT = 44

PLAIN = ("ck", "cv")
NW, NR = 4, 4
HC = CH // 2

PAR = {}
_at = 0
for _n, _w in (("norm_mix", 16), ("norm_xattn", 16), ("norm_mem", 16), ("norm_mlp", 16), ("final_norm", 16),
               ("b_ada", 96), ("gla_gain", 16), ("pool_scale", 8), ("lnm_g", 16), ("lnm_b", 16),
               ("lnf_g", 16), ("lnf_b", 16), ("b_decay", 16), ("c", 16), ("c_ctx", 16)):
    PAR[_n] = (_at, _at + _w)
    _at += _w
NPAR = _at

CA = {}
_at = 0
for _n, _w in (("dil", 512), ("cau", 512), ("bcmp", 32), ("vcmp", 32), ("ln_g", 512), ("ln_b", 512),
               ("b_s", 512), ("w_s", 512), ("tri", 128), ("pos", 32), ("ckw2", 128), ("cvw2", 128)):
    CA[_n] = (_at, _at + _w)
    _at += _w
NCA = _at

CG = {}
_at = 0
for _n, _w in (("scan", 512), ("pad", 512), ("decay", 1024)):
    CG[_n] = (_at, _at + _w)
    _at += _w
NCG = _at
CP = {"mean": (0, 2048), "group": (2048, 4096)}
NCP = 4096


class Queue:

    def __init__(self, engine, sem):
        self.engine, self.sem, self.n, self.seen = engine, sem, 0, {}

    def wait(self, waits):
        most = {}
        for w in flat(waits):
            key = w[0].name
            if w[1] > self.seen.get(key, 0) and w[1] > most.get(key, (0, 0))[1]:
                most[key] = w
        for key, (sem, value) in most.items():
            self.seen[key] = value
            self.engine.wait_ge(sem, value)

    def __call__(self, make, *waits, mark=True):
        self.wait(waits)
        ins = make(self.engine)
        if not mark:
            return None
        self.n += 1
        ins.then_inc(self.sem, 1)
        return (self.sem, self.n)

    def dma(self, out, in_, load, *waits):
        self.wait(waits)
        load.n += 16
        self.engine.dma_start(out, in_).then_inc(load.sem, 16)
        return (load.sem, load.n)


def flat(x):
    if x is None:
        return []
    if isinstance(x, tuple) and len(x) == 2 and isinstance(x[1], int):
        return [x]
    return [w for y in x for w in flat(y)]


class Load:

    def __init__(self, sem):
        self.sem, self.n = sem, 0

    def all(self):
        return (self.sem, self.n)


class Place:

    def __init__(self, ap):
        self.ap, self.free = ap, []


class Ring:
    def __init__(self, places):
        self.places, self.i = places, 0

    def next(self):
        self.i += 1
        return self.places[(self.i - 1) % len(self.places)]


def program(nc, io, order):
    st = ExitStack()
    found = []
    with st:
        def sem(name):
            return st.enter_context(nc.semaphore(name))

        def sb(name, width, dt=F32):
            return st.enter_context(nc.sbuf_tensor(name, [P, width], dt))

        PE, DV, AC, PO, SP = (Queue(e, sem(n)) for e, n in (
            (nc.tensor, "s_pe"), (nc.vector, "s_dve"), (nc.scalar, "s_act"), (nc.gpsimd, "s_pool"), (nc.sync, "s_sp")))
        everyone = (PE, DV, AC, PO)

        def now():
            return [(q.sem, q.n) for q in everyone if q.n]

        RW = sb("RW", NW * CH)
        RH = sb("RH", NR * HC, F32R)
        RL = sb("RL", NR * HC, F32R)
        X = sb("X", KT * S)
        AH = sb("AH", KT * S, F32R)
        AL = sb("AL", KT * S, F32R)
        C = sb("C", 256 + NPAR)
        MODT = sb("MODT", 96 + 32)
        RS = sb("RS", 3 * 256)
        SM = sb("SM", 160)
        over = ExitStack()
        HH = over.enter_context(nc.sbuf_tensor("HH", [P, 24 * S], F32R))
        HL = over.enter_context(nc.sbuf_tensor("HL", [P, 24 * S], F32R))
        over.close()
        NE = 10048
        G = sb("G", 48 * S + NE)
        E0 = 48 * S
        banks = [Place(st.enter_context(nc.psum_tensor(f"b{i}", [P, 512], F32))) for i in range(8)]
        pairs = Ring([Place((banks[0], banks[1])), Place((banks[2], banks[3]))])
        misc = Ring(banks[4:8])

        def g(at, n, **split):
            ap = G[:, at:at + n]
            if split:
                (keys, sizes), = [(k, v) for k, v in split.items()]
            return ap

        ident, ones = C[:, 0:128], C[:, 128:256]

        def par(name, i=None):
            a, b = PAR[name]
            return C[:, 256 + a:256 + b] if i is None else C[:, 256 + a + i:256 + a + i + 1]

        def mod(i, kt):
            return MODT[:, 16 * i + kt:16 * i + kt + 1]

        def cmod(i, kt):
            return MODT[:, 96 + 16 * i + kt:96 + 16 * i + kt + 1]

        w_sems = [Load(sem(f"s_w{i}")) for i in range(NW)]
        loaded, ready_at, prepared = {}, {}, [0]
        gem_used = []
        state = {"gemm": 0, "half": 0}
        side_todo = []
        side = {}

        def send(j, waits):
            if order is None or j >= len(order):
                return
            name, i = order[j]
            k = j % NW
            SP.dma(RW[:, k * CH:(k + 1) * CH], io["w_" + name][i], w_sems[k], waits)
            loaded[j] = w_sems[k].all()

        def part(t, n):
            return t[:, n % NR * HC:n % NR * HC + HC]

        def prepare():
            j = prepared[0]
            name, i = order[j]
            k = j % NW
            while j not in loaded:
                step_side()
            w = RW[:, k * CH:(k + 1) * CH]
            if name in side:
                side_todo.append((j, side[name](i, w, loaded[j])))
                prepared[0] += 1
                return
            else:
                n, half = state["gemm"], state["half"]
                state["gemm"] += 1
                state["half"] = 1 - half
                free = gem_used[n - NR] if n >= NR else None
                hi, lo = part(RH, n), part(RL, n)
                w = w[:, half * HC:half * HC + HC]
                h = AC(lambda e: e.activation(hi, w, ACT.Copy), loaded[j], free)
                lo_t = DV(lambda e: e.tensor_tensor(lo, w, hi.bitcast(F32), ALU.subtract), h, free)
                ready_at[j, half] = (n, h, lo_t)
                if half == 0:
                    return
                done = lo_t
            prepared[0] += 1
            send(j + NW, done)

        def step_side():
            j, gen = side_todo[0]
            done = next(gen)
            if done is not None:
                side_todo.pop(0)
                send(j + NW, done)

        def take(name, i, half):
            if half == 0:
                state["at"] = len(found)
                found.append((name, i))
            j = state["at"]
            if order is None:
                return 0, None, None
            assert order[j] == (name, i), (order[j], name, i)
            while (j, half) not in ready_at:
                prepare()
            n, h, lo_t = ready_at[j, half]
            while prepared[0] < len(order) and (order[prepared[0]][0] in side or state["gemm"] < n + NR):
                if order[prepared[0]][0] in PLAIN or (order[prepared[0]][0] not in side and state["gemm"] - NR >= len(gem_used)):
                    break
                prepare()
            return n, h, lo_t

        def take_side(name, i):
            j = len(found)
            found.append((name, i))
            if order is None:
                gen = side[name](i, RW[:, 0:CH], None)
                return lambda: next(gen)
            assert order[j] == (name, i)
            while prepared[0] <= j:
                prepare()

            def piece():
                if side_todo and side_todo[0][0] <= j:
                    step_side()
            return piece

        def used(mark):
            gem_used.append(mark)

        def gemm(name, first, n_blocks, kc, hi, lo, ready, form, evac, dirs=2):
            for b in range(n_blocks):
                pair = pairs.next()
                bb = pair.ap
                for c in range(2 * kc):
                    n, wh_t, wl_t = take(name, (first + b) * kc + c // 2, c % 2)
                    wh = part(RH, n).rearrange("p (k n) -> p k n", k=2)
                    wl = part(RL, n).rearrange("p (k n) -> p k n", k=2)
                    PE.wait([wh_t, wl_t, ready[c // 2], bb[0].free, bb[1].free])
                    t = None
                    if form == "T":
                        for m in range(4):
                            out = bb[m // 2].ap[:, (m % 2) * 256:(m % 2) * 256 + 256]
                            for k in range(2):
                                cols = slice(m * 128, m * 128 + 128)
                                start = c == 0 and k == 0 and m % 2 == 0
                                stop = c == 2 * kc - 1 and k == 1
                                for q, (l, r) in enumerate(((wh, hi), (wh, lo), (wl, hi))):
                                    lhs, rhs = l[:, k, cols], r(2 * c + k)
                                    a, z = start and q == 0, stop and q == 2
                                    last = m == 3 and k == 1 and q == 2
                                    t = PE(lambda e, o=out, l=lhs, r=rhs, a=a, z=z: e.matmul(
                                        o, l, r, start=a, stop=z, skip_group_check=True), mark=last) or t
                    else:
                        for m in range(2):
                            out = bb[m].ap[:, :]
                            for k in range(2):
                                start, stop = c == 0 and k == 0, c == 2 * kc - 1 and k == 1
                                for q, (l, r) in enumerate(((hi, wh), (lo, wh), (hi, wl))):
                                    lhs, rhs = l(2 * c + k)[:, m * 128:m * 128 + 128], r[:, k, :]
                                    a, z = start and q == 0, stop and q == 2
                                    last = m == 1 and k == 1 and q == 2
                                    t = PE(lambda e, o=out, l=lhs, r=rhs, a=a, z=z: e.matmul(
                                        o, l, r, start=a, stop=z, skip_group_check=True), mark=last) or t
                    used(t)
                    yield
                evac(b, bb, t)
                yield

        def small(name, hi, lo, ready, out):
            for half in range(2):
                n, wh_t, wl_t = take(name, 0, half)
                wh = part(RH, n).rearrange("p (k n) -> p k n", k=8)
                wl = part(RL, n).rearrange("p (k n) -> p k n", k=8)
                PE.wait([wh_t, wl_t, ready, out.free])
                t = None
                for k in range(8):
                    for q, (l, r) in enumerate(((wh, hi), (wh, lo), (wl, hi))):
                        t = PE(lambda e, l=l[:, k, :], r=r(8 * half + k), a=half == k == q == 0, z=half == 1 and k == 7 and q == 2: e.matmul(
                            out.ap[:, 0:256], l, r, start=a, stop=z), mark=k == 7 and q == 2) or t
                used(t)
            return t

        def ap_of(t, base=0):
            return lambda kt: t[:, (base + kt) * S:(base + kt + 1) * S]

        def split(hi, lo, src, *waits, on=None):
            h = AC(lambda e: e.activation(hi, src, ACT.Copy), *waits)
            return (on or DV)(lambda e: e.tensor_tensor(lo, src, hi.bitcast(F32), ALU.subtract), h, *waits)

        class Sums:

            def __init__(self, acc, tmps):
                self.acc, self.tmps, self.n, self.t = acc, tmps, 0, None

            def square(self, x, *waits):
                if self.n == 0:
                    self.t = AC(lambda e: e.activation(self.acc.ap, x, ACT.Square), *waits, self.acc.free)
                else:
                    tm = self.tmps.next()
                    a = AC(lambda e: e.activation(tm.ap, x, ACT.Square), *waits, tm.free)
                    self.t = DV(lambda e: e.tensor_tensor(self.acc.ap, self.acc.ap, tm.ap, ALU.add), a, self.t)
                    tm.free = [self.t]
                self.n += 1

            def plain(self, x, *waits):
                if self.n == 0:
                    self.t = DV(lambda e: e.tensor_copy(self.acc.ap, x), *waits, self.acc.free)
                else:
                    self.t = DV(lambda e: e.tensor_tensor(self.acc.ap, self.acc.ap, x, ALU.add), *waits, self.t)
                self.n += 1

            def over_partitions(self):
                bk = misc.next()
                for k in range(2):
                    t = PE(lambda e: e.matmul(bk.ap[:, 0:256], ones, self.acc.ap[:, k * 256:k * 256 + 256],
                                              start=k == 0, stop=k == 1), self.t, bk.free)
                self.acc.free = [t]
                return bk, t

        def rstd(sums, eps=1e-6):
            bk, t = sums.over_partitions()
            a = DV(lambda e: e.tensor_scalar(RS[:, 256:512], bk.ap[:, 0:256], 1.0 / D, eps, ALU.mult, ALU.add), t, state.get("rs"))
            bk.free = [a]
            b = AC(lambda e: e.activation(RS[:, 512:768], RS[:, 256:512], ACT.Sqrt), a)
            return DV(lambda e: e.reciprocal(RS[:, 0:256], RS[:, 512:768]), b, state.get("rs"))

        R2 = RS[:, 0:256].unsqueeze(1).to_broadcast([P, 2, 256])
        RC = SM[:, 128:130]

        def pair2(ap):
            return ap.rearrange("p (k t) -> p k t", k=2)

        def rstd_columns(r):
            bk = misc.next()
            for i in range(2):
                t = PE(lambda e: e.transpose(bk.ap[:, i * 128:i * 128 + 128], RS[:, i * 128:i * 128 + 128], ident), r, bk.free)
            c = DV(lambda e: e.tensor_copy(RC, bk.ap[:, 0:256:128]), t, state.get("rc"))
            bk.free = [c]
            return c

        def feed(src, kt, gain, hi, lo, waits, free):
            for k in (kt, kt + 1):
                d = slice(k * S, k * S + S)
                h = AC(lambda e: e.activation(hi[:, d], src[:, d], ACT.Copy, scale=par(gain, k)), waits, free)
                t = DV(lambda e: e.scalar_tensor_tensor(lo[:, d], src[:, d], par(gain, k), hi[:, d].bitcast(F32),
                                                        ALU.mult, ALU.subtract), h, waits, free)
            return t

        def load(name, out, in_, waits=()):
            ld = Load(sem("s_l_" + name))
            PO.dma(out, in_, ld, *waits)
            return ld.all()

        for j in range(NW):
            send(j, None)
        l_c = load("c", C[:, :], io["c_base"])
        l_x = [load(f"x{i}", X[:, 1024 * i:1024 * i + 1024], io["x_t"][:, 1024 * i:1024 * i + 1024]) for i in range(4)]
        l_ca = load("ca", G[:, E0:E0 + NCA], io["c_attn"])
        debug = io.get("debug", {})
        dbg_load = Load(sem("s_dbg")) if debug else None

        def dbg(name, ap):
            if name in debug:
                w = PO.dma(debug[name], ap, dbg_load, now())
                for q in everyone:
                    q.wait([w])

        def ca(name):
            a, b = CA[name]
            return G[:, E0 + a:E0 + b]

        F0 = E0 + NCA
        SCR = F0
        XK, XV = G[:, F0 + 4096:F0 + 5120], G[:, F0 + 5120:F0 + 6144]
        GN, KC, VC = G[:, F0 + 6144:F0 + 6208], G[:, F0 + 6208:F0 + 6240], G[:, F0 + 6240:F0 + 6496]
        assert F0 + 6496 <= E0 + NE
        bufs = [Place(G[:, SCR + 512 * i:SCR + 512 * i + 512]) for i in range(8)]
        sums = Sums(bufs[0], Ring(bufs[1:3]))
        hA, lA = ap_of(AH), ap_of(AL)
        ra = []
        for c in range(4):
            for kt in (4 * c, 4 * c + 2):
                t = feed(X, kt, "norm_mix", AH, AL, [l_x[c], l_c], None)
                sums.square(X[:, kt * S:kt * S + 512], l_x[c])
            ra.append(t)
        R = RCt = None

        UA, VA, QKB, QC = G[:, 0:1024], G[:, 1024:2048], G[:, 2048:4096], G[:, 4096:6144]
        VB, CKV, GT = G[:, 6144:7168], G[:, 7168:8192], G[:, 8192:8448]
        KSW, VSW = G[:, 10240:11264], G[:, 11264:12288]
        got = {}

        def to(dst, key, func=None, free=None):
            def evac(b, bb, t):
                for i in range(2):
                    o = dst[:, b * 1024 + i * 512:b * 1024 + i * 512 + 512]
                    r = DV(lambda e: e.tensor_tensor(pair2(o), pair2(bb[i].ap[:, :]), R2, ALU.mult), t, R, free)
                    bb[i].free = [r]
                    if func is not None:
                        r = AC(lambda e: e.activation(o, o, func), r)
                    got.setdefault(key, []).append(r)
                state["rs"] = [(DV.sem, DV.n)]
            return evac

        def to_n(dst, key, func=ACT.Copy, free=None):
            def evac(b, bb, t):
                for i in range(2):
                    o = dst[:, i * 512:i * 512 + 512]
                    r = AC(lambda e: e.activation(o, bb[i].ap[:, :], func, scale=RC[:, i:i + 1]), t, RCt, free)
                    bb[i].free = [r]
                    got.setdefault(key, []).append(r)
                state["rc"] = [r]
            return evac

        def run(*gens):
            gens = list(gens)
            while gens:
                for x in list(gens):
                    if next(x, "end") == "end":
                        gens.remove(x)

        def w_in(*names):
            for name in names:
                if name == "ua":
                    yield from gemm("in", 0, 1, 4, hA, lA, ra, "T", to(UA, "ua", ACT.Gelu_apprx_tanh))
                elif name == "va":
                    yield from gemm("in", 1, 1, 4, hA, lA, ra, "N", to_n(VA, "va", ACT.Gelu_apprx_tanh))
                elif name == "ckv":
                    yield from gemm("in", 2, 1, 4, hA, lA, ra, "T", to(CKV, "ckv"))
                elif name == "qkb":
                    yield from gemm("in", 3, 2, 4, hA, lA, ra, "T", to(QKB, "qkb"))
                elif name == "vb":
                    yield from gemm("in", 5, 1, 4, hA, lA, ra, "N", to_n(VB, "vb"))
                elif name == "qc":
                    yield from gemm("in", 6, 2, 4, hA, lA, ra, "T", to(QC, "qc"))
                elif name == "ksw":
                    yield from gemm("in", 8, 1, 4, hA, lA, ra, "T", to(KSW, "ksw"))
                elif name == "vsw":
                    yield from gemm("in", 9, 1, 4, hA, lA, ra, "N", to_n(VSW, "vsw", free=got["b1free"]))
                elif name == "gates":
                    bk = misc.next()
                    t = small("gates", hA, lA, ra, bk)
                    r = DV(lambda e: e.tensor_tensor(GT[0:32, :], bk.ap[0:32, 0:256], RS[0:32, 0:256], ALU.mult), t, R)
                    bk.free = [r]
                    state["rs"] = [r]
                    r = AC(lambda e: e.activation(GT[0:32, :], GT[0:32, :], ACT.Sigmoid), r)
                    bk = misc.next()
                    for i in range(2):
                        t = PE(lambda e: e.transpose(bk.ap[:, i * 32:i * 32 + 32], GT[0:32, i * 128:i * 128 + 128],
                                                     ident[0:32, 0:32]), r, bk.free)
                    r = DV(lambda e: e.tensor_copy(GN, bk.ap[:, 0:64]), t)
                    bk.free = [r]
                    got["gates"] = [r]

        SIL = SM[:, 132:132 + 16], SM[:, 132:132 + 16]
        SILT = sb("SILT", 32)
        sil = AC(lambda e: e.activation(SILT[:, :], C[:, 256 + PAR["c"][0]:256 + PAR["c_ctx"][1]], ACT.Silu), l_c)
        ada_at = {"acc": None, "t": [[None] * 4, [None] * 4]}

        def ada(i, w, ld):
            cb, kt = divmod(i, 16)
            done = []
            for m in range(4):
                for which in range(2 if cb < 2 else 1):
                    pl = ada_at["acc"][which]
                    d = slice(512 * m, 512 * m + 512)
                    a, s_ = pl.ap[:, d], SILT[:, which * 16 + kt:which * 16 + kt + 1]
                    if kt == 0:
                        t = DV(lambda e: e.tensor_scalar(a, w[:, d], s_, None, ALU.mult), ld, sil, pl.free)
                    else:
                        t = DV(lambda e: e.scalar_tensor_tensor(a, w[:, d], s_, a, ALU.mult, ALU.add), ld, ada_at["t"][which][m])
                    ada_at["t"][which][m] = t
                    done.append(t)
                    if kt == 15:
                        ada_late.append([2, cb, m, which, pl, t])
                yield done if m == 3 else None

        def over_rows(cb, m, which, pl, t):
            bk = misc.next()
            for j in range(4):
                p = PE(lambda e: e.transpose(bk.ap[:, j * 128:j * 128 + 128],
                                             pl.ap[:, (4 * m + j) * 128:(4 * m + j) * 128 + 128], ident), t, bk.free)
            o = 96 * which + cb * 16 + 4 * m
            r = DV(lambda e: e.tensor_reduce(MODT[:, o:o + 4], bk.ap[:, :].rearrange("p (j t) -> p j t", j=4), AX, ALU.add), p)
            bk.free = [r]
            pl.free = [pl.free, p]
            r = DV(lambda e: e.tensor_tensor(MODT[:, o:o + 4], MODT[:, o:o + 4],
                                             par("b_ada")[:, cb * 16 + 4 * m:cb * 16 + 4 * m + 4], ALU.add), r)
            got.setdefault("mod", []).append(r)

        ada_late = []
        side["ada"] = ada

        def late(age=1):
            for x in ada_late:
                x[0] -= age
            while ada_late and ada_late[0][0] <= 0:
                over_rows(*ada_late.pop(0)[1:])

        def ada_steps(blocks_of_columns, pause):
            due = 0.0
            for cb in blocks_of_columns:
                for kt in range(16):
                    due += 2 * pause - 1
                    while due >= 1:
                        due -= 1
                        yield
                    piece = take_side("ada", cb * 16 + kt)
                    for m in range(4):
                        if m == 2:
                            yield
                        late()
                        piece()
            for _ in range(2):
                yield
                late()

        def both(*gens):
            gens = list(gens)
            while gens:
                for x in list(gens):
                    if next(x, "end") == "end":
                        gens.remove(x)
                yield

        def slow(gen, pause):
            due = 0.0
            for _ in gen:
                due += pause
                while due >= 1:
                    due -= 1
                    yield

        def late_rstd(sums, columns=False):
            nonlocal R, RCt
            yield
            yield
            R = rstd(sums)
            if columns:
                RCt = rstd_columns(R)

        run(w_in("ckv", "qkb", "vb", "ua", "va"), late_rstd(sums, True))
        scr = Ring(bufs[0:5])
        pts = Ring(bufs[5:8])
        base = now()
        for b_ in bufs:
            b_.free = list(base)
        sms = Ring([Place(SM[:, 8 * i:8 * i + 8]) for i in range(8)])
        in_done = []

        def gmlp():
            sm = sms.next()
            W = scr.next()
            w_m = pts.next()
            mk = DV(lambda e: e.tensor_tensor(
                w_m.ap.rearrange("p (g t) -> p g t", g=4), ca("w_s").rearrange("p (g t) -> p g t", g=4),
                ca("tri").unsqueeze(1).to_broadcast([P, 4, 128]), ALU.mult), l_ca, w_m.free)
            outs = []
            for i in range(2):
                v = VA[:, i * 512:i * 512 + 512]
                a = AC(lambda e, v=v, i=i: e.activation(W.ap, v, ACT.Copy, accum_out=sm.ap[:, i:i + 1]), got["va"], W.free, sm.free)
                b = DV(lambda e, i=i: e.tensor_scalar(sm.ap[:, i:i + 1], sm.ap[:, i:i + 1], -1.0 / 512, None, ALU.mult), a)
                c = DV(lambda e, v=v, i=i: e.tensor_scalar(v, v, sm.ap[:, i:i + 1], None, ALU.add), b)
                d = AC(lambda e, v=v, i=i: e.activation(W.ap, v, ACT.Square, accum_out=sm.ap[:, 2 + i:3 + i]), c)
                W.free = [d]
                f = DV(lambda e, i=i: e.tensor_scalar(sm.ap[:, 2 + i:3 + i], sm.ap[:, 2 + i:3 + i], 1.0 / 512, 1e-6, ALU.mult, ALU.add), d)
                h = AC(lambda e, i=i: e.activation(sm.ap[:, 4 + i:5 + i], sm.ap[:, 2 + i:3 + i], ACT.Sqrt), f)
                k = DV(lambda e, i=i: e.reciprocal(sm.ap[:, 6 + i:7 + i], sm.ap[:, 4 + i:5 + i]), h)
                m = DV(lambda e, v=v, i=i: e.scalar_tensor_tensor(v, v, sm.ap[:, 6 + i:7 + i], ca("ln_g"), ALU.mult, ALU.mult), k)
                o = DV(lambda e, v=v: e.tensor_tensor(v, v, ca("ln_b"), ALU.add), m)
                outs.append(o)
            sm.free = [outs[-1]]
            yield
            bk = [misc.next(), misc.next()]
            ts = []
            for i in range(2):
                for q in range(4):
                    t = PE(lambda e, i=i, q=q: e.matmul(
                        bk[q // 2].ap[:, (q % 2) * 256 + i * 128:(q % 2) * 256 + i * 128 + 128],
                        VA[:, i * 512 + q * 128:i * 512 + q * 128 + 128], w_m.ap[:, q * 128:q * 128 + 128],
                        start=True, stop=True), outs[i], mk, bk[0].free, bk[1].free)
            w_m.free = [t]
            yield
            for j in range(2):
                W = scr.next()
                bs = ca("b_s")[:, j * 256:j * 256 + 256].rearrange("p (g t) -> p g t", g=2).unsqueeze(2).to_broadcast([P, 2, 2, 128])
                a = DV(lambda e, j=j, W=W, bs=bs: e.tensor_tensor(
                    W.ap.rearrange("p (g i t) -> p g i t", g=2, i=2), bk[j].ap[:, :].rearrange("p (g i t) -> p g i t", g=2, i=2),
                    bs, ALU.add), t, W.free)
                bk[j].free = [a]
                b = DV(lambda e: e.tensor_tensor(UA[:, j * 512:j * 512 + 512], W.ap, UA[:, j * 512:j * 512 + 512], ALU.mult), a, got["ua"])
                W.free = [b]
                got.setdefault("whole", []).append(b)
                yield

        def scores(qT, kT, bias, gate, ready, n=256):
            bk, sc, sm = misc.next(), scr.next(), sms.next()
            for i in range(2):
                t = PE(lambda e, i=i: e.matmul(bk.ap[:, i * n:i * n + n], qT[:, i * 128:i * 128 + 128], kT,
                                               start=True, stop=True), ready, bk.free)
            sv = sc.ap[:, 0:2 * n].rearrange("p (i k) -> p i k", i=2)
            if bias is not None:
                a = DV(lambda e: e.scalar_tensor_tensor(sc.ap[:, 0:2 * n], bk.ap[:, 0:2 * n], SCALE, bias, ALU.mult, ALU.add),
                       t, sc.free, l_ca)
                bk.free = [a]
                m = DV(lambda e: e.tensor_reduce(sm.ap[:, 0:2], sv, AX, ALU.max, negate=True), a, sm.free)
                src, scale = sc.ap, 1.0
            else:
                a = DV(lambda e: e.tensor_reduce(sm.ap[:, 6:8], bk.ap[:, 0:2 * n].rearrange("p (i k) -> p i k", i=2), AX, ALU.max,
                                                 negate=True), t, sm.free)
                m = DV(lambda e: e.tensor_scalar(sm.ap[:, 0:2], sm.ap[:, 6:8], SCALE, None, ALU.mult), a)
                src, scale = bk.ap, SCALE
            for i in range(2):
                b = AC(lambda e, i=i: e.activation(sc.ap[:, i * n:i * n + n], src[:, i * n:i * n + n], ACT.Exp,
                                                   bias=sm.ap[:, i:i + 1], scale=scale, accum_out=sm.ap[:, 2 + i:3 + i]), m, sc.free)
            if bias is None:
                bk.free = [b]
            r = DV(lambda e: e.reciprocal(sm.ap[:, 4:6], sm.ap[:, 2:4]), b)
            if gate is not None:
                r = DV(lambda e: e.tensor_tensor(sm.ap[:, 4:6], sm.ap[:, 4:6], gate, ALU.mult), r, got["gates"])
            p = DV(lambda e: e.tensor_tensor(sv, sv, sm.ap[:, 4:6].unsqueeze(2).to_broadcast([P, 2, n]), ALU.mult), r)
            sm.free = [p]
            return sc, p

        def turned(sc, p, n=256, causal=True):
            bk, pt = misc.next(), pts.next()
            if n < 128:
                for i in range(2):
                    t = PE(lambda e, i=i: e.transpose(bk.ap[0:n, i * 128:i * 128 + 128], sc.ap[:, i * n:i * n + n], ident), p, bk.free)
                c = AC(lambda e: e.activation(pt.ap[0:n, 0:256], bk.ap[0:n, 0:256], ACT.Copy), t, pt.free)
                blocks = [(0, 0), (1, 0)]
            else:
                blocks = [(0, 0), (1, 0), (1, 1)] if causal else [(0, 0), (0, 1), (1, 0), (1, 1)]
                for j, (i, k) in enumerate(blocks):
                    t = PE(lambda e, i=i, k=k, j=j: e.transpose(
                        bk.ap[:, j * 128:j * 128 + 128], sc.ap[:, i * 256 + k * 128:i * 256 + k * 128 + 128], ident), p, bk.free)
                w = len(blocks) * 128
                c = AC(lambda e: e.activation(pt.ap[:, 0:w], bk.ap[:, 0:w], ACT.Copy), t, pt.free)
            sc.free = [t]
            bk.free = [c]
            return pt, c, blocks

        def attend(units, out_hi, out_lo, extra):
            bk = misc.next()
            for i in range(2):
                ops = [(pt, j, n, v(k), c) for (pt, c, blocks), v, n in units for j, (ii, k) in enumerate(blocks) if ii == i]
                for a, (pt, j, n, v, c) in enumerate(ops):
                    t = PE(lambda e, i=i, j=j, n=n, v=v, pt=pt, a=a, z=len(ops) - 1: e.matmul(
                        bk.ap[:, i * 128:i * 128 + 128], v, pt.ap[0:n, j * 128:j * 128 + 128], start=a == 0, stop=a == z),
                        c, bk.free, extra)
            for (pt, _, _), _, _ in units:
                pt.free = [t]
            if out_lo is None:
                r = AC(lambda e: e.activation(out_hi, bk.ap[:, 0:256], ACT.Copy), t)
                bk.free = [r]
                got.setdefault("whole", []).append(r)
                return
            h = AC(lambda e: e.activation(out_hi, bk.ap[:, 0:256], ACT.Copy), t, in_done)
            r = DV(lambda e: e.tensor_tensor(out_lo, bk.ap[:, 0:256], out_hi.bitcast(F32), ALU.subtract), h, t, in_done)
            bk.free = [r]
            got.setdefault("mix", []).append(r)

        def dilated():
            held = None
            for h in range(5):
                new = None
                if h < 4:
                    new = scores(QKB[:, h * 256:h * 256 + 256], QKB[:, 1024 + h * 256:1024 + h * 256 + 256], ca("dil"), None, got["qkb"])
                    yield
                if held is not None:
                    tr = turned(*held)
                    attend([(tr, lambda k, h=h: VB[:, k * 512 + (h - 1) * 128:k * 512 + h * 128], 128)],
                           QKB[:, (h - 1) * S:h * S], None, got["vb"])
                    yield
                held = new

        B1 = VSW[:, 0:960]

        def compress():
            for kv in range(2):
                w_name = ("ck", "cv")[kv]
                hid = misc.next()
                vb = B1.rearrange("p (g n j) -> p g n j", g=2, n=15)
                ov = CKV[:, kv * 512:kv * 512 + 512].rearrange("p (g n j) -> p g n j", g=2, n=16)
                po = ca("pos").rearrange("p (h j) -> p h j", h=2)
                for h in range(2):
                    a = DV(lambda e, h=h: e.tensor_tensor(
                        vb[:, :, :, h * 16:h * 16 + 16], ov[:, :, h:h + 15, :],
                        po[:, h, :].unsqueeze(1).unsqueeze(1).to_broadcast([P, 2, 15, 16]), ALU.add),
                        got["ckv"], l_ca, got.get("b1free"))
                t = None
                for c in range(2):
                    w, wt, rel = take_plain(w_name, c)
                    for j in range(16):
                        jj = 16 * c + j
                        t = PE(lambda e, w=w, j=j, jj=jj: e.matmul(
                            hid.ap[:, 0:30], w[:, j * 128:j * 128 + 128], vb[:, :, :, jj], start=jj == 0, stop=jj == 31),
                            wt, a, hid.free, mark=j == 15) or t
                    rel(t)
                    yield
                got["b1free"] = [t]
                h_sb = sms8.next()
                b = AC(lambda e: e.activation(h_sb.ap[:, 0:30], hid.ap[:, 0:30], ACT.Gelu_apprx_tanh), t, h_sb.free)
                hid.free = [b]
                o = misc.next()
                if kv == 0:
                    t = PE(lambda e: e.matmul(o.ap[:, 0:30], ca("ckw2"), h_sb.ap[:, 0:30], start=True, stop=True), b, o.free)
                    r = DV(lambda e: e.tensor_copy(KC[:, 0:30], o.ap[:, 0:30]), t)
                    got["kc"] = [r]
                else:
                    for q in range(2):
                        t = PE(lambda e, q=q: e.matmul(o.ap[0:15, q * 128:q * 128 + 128], h_sb.ap[:, q * 15:q * 15 + 15],
                                                       ca("cvw2"), start=True, stop=True), b, o.free)
                    r = DV(lambda e: e.tensor_copy(VC[0:15, :], o.ap[0:15, 0:256]), t)
                    got["vc"] = [r]
                o.free = [r]
                h_sb.free = [t]
                yield

        sms8 = Ring([Place(SM[:, 64 + 32 * i:64 + 32 * i + 32]) for i in range(2)])
        def take_plain(name, i):
            j = len(found)
            found.append((name, i))
            if order is None:
                return RW[:, 0:CH], None, lambda t: None
            assert order[j] == (name, i)
            while prepared[0] < j:
                prepare()
            assert prepared[0] == j
            prepared[0] += 1
            k = j % NW
            return RW[:, k * CH:(k + 1) * CH], loaded[j], lambda t: send(j + NW, t)

        def nsa():
            held = None
            for h in range(9):
                new = None
                if held is not None:
                    tc = turned(*held[0], n=15)
                if h < 8:
                    q, gq = QC[:, h * 256:h * 256 + 256], h // 4
                    gate = lambda i: GN.rearrange("p (i c) -> p i c", i=2)[:, :, h * 3 + i]
                    sc, p = scores(q, KC[:, gq * 15:gq * 15 + 15], ca("bcmp")[:, 0:30], gate(0), [got["qc"], got["kc"]], n=15)
                    p = DV(lambda e: e.tensor_tensor(sc.ap[:, 0:30], sc.ap[:, 0:30], ca("vcmp")[:, 0:30], ALU.mult), p)
                    yield
                    if held is not None:
                        t1 = turned(*held[1])
                        yield
                    s1 = scores(q, KSW[:, gq * 256:gq * 256 + 256], ca("cau"), gate(1), [got["qc"], got["ksw"]])
                    yield
                    if held is not None:
                        t2 = turned(*held[2])
                        yield
                    s2 = scores(q, KSW[:, 512 + gq * 256:512 + gq * 256 + 256], ca("cau"), gate(2), [got["qc"], got["ksw"]])
                    yield
                    new = ((sc, p), s1, s2)
                elif held is not None:
                    t1, t2 = turned(*held[1]), turned(*held[2])
                if held is not None:
                    gq, o = (h - 1) // 4, (8 + h - 1) * S
                    attend([(t1, lambda k: VSW[:, k * 512 + gq * 128:k * 512 + gq * 128 + 128], 128),
                            (t2, lambda k: VSW[:, k * 512 + 256 + gq * 128:k * 512 + 256 + gq * 128 + 128], 128),
                            (tc, lambda k: VC[0:15, gq * 128:gq * 128 + 128], 15)],
                           AH[:, o:o + S], AL[:, o:o + S], [got["vsw"], got["vc"]])
                    yield
                held = new

        def early():
            yield from compress()
            yield from gmlp()
            yield from dilated()

        got["b1free"] = []
        run(early(), w_in("qc", "ksw", "gates", "vsw"))
        in_done = [(PE.sem, PE.n)]
        got["mix_ab"] = []
        for i in range(4):
            src = (UA if i < 2 else QKB)[:, (i % 2) * 512:(i % 2) * 512 + 512]
            d = slice(512 * i, 512 * i + 512)
            got["mix_ab"].append(split(AH[:, d], AL[:, d], src, got["whole"], in_done))
        dbg("mixh", AH[:, :].bitcast(F32))

        MEM = G[:, 24 * S:24 * S + 4096]
        z_free = now()
        rm = []
        sums = Sums(scr.next(), Ring([scr.next()]))
        for i in range(4):
            d = slice(1024 * i, 1024 * i + 1024)
            l_m = load(f"mem{i}", MEM[:, d], io["mem_t"][:, d], [z_free])
            for kt in (4 * i, 4 * i + 2):
                sums.square(MEM[:, kt * S:kt * S + 512], l_m)
                for k in (kt, kt + 1):
                    d2 = slice(k * S, k * S + S)
                    h = AC(lambda e: e.activation(HH[:, d2], MEM[:, d2], ACT.Copy, scale=par("norm_mem", k)), l_m, z_free)
                    t = DV(lambda e: e.scalar_tensor_tensor(HL[:, d2], MEM[:, d2], par("norm_mem", k), HH[:, d2].bitcast(F32),
                                                            ALU.mult, ALU.subtract), h, l_m, sums.t, z_free)
            rm.append(t)
        R = rstd(sums)
        RCt = rstd_columns(R)
        hM, lM = ap_of(HH), ap_of(HL)

        got["x"] = []

        def add_x(b, bb, t):
            for i in range(2):
                x = X[:, b * 1024 + i * 512:b * 1024 + i * 512 + 512]
                r = DV(lambda e: e.tensor_tensor(x, bb[i].ap[:, :], x, ALU.add), t, got["x"])
                bb[i].free = [r]
            got["x"] = [r]

        def beside_nsa():
            yield from gemm("outa", 0, 4, 2, hA, lA, [got["mix_ab"]] * 2, "T", add_x)
            yield from gemm("xkv", 0, 1, 4, hM, lM, rm, "T", to(XK, "xk"))
            yield from gemm("xkv", 1, 1, 4, hM, lM, rm, "N", to_n(XV, "xv"))

        got["mix"] = []
        run(nsa(), slow(beside_nsa(), 1.2))

        def add_feed(sums, gain, wait_from, fed):
            def evac(b, bb, t):
                for i in range(2):
                    kt = 4 * b + 2 * i
                    x = X[:, kt * S:kt * S + 512]
                    r = DV(lambda e: e.tensor_tensor(x, bb[i].ap[:, :], x, ALU.add), t, got["x"])
                    bb[i].free = [r]
                    if wait_from[0] <= kt < wait_from[1]:
                        fed.append((kt, r))
                    else:
                        fed.append((kt, feed(X, kt, gain, AH, AL, r, wait_from[2])))
                    sums.square(x, r)
            return evac

        def fed_tiles(fed, wait_from, gain):
            free = [(PE.sem, PE.n)]
            out = [[] for _ in range(4)]
            for kt, r in fed:
                if wait_from[0] <= kt < wait_from[1]:
                    r = feed(X, kt, gain, AH, AL, r, free)
                out[kt // 4].append(r)
            return out

        base = now()
        for b_ in bufs:
            b_.free = list(base)
        sums = Sums(bufs[0], Ring(bufs[1:3]))
        fed, held_back = [], (8, 16, base)
        run(gemm("outb", 0, 4, 2, ap_of(AH, 8), ap_of(AL, 8), [got["mix"]] * 2, "T", add_feed(sums, "norm_xattn", held_back, fed)))
        rx = fed_tiles(fed, held_back, "norm_xattn")
        dbg("x1", X[:, :])

        XQ = G[:, 0:1024]
        got["xq"] = []
        run(gemm("xq", 0, 1, 4, hA, lA, rx, "T", to(XQ, "xq")), late_rstd(sums))
        scr, pts = Ring(bufs[0:4]), Ring(bufs[4:7])
        in_done = [(PE.sem, PE.n)]
        got["mix"] = []

        def cross():
            held = None
            for h in range(5):
                new = None
                if h < 4:
                    new = scores(XQ[:, h * 256:h * 256 + 256], XK[:, h * 256:h * 256 + 256], None, None, [got["xq"], got["xk"]])
                    yield
                if held is not None:
                    tr = turned(*held, causal=False)
                    o = (h - 1) * S
                    attend([(tr, lambda k, h=h: XV[:, k * 512 + (h - 1) * 128:k * 512 + h * 128], 128)],
                           AH[:, o:o + S], AL[:, o:o + S], got["xv"])
                    yield
                held = new

        run(cross())
        base = now()
        for b_ in bufs:
            b_.free = list(base)
        sums = Sums(bufs[7], Ring(bufs[1:3]))
        fed, held_back = [], (0, 4, base)
        run(gemm("xo", 0, 4, 1, hA, lA, [got["mix"]], "T", add_feed(sums, "norm_mlp", held_back, fed)))
        rm = fed_tiles(fed, held_back, "norm_mlp")
        dbg("x2", X[:, :])

        tmps = Ring([Place(G[:, E0 + 4096 + 512 * i:E0 + 4608 + 512 * i]) for i in range(3)])
        base = now()
        for s_ in tmps.places:
            s_.free = list(base)
        sums_x2 = sums
        ada_at["acc"] = [Place(G[:, E0:E0 + 2048]), Place(G[:, E0 + 2048:E0 + 4096])]
        for s_ in ada_at["acc"]:
            s_.free = list(base)
        hid_free = [base] * 24
        hid_ready = [None] * 24

        def up(qn, b0, nb):
            def evac(b, bb, t):
                for i in range(2):
                    kt = (16 * qn + 4 * (b0 + b) + 2 * i) % 24
                    tm = tmps.next()
                    r = DV(lambda e: e.scalar_tensor_tensor(pair2(tm.ap), pair2(bb[i].ap[:, :]), 0.0, R2, ALU.max, ALU.mult), t, R, tm.free)
                    bb[i].free = [r]
                    r2 = AC(lambda e, tm=tm: e.activation(tm.ap, tm.ap, ACT.Square), r)
                    d = slice(kt * S, kt * S + 512)
                    z = split(HH[:, d], HL[:, d], tm.ap, r2, hid_free[kt])
                    tm.free = [z]
                    hid_ready[kt] = hid_ready[kt + 1] = z
            yield from gemm("up", 4 * qn + b0, nb, 4, hA, lA, rm, "T", evac)

        def ring24(t, qn):
            return lambda kt: t[:, ((16 * qn + kt) % 24) * S:((16 * qn + kt) % 24 + 1) * S]

        def down(qn):
            ready = [[hid_ready[(16 * qn + 4 * c + k) % 24] for k in range(4)] for c in range(4)]
            yield from gemm("down", 4 * qn, 4, 4, ring24(HH, qn), ring24(HL, qn), ready, "T", add_x)
            for k in range(16):
                hid_free[(16 * qn + k) % 24] = [(PE.sem, PE.n)]

        def mlp():
            yield from up(0, 0, 4)
            for qn in range(3):
                yield from up(qn + 1, 0, 2)
                yield from down(qn)
                yield from up(qn + 1, 2, 2)

        run(mlp(), ada_steps((0, 1, 4), 2.4), late_rstd(sums_x2))
        state["rs"] = [(DV.sem, DV.n)]
        one = []
        for a in (16, 64, 96 + 16):
            one.append(DV(lambda e: e.tensor_scalar(MODT[:, a:a + 16], MODT[:, a:a + 16], 1.0, None, ALU.add), got["mod"]))

        base = now()
        l_cg = load("cg", G[:, E0:E0 + NCG], io["c_gla"], [base])
        CTX = G[:, E0 + 5632:E0 + 9728]
        l_ctx = load("ctx", CTX, io["ctx_t"], [base])
        bufs = [Place(G[:, E0 + 2048 + 512 * i:E0 + 2560 + 512 * i]) for i in range(4)]
        for b_ in bufs:
            b_.free = list(base)

        def cg(name):
            a, b = CG[name]
            return G[:, E0 + a:E0 + b]

        def modulate(src, sh, sc, tms, ready, free, out):
            for kt in range(0, 16, 2):
                tm = tms.next()
                for k in range(2):
                    t = DV(lambda e: e.tensor_scalar(tm.ap[:, k * 256:k * 256 + 256], src[:, (kt + k) * S:(kt + k + 1) * S],
                                                     sc(kt + k), sh(kt + k), ALU.mult, ALU.add),
                           ready[kt // 2], one, tm.free)
                d = slice(kt * S, kt * S + 512)
                t2 = split(AH[:, d], AL[:, d], tm.ap, t, free)
                tm.free = [t2]
                out[kt // 4].append(t2)
                yield

        sums = Sums(bufs[0], Ring([bufs[1]]))
        squares = sums

        def squared(b, r):
            for i in range(2):
                kt = 4 * b + 2 * i
                squares.square(X[:, kt * S:kt * S + 512], r)

        def last_down():
            ready = [[hid_ready[(48 + 4 * c + k) % 24] for k in range(4)] for c in range(4)]

            def evac(b, bb, t):
                add_x(b, bb, t)
                squared(b, got["x"])
            yield from gemm("down", 12, 4, 4, ring24(HH, 3), ring24(HL, 3), ready, "T", evac)

        rc = [[] for _ in range(4)]
        run(last_down(), modulate(CTX, lambda kt: cmod(0, kt), lambda kt: cmod(1, kt), Ring(bufs[2:4]), [l_ctx] * 8,
                                  [base], rc))
        dbg("x3", X[:, :])
        dbg("mod", MODT[:, :])

        R = rstd(sums)
        x_ready = []
        for kt in range(16):
            t = DV(lambda e: e.scalar_tensor_tensor(X[:, kt * S:kt * S + S], X[:, kt * S:kt * S + S], par("final_norm", kt),
                                                    RS[:, 0:256], ALU.mult, ALU.mult), R)
            if kt % 2:
                x_ready.append(t)
        state["rs"] = [t]
        got["x"] = [t]
        dbg("x4", X[:, :])

        base = now()
        K, Q = G[:, 0:2048], G[:, 2048:4096]
        Vr = Ring([Place(G[:, 4096:5120]), Place(G[:, 5120:6144])])
        SS = Place(G[:, 6144:8192])
        Zr = Ring([Place(G[:, 8192:8704]), Place(G[:, E0 + 9472:E0 + 9984])])
        TM = [Place(G[:, 8704:9216]), Place(G[:, 9216:9728])]
        QN, KN, QA, KB, Q4 = (Place(G[:, 9728 + 512 * i:10240 + 512 * i]) for i in range(5))
        T0 = E0 + NCG
        K3, Q3 = Place(G[:, T0:T0 + 256]), Place(G[:, T0 + 256:T0 + 512])
        ATD = [Place(G[:, T0 + 512 + 128 * i:T0 + 640 + 128 * i]) for i in range(2)]
        AT = Place(G[:, T0 + 768:T0 + 1024])
        AT3 = [Place(G[:, T0 + 1024 + 128 * i:T0 + 1152 + 128 * i]) for i in range(2)]
        ON = [Place(G[:, T0 + 1280 + 512 * i:T0 + 1792 + 512 * i]) for i in range(2)]
        OT = G[:, T0 + 2304:T0 + 6400]
        modt = [Place(G[:, T0 + 6400 + 512 * i:T0 + 6912 + 512 * i]) for i in range(2)]
        assert T0 + 7424 <= E0 + 9472
        TD, GB = modt
        ALR = [sb("ALR", 256), None]
        ET = [Place(SM[:, 8 * i:8 * i + 8]) for i in range(2)]
        PX = Place(SM[:, 16:24])
        places = Vr.places + [SS] + Zr.places + TM + [QN, KN, QA, KB, Q4, K3, Q3, AT, PX] + ATD + AT3 + ON + modt + ET
        for pl in places:
            pl.free = list(base)
        kq = {"k": base, "q": base}
        spill = Load(sem("s_spill"))
        v8 = lambda ap: ap.rearrange("p (c t) -> p c t", c=8)
        k4 = lambda ap: ap.rearrange("p (k c t) -> p k c t", k=2, c=4)

        def bcast(small, n=8):
            return small.unsqueeze(2).to_broadcast([P, n, 64])

        def decay(d, h, alr_t):
            bk, z = misc.next(), Zr.next()
            for k in range(2):
                f = (2 * h + k) * 128
                t = PE(lambda e: e.matmul(bk.ap[:, k * 256:k * 256 + 256], cg("decay")[32 * d:32 * d + 32, f:f + 128],
                                          ALR[0][32 * d:32 * d + 32, :], start=True, stop=True, tile_position=(32 * d, 0)),
                       alr_t, bk.free, l_cg)
            for k in range(2):
                a = AC(lambda e: e.activation(z.ap[:, k * 256:k * 256 + 256], bk.ap[:, k * 256:k * 256 + 256], ACT.Identity,
                                              bias=par("b_decay", 8 * d + 2 * h + k)), t, z.free)
            bk.free = [a]
            b = DV(lambda e: e.scalar_tensor_tensor(TD.ap, z.ap, -1.0, z.ap, ALU.mult, ALU.min), a, TD.free)
            c = AC(lambda e: e.activation(TD.ap, TD.ap, ACT.Exp), b)
            c = AC(lambda e: e.activation(TD.ap, TD.ap, ACT.Ln, bias=1.0), c)
            a = DV(lambda e: e.scalar_tensor_tensor(z.ap, z.ap, 0.0, TD.ap, ALU.min, ALU.subtract), c)
            TD.free = [a]
            rev = (lambda ap: ap) if d == 0 else (lambda ap: ap[:, ::-1])
            t = DV(lambda e: e.tensor_tensor_scan(rev(z.ap), cg("scan"), rev(z.ap), 0.0, ALU.mult, ALU.add), a)
            return z, t

        def totals(d, z):
            zc = v8(z.ap)
            return zc[:, :, 63:64] if d == 0 else zc[:, :, 0:1]

        def chunk_factors(d, z, zt):
            et = ET[d]
            t = AC(lambda e: e.activation(et.ap, totals(d, z).rearrange("p c t -> p (c t)"), ACT.Exp, scale=1 / 16.0), zt, et.free)
            return et, t

        def products(et, et_t, towards_end):
            e4, p4 = (ap.rearrange("p (k c) -> p k c", k=2) for ap in (et.ap, PX.ap))
            order_ = (3, 2, 1, 0) if towards_end else (0, 1, 2, 3)
            a = DV(lambda e: e.memset(p4[:, :, order_[0]:order_[0] + 1], 1.0), PX.free)
            for was, c in zip(order_, order_[1:]):
                a = DV(lambda e: e.tensor_tensor(p4[:, :, c:c + 1], p4[:, :, was:was + 1], e4[:, :, was:was + 1], ALU.mult), a, et_t)
            return a

        def towards(d, z, zt, src, src_t, out):
            tm = TM[1]
            a = DV(lambda e: e.tensor_tensor(v8(tm.ap), totals(d, z).to_broadcast([P, 8, 64]), v8(z.ap), ALU.subtract), zt, tm.free)
            b = AC(lambda e: e.activation(tm.ap, tm.ap, ACT.Exp, scale=1 / 16.0), a)
            c = DV(lambda e: e.tensor_tensor(out.ap, src, tm.ap, ALU.mult), b, src_t, out.free)
            tm.free = [c]
            return c

        def low_rank(ready, waits):
            bk = misc.next()
            t = small("alr", hA, lA, ready, bk)
            r = DV(lambda e: e.tensor_copy(ALR[0][:, :], bk.ap[:, 0:256]), t, waits)
            bk.free = [r]
            return r

        def to_k(dst, key, scale=1.0):
            def evac(b, bb, t):
                for i in range(2):
                    o = dst[:, b * 1024 + i * 512:b * 1024 + i * 512 + 512]
                    r = AC(lambda e: e.activation(o, bb[i].ap[:, :], ACT.Copy, scale=scale), t, kq[key])
                    bb[i].free = [r]
                    got.setdefault(key, []).append(r)
            return evac

        def v_block(h):
            v = Vr.next()
            v.ready = []

            def evac(b, bb, t):
                for i in range(2):
                    o = v.ap[:, i * 512:i * 512 + 512]
                    v.ready.append(AC(lambda e: e.activation(o, bb[i].ap[:, :], ACT.Copy), t, v.free))
                    bb[i].free = [v.ready[-1]]
            return v, gemm("v2", h, 1, 4, hA, lA, rc, "N", evac)

        def ctx_head(h, v, alr_t):
            zs = decay(0, h, alr_t)
            yield
            for d in range(2):
                z, zt = zs
                if d == 0:
                    zs = decay(1, h, alr_t)
                    yield
                et, et_t = chunk_factors(d, z, zt)
                p_t = products(et, et_t, d == 0)
                et.free = [p_t]
                ks = towards(d, z, zt, K[:, h * 512:h * 512 + 512], got["k"], KB)
                z.free = [ks, et_t]
                ks = DV(lambda e: e.tensor_tensor(v8(KN.ap), v8(KB.ap), bcast(PX.ap), ALU.mult), ks, p_t, KN.free)
                PX.free = KB.free = [ks]
                kq["used"] = [ks]
                yield
                bk = misc.next()
                for i in range(2):
                    for k in range(2):
                        t = PE(lambda e: e.transpose(bk.ap[:, i * 256 + k * 128:i * 256 + k * 128 + 128],
                                                     KN.ap[:, k * 256 + i * 128:k * 256 + i * 128 + 128], ident), ks, bk.free)
                KN.free = [t]
                kn = DV(lambda e: e.tensor_copy(QA.ap, bk.ap[:, :]), t, QA.free)
                bk.free = [kn]
                yield
                for k in range(2):
                    bk = misc.next()
                    for i in range(2):
                        t = PE(lambda e: e.matmul(bk.ap[:, :], QA.ap[:, i * 256 + k * 128:i * 256 + k * 128 + 128],
                                                  v.ap[:, i * 512:i * 512 + 512], start=i == 0, stop=i == 1), kn, v.ready, bk.free)
                    c = AC(lambda e: e.activation(SS.ap[:, d * 1024 + k * 512:d * 1024 + k * 512 + 512], bk.ap[:, :], ACT.Copy), t, SS.free)
                    bk.free = [c]
                QA.free = [t]
                yield
            z = AC.dma(io["state"][h], SS.ap, spill, c)
            SS.free = [z]
            v.free = [t]

        got["k"], got["q"] = [], []
        alr_t = low_rank(rc, None)
        run(gemm("k2", 0, 2, 4, hA, lA, rc, "T", to_k(K, "k")))
        v, gen = v_block(0)
        run(gen)
        for h in range(4):
            if h == 3:
                nxt, gen = None, gemm("q2", 0, 2, 4, hA, lA, rl, "T", to_k(Q, "q", 1.0 / 16.0))
            else:
                nxt, gen = v_block(h + 1)
            run(ctx_head(h, v, alr_t), gen)
            v = nxt
            if h == 2:
                free, rl = [(PE.sem, PE.n)], [[] for _ in range(4)]
                GB.free = TD.free = list(flat([GB.free, TD.free]))
                for _ in modulate(X, lambda kt: mod(0, kt), lambda kt: mod(1, kt), Ring([ON[0], ON[1]]), x_ready, free, rl):
                    pass

        rc = rl
        alr_t = low_rank(rc, [(PE.sem, PE.n)])
        base = [(PE.sem, PE.n)]
        zs0 = decay(0, 0, alr_t)
        got["k"] = []
        kq["k"] = [kq["used"]]
        run(gemm("k2", 0, 2, 4, hA, lA, rc, "T", to_k(K, "k")))
        zero = [PO(lambda e: e.memset(pl.ap, 0.0), pl.free) for pl in ATD]
        for pl in ATD:
            pl.free = list(zero)
        MK = [sb(f"MK{d}", 64, U32) for d in range(2)]
        l_mk = [load(f"mk{d}", MK[d][:, :], io["masks"][d]) for d in range(2)]
        back = Load(sem("s_back"))
        ob = [banks[4], banks[5]]
        misc = Ring([banks[6], banks[7]])
        got["ot"] = [base]
        ot_free = now()

        def lat_head(h, v, zs):
            AC.wait([spill.all(), SS.free])
            lt = AC.dma(SS.ap, io["state"][h], back)
            PE.wait([ob[0].free, ob[1].free])
            first = [True, True]
            for d in range(2):
                z, zt = zs
                if d == 0:
                    zs = decay(1, h, alr_t)
                elif h < 3:
                    zs = decay(0, h + 1, alr_t)
                yield
                q, kk = Q[:, h * 512:h * 512 + 512], K[:, h * 512:h * 512 + 512]
                ref = v8(z.ap)[:, :, 31:32] if d == 0 else v8(z.ap)[:, :, 32:33]
                t0, t1 = TM
                a = DV(lambda e: e.tensor_tensor(v8(t0.ap), v8(z.ap), ref.to_broadcast([P, 8, 64]), ALU.subtract), zt, t0.free)
                b = AC(lambda e: e.activation(t1.ap, t0.ap, ACT.Exp, scale=1 / 16.0), a, t1.free)
                b2 = AC(lambda e: e.activation(t0.ap, t0.ap, ACT.Exp, scale=-1 / 16.0), a)
                qn = DV(lambda e: e.tensor_tensor(QN.ap, q, t1.ap, ALU.mult), b, got["q"], QN.free)
                t1.free = [qn]
                kn = DV(lambda e: e.tensor_tensor(KN.ap, kk, t0.ap, ALU.mult), b2, got["k"], KN.free)
                t0.free = [kn]
                et, et_t = chunk_factors(d, z, zt)
                yield
                a = AC(lambda e: e.activation(t0.ap, z.ap, ACT.Exp, scale=1 / 16.0), zt, t0.free)
                qa = DV(lambda e: e.tensor_tensor(QA.ap, q, t0.ap, ALU.mult), a, got["q"], QA.free)
                t0.free = [qa]
                kb = towards(d, z, zt, kk, got["k"], KB)
                z.free = [kb, et_t, qa]
                yield
                e4 = et.ap.rearrange("p (k c) -> p k c", k=2)
                tk, tq = (0, 1) if d == 0 else (1, 0)
                far = []
                for out, src, tile, src_t in ((K3, KB, tk, kb), (Q3, QA, tq, qa)):
                    o4 = out.ap.rearrange("p (k c t) -> p k c t", k=2, c=2)
                    near_c, far_c, f = (1, 0, 1) if tile == 0 else (2, 3, 2)
                    far.append(DV(lambda e: e.tensor_copy(o4[:, :, near_c % 2, :], k4(src.ap)[:, :, near_c, :]), src_t, out.free))
                    far.append(DV(lambda e: e.tensor_tensor(o4[:, :, far_c % 2, :], k4(src.ap)[:, :, far_c, :],
                                                            e4[:, :, f:f + 1].to_broadcast([P, 2, 64]), ALU.mult), src_t, et_t, out.free))
                p_t = products(et, et_t, d == 1)
                q4 = DV(lambda e: e.tensor_tensor(v8(Q4.ap), v8(QA.ap), bcast(PX.ap), ALU.mult), p_t, qa, Q4.free)
                PX.free = [q4]
                et.free = [q4]
                yield
                bk = misc.next()
                parts = ((0, 0, 64), (32, 32, 32)) if d == 0 else ((32, 0, 64), (0, 0, 32))
                for c in range(4):
                    half = 64 * (c % 2)
                    for j0, i0, ni in parts:
                        for k in range(2):
                            o = k * 256 + c * 64
                            t = PE(lambda e: e.matmul(
                                bk.ap[half + j0:half + j0 + 32, (c // 2) * 64 + i0:(c // 2) * 64 + i0 + ni],
                                KN.ap[:, o + j0:o + j0 + 32], QN.ap[:, o + i0:o + i0 + ni],
                                start=k == 0, stop=k == 1, tile_position=(0, half + j0)), qn, kn, bk.free)
                QN.free = KN.free = [t]
                rk, rq = (0, 64) if d == 0 else (64, 0)
                for tile in range(2):
                    for k in range(2):
                        o = k * 256 + tile * 128
                        t = PE(lambda e: e.matmul(
                            bk.ap[rk:rk + 64, 128 + tile * 64:192 + tile * 64], KB.ap[:, o + rk:o + rk + 64],
                            QA.ap[:, o + rq:o + rq + 64], start=k == 0, stop=k == 1, tile_position=(0, rk)), kb, qa)
                KB.free = QA.free = [t]
                KB.free, QA.free = [t, far], [t, far, q4]
                for k in range(2):
                    t = PE(lambda e: e.matmul(bk.ap[:, 256:384], K3.ap[:, k * 128:k * 128 + 128], Q3.ap[:, k * 128:k * 128 + 128],
                                              start=k == 0, stop=k == 1), far)
                K3.free = Q3.free = [t]
                dd = ATD[d]
                ad = dd.ap.rearrange("p (i t) -> p i t", i=2)
                pd = bk.ap[:, 0:128].rearrange("p (i t) -> p i t", i=2)
                for half in (0, 64):
                    for j0, i0, ni in parts:
                        r, q_ = slice(half + j0, half + j0 + 32), slice(i0, i0 + ni)
                        c = DV(lambda e: e.copy_predicated(ad[r, :, q_], MK[d][r, q_].unsqueeze(1).to_broadcast([32, 2, ni]),
                                                           pd[r, :, q_]), t, l_mk, dd.free)
                at = AT.ap.rearrange("p (i t) -> p i t", i=2)
                c2 = DV(lambda e: e.tensor_copy(at[rk:rk + 64, :, rq:rq + 64],
                                                bk.ap[rk:rk + 64, 128:256].rearrange("p (i t) -> p i t", i=2)), t, AT.free)
                c3 = DV(lambda e: e.tensor_copy(AT3[d].ap, bk.ap[:, 256:384]), t, AT3[d].free)
                bk.free = [c3]
                yield
                for i in range(2):
                    for k in range(2):
                        s_ap = SS.ap[:, d * 1024 + k * 512:d * 1024 + k * 512 + 512]
                        t = PE(lambda e: e.matmul(ob[i].ap[:, :], Q4.ap[:, k * 256 + i * 128:k * 256 + i * 128 + 128], s_ap,
                                                  start=first[i], stop=False, skip_group_check=True), q4, lt)
                        first[i] = False
                Q4.free = [t]
                yield
            SS.free = [t]
            kq["used"] = [kn, kb]
            ds = []
            for r in (slice(0, 64), slice(64, 128)):
                ds.append(DV(lambda e: e.tensor_tensor(at[r, :, r], ATD[0].ap.rearrange("p (i t) -> p i t", i=2)[r, :, :],
                                                       ATD[1].ap.rearrange("p (i t) -> p i t", i=2)[r, :, :], ALU.add), c, AT.free))
            ATD[0].free = ATD[1].free = [ds[-1]]
            for i in range(2):
                t = PE(lambda e: e.matmul(ob[i].ap[:, :], AT.ap[:, i * 128:i * 128 + 128], v.ap[:, i * 512:i * 512 + 512],
                                          start=False, stop=False, skip_group_check=True), ds, c2, c3, v.ready)
                t = PE(lambda e: e.matmul(ob[i].ap[:, :], AT3[1 - i].ap, v.ap[:, (1 - i) * 512:(1 - i) * 512 + 512],
                                          start=False, stop=True, skip_group_check=True), c3)
            AT.free = AT3[0].free = AT3[1].free = [t]
            v.free = [t]
            yield
            ready = []
            for i in range(2):
                o = 24 + 4 * i
                a = AC(lambda e: e.activation(ON[i].ap, ob[i].ap[:, :], ACT.Square, accum_out=SM[:, o:o + 1]), t, ON[i].free)
                b = DV(lambda e: e.tensor_scalar(SM[:, o + 1:o + 2], SM[:, o:o + 1], 1.0 / 512, 1e-6, ALU.mult, ALU.add), a)
                b = AC(lambda e: e.activation(SM[:, o + 2:o + 3], SM[:, o + 1:o + 2], ACT.Sqrt), b)
                b = DV(lambda e: e.reciprocal(SM[:, o + 3:o + 4], SM[:, o + 2:o + 3]), b)
                c = DV(lambda e: e.tensor_scalar(ON[i].ap, ob[i].ap[:, :], SM[:, o + 3:o + 4], None, ALU.mult), b)
                ob[i].free = [c]
                ready.append(c)
            yield
            for j in range(2):
                bk = misc.next()
                for k in range(2):
                    for i in range(2):
                        f = (2 * j + k) * 128
                        t = PE(lambda e: e.transpose(bk.ap[:, k * 256 + i * 128:k * 256 + i * 128 + 128],
                                                     ON[i].ap[:, f:f + 128], ident), ready[i], bk.free)
                for k in range(2):
                    ft = 4 * h + 2 * j + k
                    c = DV(lambda e: e.tensor_scalar(OT[:, ft * 256:ft * 256 + 256], bk.ap[:, k * 256:k * 256 + 256],
                                                     par("gla_gain", ft), None, ALU.mult), t, ot_free)
                bk.free = [c]
                yield
            ON[0].free = ON[1].free = [t]
            got["ot"] = [c]
            got["next"] = zs

        kept = Load(sem("s_kept"))

        def gates_kept(b0, nb):
            def evac(b, bb, t):
                for i in range(2):
                    a = AC(lambda e: e.activation(GB.ap, bb[i].ap[:, :], ACT.Sigmoid), t, GB.free)
                    bb[i].free = [a]
                    GB.free = [AC.dma(io["gate"][b0 + b][:, i * 512:i * 512 + 512], GB.ap, kept, a)]
            yield from gemm("bg2", b0, nb, 4, hA, lA, rc, "T", evac)

        v, gen = v_block(0)
        run(gen)
        zs = zs0
        for h in range(4):
            nxt, gen = (None, iter(())) if h == 3 else v_block(h + 1)

            def beside(gen=gen, h=h):
                yield from gen
                yield from gates_kept(h, 1)
            run(lat_head(h, v, zs), beside())
            zs, v = got["next"], nxt
        dbg("ot", OT)
        misc = Ring(banks[4:8])

        base = now()

        def half_tiles(lo_base, hi_base):
            def at(i, n):
                b = (lo_base if i < 8 else hi_base) + (i % 8) * S
                return G[:, b:b + n * S]
            return at

        BG = half_tiles(16 * S, (24 + 16) * S)
        tm2 = Ring([Place(G[:, E0 + 512 * i:E0 + 512 + 512 * i]) for i in range(3)])
        for s in tm2.places:
            s.free = list(base)

        def gate_evac(dst, key):
            def evac(b, bb, t):
                for i in range(2):
                    o = dst(4 * b + 2 * i, 2)
                    r = AC(lambda e, o=o, s=bb[i]: e.activation(o, s.ap[:, :], ACT.Sigmoid), t, got["y_done"])
                    bb[i].free = [r]
                    got.setdefault(key, []).append(r)
            return evac

        got["y"] = []

        def g_evac(b, bb, t):
            for i in range(2):
                tm = tm2.next()
                a = AC(lambda e, tm=tm, s=bb[i]: e.activation(tm.ap, s.ap[:, :], ACT.Silu), t, tm.free)
                bb[i].free = [a]
                d = slice(b * 1024 + i * 512, b * 1024 + i * 512 + 512)
                m = DV(lambda e, tm=tm, d=d: e.tensor_tensor(tm.ap, tm.ap, OT[:, d], ALU.mult), a, got["ot"])
                z = split(HH[:, d], HL[:, d], tm.ap, m, base)
                tm.free = [z]
                got["y"].append(z)

        l_bg = Load(sem("s_l_bg"))
        AC.wait([kept.all(), base])
        for b in range(4):
            AC.dma(BG(4 * b, 4), io["gate"][b], l_bg)
        got["bg"] = [l_bg.all()]
        run(gemm("g2", 0, 4, 4, hA, lA, rc, "T", g_evac))
        PN = G[:, E0 + 1536:E0 + 1536 + 2048]
        PM = G[:, E0 + 3584:E0 + 5632].rearrange("p (w i t) -> p w i t", w=4, i=2)
        PG = G[:, E0 + 5632:E0 + 7680].rearrange("p (k w n) -> p k w n", k=2, w=4)
        l_cp = load("cp", G[:, E0 + 3584:E0 + 7680], io["c_pool"], [got["y"]])
        ada_at["acc"] = [Place(G[:, E0 + 7680:E0 + 9728])]
        ada_at["acc"][0].free = now()

        def y_evac(b, bb, t):
            for i in range(2):
                o = BG(4 * b + 2 * i, 2)
                r = DV(lambda e, o=o, s=bb[i]: e.tensor_tensor(o, s.ap[:, :], o, ALU.mult), t, got["bg"])
                bb[i].free = [r]
            got["yg"] = [r]

        got["pn"] = []

        def pn_evac(b, bb, t):
            for i in range(2):
                o = PN[:, i * 1024 + b * 512:i * 1024 + b * 512 + 512]
                r = DV(lambda e, o=o, s=bb[i]: e.tensor_copy(o, s.ap[:, :]), t)
                bb[i].free = [r]
                got["pn"].append(r)

        BP = half_tiles(8 * S, (24 + 8) * S)
        got["pp"] = []

        def pool():
            for w in range(4):
                bk = misc.next()
                for k in range(2):
                    for i in range(2):
                        t = PE(lambda e, w=w, k=k, i=i, bk=bk: e.matmul(
                            bk.ap[:, k * 256:k * 256 + 256], PN[:, i * 1024 + (2 * w + k) * 128:i * 1024 + (2 * w + k) * 128 + 128],
                            PM[:, w, i, :], start=i == 0, stop=i == 1), got["pn"], l_cp, bk.free)
                tm = tm2.next()
                a = AC(lambda e, tm=tm, bk=bk: e.activation(tm.ap, bk.ap[:, :], ACT.Copy), t, tm.free)
                bk.free = [a]
                yield
                bk = misc.next()
                for m in range(2):
                    for k in range(2):
                        t = PE(lambda e, w=w, k=k, m=m, bk=bk, tm=tm: e.matmul(
                            bk.ap[:, m * 256:m * 256 + 256], PG[:, k, w, m * 128:m * 128 + 128], tm.ap[:, k * 256:k * 256 + 256],
                            start=k == 0, stop=k == 1), a, bk.free)
                tm.free = [t]
                tm = tm2.next()
                for m in range(2):
                    b = DV(lambda e, m=m, w=w, tm=tm, bk=bk: e.tensor_scalar(tm.ap[:, m * 256:m * 256 + 256], bk.ap[:, m * 256:m * 256 + 256],
                                                                            par("pool_scale", 2 * w + m), None, ALU.mult), t, tm.free)
                bk.free = [b]
                d = slice(w * 512, w * 512 + 512)
                z = split(HH[:, d], HL[:, d], tm.ap, b, got["y_done"])
                tm.free = [z]
                got["pp"].append(z)
                yield

        got["m"] = []

        def merge_evac(b, bb, t):
            for i in range(2):
                tm = tm2.next()
                r = DV(lambda e, tm=tm, s=bb[i], o=BP(4 * b + 2 * i, 2): e.tensor_tensor(tm.ap, s.ap[:, :], o, ALU.mult), t, got["bp"], tm.free)
                bb[i].free = [r]
                r = DV(lambda e, tm=tm, o=BG(4 * b + 2 * i, 2): e.tensor_tensor(tm.ap, tm.ap, o, ALU.add), r, got["yg"])
                d = slice(b * 1024 + i * 512, b * 1024 + i * 512 + 512)
                z = split(AH[:, d], AL[:, d], tm.ap, r, got["a_done"])
                tm.free = [z]
                got["m"].append(z)

        def merge():
            yield from gemm("p2", 0, 2, 4, hA, lA, rc, "N", pn_evac)
            yield from gemm("gout", 0, 4, 4, ap_of(HH), ap_of(HL), [got["y"]] * 4, "T", y_evac)
            got["y_done"] = [(PE.sem, PE.n), got["yg"]]
            yield from both(pool(), gemm("bg2", 4, 4, 4, hA, lA, rc, "T", gate_evac(BP, "bp")))
            got["a_done"] = [(PE.sem, PE.n)]
            yield from gemm("pout", 0, 4, 2, ap_of(HH), ap_of(HL), [got["pp"]] * 2, "T", merge_evac)

        run(merge(), ada_steps((2, 3), 1.25))

        def gated_x(which):
            def evac(b, bb, t):
                for i in range(2):
                    for m in range(2):
                        kt = 4 * b + 2 * i + m
                        x = X[:, kt * S:kt * S + S]
                        a = DV(lambda e, x=x: e.tensor_scalar(x, x, ALPHA, None, ALU.mult), got["x"])
                        r = DV(lambda e, x=x, kt=kt, m=m, s=bb[i]: e.scalar_tensor_tensor(
                            x, s.ap[:, m * 256:m * 256 + 256], mod(which, kt), x, ALU.mult, ALU.add), t, a, got["mod"])
                    bb[i].free = [r]
                    sums.plain(X[:, (kt - 1) * S:(kt + 1) * S], r)
                got["xn"] = [r]
            return evac

        bufs = [Place(G[:, E0 + 4608 + 512 * i:E0 + 5120 + 512 * i]) for i in range(6)]
        base = now()
        for b_ in bufs:
            b_.free = list(base)
        sums = Sums(bufs[0], None)
        run(gemm("out2", 0, 4, 4, hA, lA, [got["m"]] * 4, "T", gated_x(2)))
        got["x"] = got["xn"]
        dbg("x5", X[:, :])

        def layer_norm(sums, gain, bias):
            bk, t = sums.over_partitions()
            a = AC(lambda e: e.activation(RS[:, 0:256], bk.ap[:, 0:256], ACT.Copy, scale=1.0 / D), t, state["rs"])
            bk.free = [a]
            sq = Sums(bufs[3], Ring(bufs[1:3]))
            for kt in range(0, 16, 2):
                x = X[:, kt * S:kt * S + 512]
                c = DV(lambda e: e.tensor_tensor(pair2(x), pair2(x), R2, ALU.subtract), a, got["x"])
                sq.square(x, c)
            state["rs"] = [c]
            r = rstd(sq, eps=1e-5)
            for kt in range(0, 16, 2):
                x = X[:, kt * S:kt * S + 512]
                t = DV(lambda e: e.tensor_tensor(pair2(x), pair2(x), R2, ALU.mult), r)
                for k in (kt, kt + 1):
                    x1 = X[:, k * S:k * S + S]
                    t2 = AC(lambda e: e.activation(x1, x1, ACT.Identity, scale=par(gain, k), bias=par(bias, k)), t)
                state["rs"] = [t]
                yield t2

        x_ready, rf, tms = [], [[] for _ in range(4)], Ring(bufs[4:6])
        ln = layer_norm(sums, "lnm_g", "lnm_b")
        md = modulate(X, lambda kt: mod(3, kt), lambda kt: mod(4, kt), tms, x_ready, [(PE.sem, PE.n)], rf)
        for t in ln:
            x_ready.append(t)
            next(md)
        got["x"] = list(x_ready)
        dbg("x6", X[:, :])

        hid_free = [now()] * 24
        silu_tm = Ring([Place(G[:, E0 + 512 * i:E0 + 512 + 512 * i]) for i in range(3)])
        for s_ in silu_tm.places:
            s_.free = now()

        def ffn_up(b0, nb):
            def evac(b, bb, t):
                kt = (2 * (b0 + b)) % 24
                tm = silu_tm.next()
                a = AC(lambda e, tm=tm: e.activation(tm.ap, bb[0].ap[:, :], ACT.Silu), t, tm.free)
                bb[0].free = [a]
                m = DV(lambda e, tm=tm: e.tensor_tensor(tm.ap, bb[1].ap[:, :], tm.ap, ALU.mult), a, t)
                bb[1].free = [m]
                d = slice(kt * S, kt * S + 512)
                z = split(HH[:, d], HL[:, d], tm.ap, m, hid_free[kt])
                tm.free = [z]
                hid_ready[kt] = hid_ready[kt + 1] = z
            yield from gemm("fin", b0, nb, 4, hA, lA, rf, "T", evac)

        PARTS = [(0, 16), (16, 16), (32, 12)]
        first_part = [True]

        def ffn_down(part):
            a, n = PARTS[part]

            def evac(b, bb, t):
                for i in range(2):
                    for m in range(2):
                        kt = 4 * b + 2 * i + m
                        x = X[:, kt * S:kt * S + S]
                        w = got["x"]
                        if part == 0:
                            w = DV(lambda e, x=x: e.tensor_scalar(x, x, ALPHA, None, ALU.mult), got["x"], rf)
                        r = DV(lambda e, x=x, kt=kt, m=m, s=bb[i]: e.scalar_tensor_tensor(
                            x, s.ap[:, m * 256:m * 256 + 256], mod(5, kt), x, ALU.mult, ALU.add), t, w, got["mod"])
                    bb[i].free = [r]
                    if part == 2:
                        sums.plain(X[:, (kt - 1) * S:(kt + 1) * S], r)
                got["xn"] = [r]
            ready = [[hid_ready[(a + 4 * c + k) % 24] for k in range(4)] for c in range(n // 4)]
            yield from gemm(f"fout{part}", 0, 4, n // 4, lambda kt: HH[:, ((a + kt) % 24) * S:((a + kt) % 24 + 1) * S],
                            lambda kt: HL[:, ((a + kt) % 24) * S:((a + kt) % 24 + 1) * S], ready, "T", evac)
            got["x"] = got["xn"]
            for k in range(n):
                hid_free[(a + k) % 24] = [(PE.sem, PE.n)]

        def ffn():
            yield from ffn_up(0, 8)
            yield from ffn_up(8, 4)
            yield from ffn_down(0)
            yield from ffn_up(12, 4)
            yield from ffn_up(16, 4)
            yield from ffn_down(1)
            yield from ffn_up(20, 2)
            yield from ffn_down(2)

        sums = Sums(bufs[0], None)
        ada_at["acc"] = [Place(G[:, E0 + 7680:E0 + 9728])]
        ada_at["acc"][0].free = now()
        run(ffn(), ada_steps((5,), 2.2))
        dbg("x7", X[:, :])
        o = Load(sem("s_out"))
        for i, t in enumerate(layer_norm(sums, "lnf_g", "lnf_b")):
            if i % 2:
                d = slice(1024 * (i // 2), 1024 * (i // 2) + 1024)
                SP.dma(io["out"][:, d], X[:, d], o, t)
        SP.wait([o.all(), spill.all(), kept.all()])
        if debug:
            PO.wait([dbg_load.all()])

        if order is None:
            return found
        assert found == order
    return found


def blocks(w, kt=4, width=512):
    k, n = w.shape
    v = w.reshape(k // (P * kt), kt, P, n // width, width)
    return np.ascontiguousarray(v.transpose(3, 0, 2, 1, 4)).reshape(-1, P, kt * width)


def padded(w, width):
    out = np.zeros((w.shape[0], width), w.dtype)
    return out, w


def columns(v):
    return v.reshape(-1, P).T


def tokens(x):
    return np.ascontiguousarray(x.reshape(S, -1, P).transpose(2, 1, 0)).reshape(P, -1)


def constants():
    t = np.arange(S)
    dist = t[:, None] - t[None, :]
    count = (((dist >= 0) & (dist <= 128)).astype(np.float64) + ((dist >= 0) & (dist % 4 == 0) & (dist // 4 <= 128))
             + ((dist >= 0) & (dist % 16 == 0) & (dist // 16 <= 128)))
    dil = np.where(count > 0, np.log(np.maximum(count, 1)), NEG).astype(np.float32)
    cau = np.where(dist >= 0, 0.0, NEG).astype(np.float32)
    end = np.arange(15) * 16 + 31
    valid = end[None, :] <= t[:, None]
    bcmp = np.where(valid, 0.0, NEG).astype(np.float32)
    rows = lambda a: a.reshape(2, P, -1).transpose(1, 0, 2).reshape(P, -1)
    pad = lambda a: np.pad(a, ((0, 0), (0, 32 - a.shape[1])))
    tri = (np.arange(P)[:, None] <= np.arange(P)[None, :]).astype(np.float32)
    mean = np.zeros((4, S, S))
    for i, w in enumerate((2, 4, 8, 16)):
        def axis(n):
            m = np.zeros((n, n))
            for a in range(n):
                lo, hi = max(a - w // 2, 0), min(a + w - w // 2, n)
                m[a, lo:hi] = 1.0 / (hi - lo)
            return m
        mean[i] = np.kron(axis(4), axis(64)) - np.eye(S)
    pm = mean.transpose(2, 0, 1).reshape(2, P, 4, S).transpose(1, 2, 0, 3).reshape(P, -1).astype(np.float32)
    scan = np.ones(512, np.float32)
    scan[::64] = 0
    scan_all = np.ones(512, np.float32)
    scan_all[::256] = 0
    j, i = np.arange(64)[:, None], np.arange(64)[None, :]
    masks = np.stack([np.tile((j <= i).astype(np.uint32), (2, 1)), np.tile((j >= i).astype(np.uint32), (2, 1))])
    return dict(dil=rows(dil), cau=rows(cau), bcmp=pad(rows(bcmp)), vcmp=pad(rows(valid.astype(np.float32))), tri=tri,
                pm=pm, scan=np.tile(scan, (P, 1)), scan_all=np.tile(scan_all, (P, 1)), masks=masks)


def layout(a):
    k = constants()
    wi, w2 = a["w_in"][0], a["w_in_2"][0]
    cat = np.concatenate
    cols = cat([wi[:, 0:1024], wi[:, 3584:4096], wi[:, 1024:2048], wi[:, 2048:2560], wi[:, 2560:3584],
                wi[:, 4096:4352], wi[:, 4608:4864], wi[:, 4352:4608], wi[:, 4864:5120]], axis=1)
    gates = np.zeros((D, 128), np.float32)
    gates[:, 0:24] = wi[:, 5120:5144]
    alr = np.zeros((D, 128), np.float32)
    alr[:, 0:16] = w2[:, 6144:6160]
    alr[:, 32:48] = w2[:, 6160:6176]
    dn = a["w_down"][0]
    fi, fo = a["w_ffn_in_2"][0], a["w_ffn_out_2"][0]
    pair = cat([x for b in range(22) for x in (fi[:, 256 * b:256 * b + 256], fi[:, 5632 + 256 * b:5632 + 256 * b + 256])], axis=1)
    ada = a["w_ada_2"][0].reshape(16, P, 6, CH).transpose(2, 0, 1, 3).reshape(96, P, CH)
    out = {
        "w_in": blocks(cols), "w_gates": blocks(gates, 16, 128), "w_alr": blocks(alr, 16, 128),
        "w_ck": blocks(a["cmp_k_w1"][0], 16, 128), "w_cv": blocks(a["cmp_v_w1"][0], 16, 128),
        "w_outa": blocks(a["w_out"][0][0:1024]), "w_outb": blocks(a["w_out"][0][1024:2048]), "w_xkv": blocks(a["xattn_wkv"][0]), "w_xq": blocks(a["xattn_wq"][0]),
        "w_xo": blocks(a["xattn_wo"][0]), "w_up": blocks(a["w_up"][0]),
        "w_down": cat([blocks(dn[2048 * q:2048 * q + 2048]) for q in range(4)]),
        "w_ada": np.ascontiguousarray(ada),
        "w_q2": blocks(w2[:, 0:1024]), "w_k2": blocks(w2[:, 1024:2048]), "w_v2": blocks(w2[:, 2048:4096]),
        "w_g2": blocks(w2[:, 4096:6144]), "w_p2": blocks(w2[:, 6176:7200]), "w_bg2": blocks(w2[:, 7200:11296]),
        "w_gout": blocks(a["w_gla_out_2"][0]), "w_pout": blocks(a["w_pool_out_2"][0]), "w_out2": blocks(a["w_out_2"][0]),
        "w_fin": blocks(pair), "w_fout0": blocks(fo[0:2048]), "w_fout1": blocks(fo[2048:4096]), "w_fout2": blocks(fo[4096:5632]),
    }
    small = cat([columns(np.asarray(x).reshape(-1)) for x in (
        a["norm_mix"], a["norm_xattn"], a["norm_mem"], a["norm_mlp"], a["final_norm"], a["b_ada_2"], a["gla_norm_gain_2"],
        a["pool_scale_2"], a["ln_mix_gain_2"], a["ln_mix_bias_2"], a["ln_ffn_gain_2"], a["ln_ffn_bias_2"], a["b_decay_up_2"],
        a["c_2"], a["c_ctx_2"])], axis=1)
    out["c_base"] = cat([np.eye(P, dtype=np.float32), np.ones((P, P), np.float32), small], axis=1)
    row = lambda v: np.tile(np.asarray(v).reshape(1, -1), (P, 1))
    ws = a["gmlp_w_s"][0].transpose(2, 0, 1).reshape(P, -1)
    out["c_attn"] = cat([k["dil"], k["cau"], k["bcmp"], k["vcmp"], row(a["gmlp_ln_g"]), row(a["gmlp_ln_b"]), row(a["gmlp_b_s"]), ws,
                         k["tri"], a["cmp_pos"][0].T, a["cmp_k_w2"][0], a["cmp_v_w2"][0]], axis=1)
    dec = np.zeros((P, 1024), np.float32)
    dec[0:16] = a["w_decay_up_2"][0, 0]
    dec[32:48] = a["w_decay_up_2"][0, 1]
    out["c_gla"] = cat([k["scan"], k["scan_all"], dec], axis=1)
    pg = a["w_pool_group_2"][0].reshape(4, 2, P, 256).transpose(2, 1, 0, 3).reshape(P, -1)
    out["c_pool"] = cat([k["pm"], pg], axis=1)
    out["masks"] = k["masks"]
    out["x_t"], out["mem_t"], out["ctx_t"] = tokens(a["x"][0]), tokens(a["mem"][0]), tokens(a["ctx_2"][0])
    return {n: np.ascontiguousarray(v) for n, v in out.items()}


def build(nc, shapes, debug=()):
    dts = {"float32": F32, "uint32": U32}
    io = {n: nc.dram_tensor(f"in_{n}", list(s), dts[d], kind="ExternalInput").ap() for n, (s, d) in shapes.items()}
    io["out"] = nc.dram_tensor("out_0", [P, KT * S], F32, kind="ExternalOutput").ap()
    io["state"] = nc.dram_tensor("state", [4, P, 2048], F32).ap()
    io["gate"] = nc.dram_tensor("gate", [4, P, 1024], F32).ap()
    dbg = {n: nc.dram_tensor("dbg_" + n, [P, w], F32, kind="ExternalOutput").ap() for n, w in debug}
    return io, dbg


def kernel(**inputs):
    from concourse import bacc
    from concourse.bass_utils import run_bass_kernel_spmd

    arrays = layout({n: np.asarray(v) for n, v in inputs.items()})
    shapes = {n: (v.shape, v.dtype.name) for n, v in arrays.items()}
    dry = bacc.Bacc("TRN2", target_bir_lowering=False, num_devices=1)
    order = program(dry, build(dry, shapes)[0], None)
    nc = bacc.Bacc("TRN2", target_bir_lowering=False, num_devices=1)
    program(nc, build(nc, shapes)[0], order)
    r = run_bass_kernel_spmd(nc, [{f"in_{n}": v for n, v in arrays.items()}], core_ids=[0])
    got = r.results[0]["out_0"]
    return np.ascontiguousarray(got.reshape(P, KT, S).transpose(2, 1, 0)).reshape(1, S, D)
```

```python
from contextlib import ExitStack

import numpy as np

import concourse.bass as bass
from concourse import mybir

F32 = mybir.dt.float32
F32R = mybir.dt.float32r
U32 = mybir.dt.uint32
ALU = mybir.AluOpType
ACT = mybir.ActivationFunctionType
AX = mybir.AxisListType.X

P = 128
S = 256
D = 2048
KT = D // P
CH = 2048
SCALE = 128 ** -0.5
ALPHA = 2.0 ** 0.25
NEG = -1e30

PLAIN = ("ck", "cv")
NW, NR = 4, 4
HC = CH // 2
LAG = 4

PAR = {}
_at = 0
for _n, _w in (("norm_mix", 16), ("norm_xattn", 16), ("norm_mem", 16), ("norm_mlp", 16), ("final_norm", 16),
               ("b_ada", 96), ("gla_gain", 16), ("pool_scale", 8), ("lnm_g", 16), ("lnm_b", 16),
               ("lnf_g", 16), ("lnf_b", 16), ("b_decay", 16), ("c", 16), ("c_ctx", 16)):
    PAR[_n] = (_at, _at + _w)
    _at += _w
NPAR = _at

CA = {}
_at = 0
for _n, _w in (("dil", 512), ("cau", 512), ("bcmp", 32), ("vcmp", 32), ("ln_g", 512), ("ln_b", 512),
               ("b_s", 512), ("w_s", 512), ("tri", 128), ("pos", 32), ("ckw2", 128), ("cvw2", 128)):
    CA[_n] = (_at, _at + _w)
    _at += _w
NCA = _at

CG = {}
_at = 0
for _n, _w in (("scan", 512), ("pad", 512), ("decay", 1024)):
    CG[_n] = (_at, _at + _w)
    _at += _w
NCG = _at
NCP = 4096


class Queue:

    def __init__(self, engine, sem):
        self.engine, self.sem, self.n, self.seen = engine, sem, 0, {}

    def wait(self, waits):
        most = {}
        for w in flat(waits):
            key = w[0].name
            if w[1] > self.seen.get(key, 0) and w[1] > most.get(key, (0, 0))[1]:
                most[key] = w
        for key, (sem, value) in most.items():
            self.seen[key] = value
            self.engine.wait_ge(sem, value)

    def __call__(self, make, *waits, mark=True):
        self.wait(waits)
        ins = make(self.engine)
        if not mark:
            return None
        self.n += 1
        ins.then_inc(self.sem, 1)
        return (self.sem, self.n)

    def dma(self, out, in_, load, *waits):
        self.wait(waits)
        load.n += 16
        self.engine.dma_start(out, in_).then_inc(load.sem, 16)
        return (load.sem, load.n)


def flat(x):
    if x is None:
        return []
    if isinstance(x, tuple) and len(x) == 2 and isinstance(x[1], int):
        return [x]
    return [w for y in x for w in flat(y)]


class Load:

    def __init__(self, sem):
        self.sem, self.n = sem, 0

    def all(self):
        return (self.sem, self.n)


class Place:

    def __init__(self, ap):
        self.ap, self.free = ap, []


class Ring:
    def __init__(self, places):
        self.places, self.i = places, 0

    def next(self):
        self.i += 1
        return self.places[(self.i - 1) % len(self.places)]


def program(nc, io, order):
    st = ExitStack()
    found = []
    with st:
        def sem(name):
            return st.enter_context(nc.semaphore(name))

        def sb(name, width, dt=F32):
            return st.enter_context(nc.sbuf_tensor(name, [P, width], dt))

        PE, DV, AC, PO, SP = (Queue(e, sem(n)) for e, n in (
            (nc.tensor, "s_pe"), (nc.vector, "s_dve"), (nc.scalar, "s_act"), (nc.gpsimd, "s_pool"), (nc.sync, "s_sp")))
        everyone = (PE, DV, AC, PO)

        def now():
            return [(q.sem, q.n) for q in everyone if q.n]

        RW = sb("RW", NW * CH)
        RH = sb("RH", NR * HC, F32R)
        RL = sb("RL", NR * HC, F32R)
        X = sb("X", KT * S)
        over = ExitStack()
        AH = over.enter_context(nc.sbuf_tensor("AH", [P, KT * S], F32R))
        AL = over.enter_context(nc.sbuf_tensor("AL", [P, KT * S], F32R))
        over.close()
        AF = sb("AF", 2 * KT * S)
        C = sb("C", 256 + NPAR)
        MODT = sb("MODT", 96 + 32)
        RS = sb("RS", 3 * 256)
        SM = sb("SM", 160)
        over = ExitStack()
        HH = over.enter_context(nc.sbuf_tensor("HH", [P, 24 * S], F32R))
        HL = over.enter_context(nc.sbuf_tensor("HL", [P, 24 * S], F32R))
        over.close()
        NE = 10048
        G = sb("G", 48 * S + NE)
        E0 = 48 * S
        banks = [Place(st.enter_context(nc.psum_tensor(f"b{i}", [P, 512], F32))) for i in range(8)]
        pairs = Ring([Place((banks[0], banks[1])), Place((banks[2], banks[3]))])
        misc = Ring(banks[4:8])

        ident, ones = C[:, 0:128], C[:, 128:256]

        def par(name, i=None):
            a, b = PAR[name]
            return C[:, 256 + a:256 + b] if i is None else C[:, 256 + a + i:256 + a + i + 1]

        def mod(i, kt):
            return MODT[:, 16 * i + kt:16 * i + kt + 1]

        def cmod(i, kt):
            return MODT[:, 96 + 16 * i + kt:96 + 16 * i + kt + 1]

        w_sems = [Load(sem(f"s_w{i}")) for i in range(NW)]
        loaded, ready_at, prepared = {}, {}, [0]
        gem_used = []
        state = {"gemm": 0, "half": 0}

        def send(j, waits):
            if order is None or j >= len(order):
                return
            name, i = order[j]
            k = j % NW
            SP.dma(RW[:, k * CH:(k + 1) * CH], io["w_" + name][i], w_sems[k], waits)
            loaded[j] = w_sems[k].all()

        def part(t, n):
            return t[:, n % NR * HC:n % NR * HC + HC]

        def prepare():
            j = prepared[0]
            name, i = order[j]
            k = j % NW
            w = RW[:, k * CH:(k + 1) * CH]
            n, half = state["gemm"], state["half"]
            state["gemm"] += 1
            state["half"] = 1 - half
            free = gem_used[n - NR] if n >= NR else None
            hi, lo = part(RH, n), part(RL, n)
            w = w[:, half * HC:half * HC + HC]
            h = AC(lambda e: e.activation(hi, w, ACT.Copy), loaded[j], free)
            lo_t = DV(lambda e: e.tensor_tensor(lo, w, hi.bitcast(F32), ALU.subtract), h, free)
            ready_at[j, half] = (n, h, lo_t)
            if half == 1:
                prepared[0] += 1
                send(j + NW, lo_t)

        def take(name, i, half):
            if half == 0:
                state["at"] = len(found)
                found.append((name, i))
            j = state["at"]
            if order is None:
                return 0, None, None
            assert order[j] == (name, i), (order[j], name, i)
            while (j, half) not in ready_at:
                prepare()
            n, h, lo_t = ready_at[j, half]
            while (prepared[0] < len(order) and order[prepared[0]][0] not in PLAIN
                   and state["gemm"] < min(n, len(gem_used)) + NR):
                prepare()
            return n, h, lo_t

        def used(mark):
            gem_used.append(mark)

        def gemm(name, first, n_blocks, kc, hi, lo, ready, form, evac):
            rest = []
            for b in range(n_blocks):
                pair = pairs.next()
                bb = pair.ap
                for c in range(2 * kc):
                    n, wh_t, wl_t = take(name, (first + b) * kc + c // 2, c % 2)
                    wh = part(RH, n).rearrange("p (k n) -> p k n", k=2)
                    wl = part(RL, n).rearrange("p (k n) -> p k n", k=2)
                    PE.wait([wh_t, wl_t, ready[c // 2], bb[0].free, bb[1].free])
                    t = None
                    if form == "T":
                        for m in range(4):
                            out = bb[m // 2].ap[:, (m % 2) * 256:(m % 2) * 256 + 256]
                            for k in range(2):
                                cols = slice(m * 128, m * 128 + 128)
                                start = c == 0 and k == 0 and m % 2 == 0
                                stop = c == 2 * kc - 1 and k == 1
                                for q, (l, r) in enumerate(((wh, hi), (wh, lo), (wl, hi))):
                                    lhs, rhs = l[:, k, cols], r(2 * c + k)
                                    a, z = start and q == 0, stop and q == 2
                                    last = m == 3 and k == 1 and q == 2
                                    t = PE(lambda e, o=out, l=lhs, r=rhs, a=a, z=z: e.matmul(
                                        o, l, r, start=a, stop=z, skip_group_check=True), mark=last) or t
                    else:
                        for m in range(2):
                            out = bb[m].ap[:, :]
                            for k in range(2):
                                start, stop = c == 0 and k == 0, c == 2 * kc - 1 and k == 1
                                for q, (l, r) in enumerate(((hi, wh), (lo, wh), (hi, wl))):
                                    lhs, rhs = l(2 * c + k)[:, m * 128:m * 128 + 128], r[:, k, :]
                                    a, z = start and q == 0, stop and q == 2
                                    last = m == 1 and k == 1 and q == 2
                                    t = PE(lambda e, o=out, l=lhs, r=rhs, a=a, z=z: e.matmul(
                                        o, l, r, start=a, stop=z, skip_group_check=True), mark=last) or t
                    used(t)
                    if rest:
                        rest.pop(0)()
                    yield
                for f in rest:
                    f()
                if b == 0 and "factor" in state:
                    state.pop("factor")()
                rest = list(evac(b, bb, t) or ())
                if b + 1 < n_blocks:
                    yield
            for f in rest:
                f()
            yield

        def small(name, hi, lo, ready, out):
            for half in range(2):
                n, wh_t, wl_t = take(name, 0, half)
                wh = part(RH, n).rearrange("p (k n) -> p k n", k=8)
                wl = part(RL, n).rearrange("p (k n) -> p k n", k=8)
                PE.wait([wh_t, wl_t, ready, out.free])
                t = None
                for k in range(8):
                    for q, (l, r) in enumerate(((wh, hi), (wh, lo), (wl, hi))):
                        t = PE(lambda e, l=l[:, k, :], r=r(8 * half + k), a=half == k == q == 0, z=half == 1 and k == 7 and q == 2: e.matmul(
                            out.ap[:, 0:256], l, r, start=a, stop=z), mark=k == 7 and q == 2) or t
                used(t)
            return t

        def ap_of(t, base=0):
            return lambda kt: t[:, (base + kt) * S:(base + kt + 1) * S]

        def split(hi, lo, src, *waits, on=None):
            h = AC(lambda e: e.activation(hi, src, ACT.Copy), *waits)
            return (on or DV)(lambda e: e.tensor_tensor(lo, src, hi.bitcast(F32), ALU.subtract), h, *waits)

        class Sums:

            def __init__(self, acc, tmps):
                self.acc, self.tmps, self.n, self.t = acc, tmps, 0, None

            def square(self, x, *waits):
                if self.n == 0:
                    self.t = AC(lambda e: e.activation(self.acc.ap, x, ACT.Square), *waits, self.acc.free)
                else:
                    tm = self.tmps.next()
                    a = AC(lambda e: e.activation(tm.ap, x, ACT.Square), *waits, tm.free)
                    self.t = DV(lambda e: e.tensor_tensor(self.acc.ap, self.acc.ap, tm.ap, ALU.add), a, self.t)
                    tm.free = [self.t]
                self.n += 1

            def plain(self, x, *waits):
                if self.n == 0:
                    self.t = DV(lambda e: e.tensor_copy(self.acc.ap, x), *waits, self.acc.free)
                else:
                    self.t = DV(lambda e: e.tensor_tensor(self.acc.ap, self.acc.ap, x, ALU.add), *waits, self.t)
                self.n += 1

            def over_partitions(self):
                bk = misc.next()
                for k in range(2):
                    t = PE(lambda e: e.matmul(bk.ap[:, 0:256], ones, self.acc.ap[:, k * 256:k * 256 + 256],
                                              start=k == 0, stop=k == 1), self.t, bk.free)
                self.acc.free = [t]
                return bk, t

        def rstd(sums, eps=1e-6):
            bk, t = sums.over_partitions()
            a = DV(lambda e: e.tensor_scalar(RS[:, 256:512], bk.ap[:, 0:256], 1.0 / D, eps, ALU.mult, ALU.add), t, state.get("rs"))
            bk.free = [a]
            b = AC(lambda e: e.activation(RS[:, 512:768], RS[:, 256:512], ACT.Sqrt), a)
            return DV(lambda e: e.reciprocal(RS[:, 0:256], RS[:, 512:768]), b, state.get("rs"))

        R2 = RS[:, 0:256].unsqueeze(1).to_broadcast([P, 2, 256])
        RC = SM[:, 128:130]

        def pair2(ap):
            return ap.rearrange("p (k t) -> p k t", k=2)

        def rstd_columns(r):
            bk = misc.next()
            for i in range(2):
                t = PE(lambda e: e.transpose(bk.ap[:, i * 128:i * 128 + 128], RS[:, i * 128:i * 128 + 128], ident), r, bk.free)
            c = DV(lambda e: e.tensor_copy(RC, bk.ap[:, 0:256:128]), t, state.get("rc"))
            bk.free = [c]
            return c

        def feed(src, kt, gain, hi, lo, waits, free):
            for k in (kt, kt + 1):
                d = slice(k * S, k * S + S)
                h = AC(lambda e: e.activation(hi[:, d], src[:, d], ACT.Copy, scale=par(gain, k)), waits, free)
                t = DV(lambda e: e.scalar_tensor_tensor(lo[:, d], src[:, d], par(gain, k), hi[:, d].bitcast(F32),
                                                        ALU.mult, ALU.subtract), h, waits, free)
            return t

        def load(name, out, in_, waits=(), q=None):
            ld = Load(sem("s_l_" + name))
            (q or PO).dma(out, in_, ld, *waits)
            return ld.all()

        l_c = load("c", C[:, :], io["c_base"], q=SP)
        l_x = []
        for i in range(4):
            l_x.append(load(f"x{i}", X[:, 1024 * i:1024 * i + 1024], io["x_t"][:, 1024 * i:1024 * i + 1024], q=SP))
            send(i, None)
        l_ca = load("ca", G[:, E0:E0 + NCA], io["c_attn"], q=SP)
        debug = io.get("debug", {})
        dbg_load = Load(sem("s_dbg")) if debug else None

        def dbg(name, ap):
            if name in debug:
                w = PO.dma(debug[name], ap, dbg_load, now())
                for q in everyone:
                    q.wait([w])

        def ca(name):
            a, b = CA[name]
            return G[:, E0 + a:E0 + b]

        F0 = E0 + NCA
        SCR = F0
        XK, XV = G[:, F0 + 4096:F0 + 5120], G[:, F0 + 5120:F0 + 6144]
        GN, KC, VC = G[:, F0 + 6144:F0 + 6208], G[:, F0 + 6208:F0 + 6240], G[:, F0 + 6240:F0 + 6496]
        assert F0 + 6496 <= E0 + NE
        bufs = [Place(G[:, SCR + 512 * i:SCR + 512 * i + 512]) for i in range(8)]
        sums = Sums(bufs[0], Ring(bufs[1:3]))
        hA, lA = ap_of(AH), ap_of(AL)
        ra = [[] for _ in range(4)]

        def feeding(sums, gain, ready, waits, free):
            for kt in range(0, 16, 2):
                ready[kt // 4].append(feed(X, kt, gain, AH, AL, waits(kt), free))
                sums.square(X[:, kt * S:kt * S + 512], waits(kt))
                yield

        R = RCt = None

        UA, VA, QKB, QC = G[:, 0:1024], G[:, 1024:2048], G[:, 2048:4096], G[:, 4096:6144]
        VB, CKV, GT = G[:, 6144:7168], G[:, 7168:8192], G[:, 8192:8448]
        KSW, VSW = G[:, 10240:11264], G[:, 11264:12288]
        got = {}

        def to(dst, key, func=None, free=None):
            def evac(b, bb, t):
                for i in range(2):
                    o = dst[:, b * 1024 + i * 512:b * 1024 + i * 512 + 512]
                    r = DV(lambda e: e.tensor_tensor(pair2(o), pair2(bb[i].ap[:, :]), R2, ALU.mult), t, R, free)
                    bb[i].free = [r]
                    if func is not None:
                        r = AC(lambda e: e.activation(o, o, func), r)
                    got.setdefault(key, []).append(r)
                state["rs"] = [(DV.sem, DV.n)]
            return evac

        def to_n(dst, key, func=ACT.Copy, free=None):
            def evac(b, bb, t):
                for i in range(2):
                    o = dst[:, i * 512:i * 512 + 512]
                    r = AC(lambda e: e.activation(o, bb[i].ap[:, :], func, scale=RC[:, i:i + 1]), t, RCt, free)
                    bb[i].free = [r]
                    got.setdefault(key, []).append(r)
                state["rc"] = [r]
            return evac

        def run(*gens, beside=None):
            gens = list(gens)
            while gens:
                if beside is not None:
                    next(beside, None)
                for x in list(gens):
                    if next(x, "end") == "end":
                        gens.remove(x)

        def w_in(*names):
            for name in names:
                if name == "ua":
                    yield from gemm("in", 0, 1, 4, hA, lA, ra, "T", to(UA, "ua", ACT.Gelu_apprx_tanh))
                elif name == "va":
                    yield from gemm("in", 1, 1, 4, hA, lA, ra, "N", to_n(VA, "va", ACT.Gelu_apprx_tanh))
                elif name == "ckv":
                    yield from gemm("in", 2, 1, 4, hA, lA, ra, "T", to(CKV, "ckv"))
                elif name == "qkb":
                    yield from gemm("in", 3, 2, 4, hA, lA, ra, "T", to(QKB, "qkb"))
                elif name == "vb":
                    yield from gemm("in", 5, 1, 4, hA, lA, ra, "N", to_n(VB, "vb"))
                elif name == "qc":
                    yield from gemm("in", 6, 2, 4, hA, lA, ra, "T", to(QC, "qc"))
                elif name == "ksw":
                    yield from gemm("in", 8, 1, 4, hA, lA, ra, "T", to(KSW, "ksw"))
                elif name == "vsw":
                    yield from gemm("in", 9, 1, 4, hA, lA, ra, "N", to_n(VSW, "vsw", free=got["b1free"]))
                elif name == "gates":
                    bk = misc.next()
                    t = small("gates", hA, lA, ra, bk)
                    r = DV(lambda e: e.tensor_tensor(GT[0:32, :], bk.ap[0:32, 0:256], RS[0:32, 0:256], ALU.mult), t, R)
                    bk.free = [r]
                    state["rs"] = [r]
                    r = AC(lambda e: e.activation(GT[0:32, :], GT[0:32, :], ACT.Sigmoid), r)
                    bk = misc.next()
                    for i in range(2):
                        t = PE(lambda e: e.transpose(bk.ap[:, i * 32:i * 32 + 32], GT[0:32, i * 128:i * 128 + 128],
                                                     ident[0:32, 0:32]), r, bk.free)
                    r = DV(lambda e: e.tensor_copy(GN, bk.ap[:, 0:64]), t)
                    bk.free = [r]
                    got["gates"] = [r]

        SILT = sb("SILT", 32)
        sil = AC(lambda e: e.activation(SILT[:, :], C[:, 256 + PAR["c"][0]:256 + PAR["c_ctx"][1]], ACT.Silu), l_c)
        ada_at = {"acc": {}, "t": [[None] * 4, [None] * 4]}

        def ada(i, w, ld):
            cb, kt = divmod(i, 16)
            done = []
            for m in range(4):
                if kt == 0:
                    late(m)
                for which in range(2 if cb < 2 else 1):
                    pl = ada_at["acc"][cb][which]
                    d = slice(512 * m, 512 * m + 512)
                    a, s_ = pl.ap[:, d], SILT[:, which * 16 + kt:which * 16 + kt + 1]
                    if kt == 0:
                        t = DV(lambda e: e.tensor_scalar(a, w[:, d], s_, None, ALU.mult), ld, sil, pl.free)
                    else:
                        t = DV(lambda e: e.scalar_tensor_tensor(a, w[:, d], s_, a, ALU.mult, ALU.add), ld, ada_at["t"][which][m])
                    ada_at["t"][which][m] = t
                    done.append(t)
                    if kt == 15:
                        ada_late.append([3, cb, m, which, pl, t])
                yield done if m == 3 else None

        def over_rows(cb, m, which, pl, t):
            bk = misc.next()
            for j in range(4):
                p = PE(lambda e: e.transpose(bk.ap[:, j * 128:j * 128 + 128],
                                             pl.ap[:, (4 * m + j) * 128:(4 * m + j) * 128 + 128], ident), t, bk.free)
            o = 96 * which + cb * 16 + 4 * m
            r = DV(lambda e: e.tensor_reduce(MODT[:, o:o + 4], bk.ap[:, :].rearrange("p (j t) -> p j t", j=4), AX, ALU.add), p)
            bk.free = [r]
            pl.free = [pl.free, p]
            r = DV(lambda e: e.tensor_tensor(MODT[:, o:o + 4], MODT[:, o:o + 4],
                                             par("b_ada")[:, cb * 16 + 4 * m:cb * 16 + 4 * m + 4], ALU.add), r)
            got.setdefault("mod", []).append(r)

        ada_late = []
        def late(m=None):
            for x in ada_late:
                x[0] -= m is None
            while ada_late and (ada_late[0][0] <= 0 or m in [x[2] for x in ada_late]):
                over_rows(*ada_late.pop(0)[1:])

        def ada_apart(blocks_of_columns, pauses, slots):
            todo = [(cb * 16 + kt, p) for cb, p in zip(blocks_of_columns, pauses) for kt in range(16)]

            def fetch(n):
                if n < len(todo):
                    s_ = slots[n % 2]
                    s_.ld = SP.dma(s_.ap, io["w_ada"][todo[n][0]], a_sems[n % 2], s_.free)

            fetch(0)
            fetch(1)
            for _ in range(LAG + 1):
                yield
            work = 0.0
            for n, (i, pause) in enumerate(todo):
                s_ = slots[n % 2]
                for done in ada(i, s_.ap, s_.ld):
                    while work >= 1:
                        work -= 1
                        late()
                        yield
                    work += pause / 2
                s_.free = done
                fetch(n + 2)
            for _ in range(3):
                yield
                late()

        a_sems = [Load(sem(f"s_a{i}")) for i in range(2)]

        def both(*gens):
            gens = list(gens)
            while gens:
                for x in list(gens):
                    if next(x, "end") == "end":
                        gens.remove(x)
                yield

        def slow(gen, pause):
            due = 0.0
            for _ in gen:
                due += pause
                while due >= 1:
                    due -= 1
                    yield

        def chain(*gens):
            for gen in gens:
                yield from gen

        def after(n, gen):
            for _ in range(n):
                yield
            yield from gen

        def rstd_later(sums, columns=False):
            def factor():
                nonlocal R, RCt
                R = rstd(sums)
                if columns:
                    RCt = rstd_columns(R)
            state["factor"] = factor

        rstd_later(sums, True)
        run(feeding(sums, "norm_mix", ra, lambda kt: [l_x[kt // 4], l_c], None), w_in("ckv", "qkb", "vb", "ua", "va"))

        scr = Ring(bufs[0:5])
        pts = Ring(bufs[5:8])
        base = now()
        for b_ in bufs:
            b_.free = list(base)
        sms = Ring([Place(SM[:, 8 * i:8 * i + 8]) for i in range(8)])
        in_done = []

        def gmlp():
            sm = sms.next()
            W = scr.next()
            w_m = pts.next()
            mk = DV(lambda e: e.tensor_tensor(
                w_m.ap.rearrange("p (g t) -> p g t", g=4), ca("w_s").rearrange("p (g t) -> p g t", g=4),
                ca("tri").unsqueeze(1).to_broadcast([P, 4, 128]), ALU.mult), l_ca, w_m.free)
            outs = []
            for i in range(2):
                v = VA[:, i * 512:i * 512 + 512]
                a = AC(lambda e, v=v, i=i: e.activation(W.ap, v, ACT.Copy, accum_out=sm.ap[:, i:i + 1]), got["va"], W.free, sm.free)
                b = DV(lambda e, i=i: e.tensor_scalar(sm.ap[:, i:i + 1], sm.ap[:, i:i + 1], -1.0 / 512, None, ALU.mult), a)
                c = DV(lambda e, v=v, i=i: e.tensor_scalar(v, v, sm.ap[:, i:i + 1], None, ALU.add), b)
                d = AC(lambda e, v=v, i=i: e.activation(W.ap, v, ACT.Square, accum_out=sm.ap[:, 2 + i:3 + i]), c)
                W.free = [d]
                f = DV(lambda e, i=i: e.tensor_scalar(sm.ap[:, 2 + i:3 + i], sm.ap[:, 2 + i:3 + i], 1.0 / 512, 1e-6, ALU.mult, ALU.add), d)
                h = AC(lambda e, i=i: e.activation(sm.ap[:, 4 + i:5 + i], sm.ap[:, 2 + i:3 + i], ACT.Sqrt), f)
                k = DV(lambda e, i=i: e.reciprocal(sm.ap[:, 6 + i:7 + i], sm.ap[:, 4 + i:5 + i]), h)
                m = DV(lambda e, v=v, i=i: e.scalar_tensor_tensor(v, v, sm.ap[:, 6 + i:7 + i], ca("ln_g"), ALU.mult, ALU.mult), k)
                o = DV(lambda e, v=v: e.tensor_tensor(v, v, ca("ln_b"), ALU.add), m)
                outs.append(o)
            sm.free = [outs[-1]]
            yield
            bk = [misc.next(), misc.next()]
            ts = []
            for i in range(2):
                for q in range(4):
                    t = PE(lambda e, i=i, q=q: e.matmul(
                        bk[q // 2].ap[:, (q % 2) * 256 + i * 128:(q % 2) * 256 + i * 128 + 128],
                        VA[:, i * 512 + q * 128:i * 512 + q * 128 + 128], w_m.ap[:, q * 128:q * 128 + 128],
                        start=True, stop=True), outs[i], mk, bk[0].free, bk[1].free)
            w_m.free = [t]
            yield
            for j in range(2):
                W = scr.next()
                bs = ca("b_s")[:, j * 256:j * 256 + 256].rearrange("p (g t) -> p g t", g=2).unsqueeze(2).to_broadcast([P, 2, 2, 128])
                a = DV(lambda e, j=j, W=W, bs=bs: e.tensor_tensor(
                    W.ap.rearrange("p (g i t) -> p g i t", g=2, i=2), bk[j].ap[:, :].rearrange("p (g i t) -> p g i t", g=2, i=2),
                    bs, ALU.add), t, W.free)
                bk[j].free = [a]
                b = DV(lambda e: e.tensor_tensor(UA[:, j * 512:j * 512 + 512], W.ap, UA[:, j * 512:j * 512 + 512], ALU.mult), a, got["ua"])
                W.free = [b]
                got.setdefault("whole", []).append(b)
                yield

        def scores(qT, kT, bias, gate, ready, n=256):
            bk, sc, sm = misc.next(), scr.next(), sms.next()
            for i in range(2):
                t = PE(lambda e, i=i: e.matmul(bk.ap[:, i * n:i * n + n], qT[:, i * 128:i * 128 + 128], kT,
                                               start=True, stop=True), ready, bk.free)
            sv = sc.ap[:, 0:2 * n].rearrange("p (i k) -> p i k", i=2)
            if bias is not None:
                a = DV(lambda e: e.scalar_tensor_tensor(sc.ap[:, 0:2 * n], bk.ap[:, 0:2 * n], SCALE, bias, ALU.mult, ALU.add),
                       t, sc.free, l_ca)
                bk.free = [a]
                m = DV(lambda e: e.tensor_reduce(sm.ap[:, 0:2], sv, AX, ALU.max, negate=True), a, sm.free)
                src, scale = sc.ap, 1.0
            else:
                a = DV(lambda e: e.tensor_reduce(sm.ap[:, 6:8], bk.ap[:, 0:2 * n].rearrange("p (i k) -> p i k", i=2), AX, ALU.max,
                                                 negate=True), t, sm.free)
                m = DV(lambda e: e.tensor_scalar(sm.ap[:, 0:2], sm.ap[:, 6:8], SCALE, None, ALU.mult), a)
                src, scale = bk.ap, SCALE
            for i in range(2):
                b = AC(lambda e, i=i: e.activation(sc.ap[:, i * n:i * n + n], src[:, i * n:i * n + n], ACT.Exp,
                                                   bias=sm.ap[:, i:i + 1], scale=scale, accum_out=sm.ap[:, 2 + i:3 + i]), m, sc.free)
            if bias is None:
                bk.free = [b]
            r = DV(lambda e: e.reciprocal(sm.ap[:, 4:6], sm.ap[:, 2:4]), b)
            if gate is not None:
                r = DV(lambda e: e.tensor_tensor(sm.ap[:, 4:6], sm.ap[:, 4:6], gate, ALU.mult), r, got["gates"])
            p = DV(lambda e: e.tensor_tensor(sv, sv, sm.ap[:, 4:6].unsqueeze(2).to_broadcast([P, 2, n]), ALU.mult), r)
            sm.free = [p]
            return sc, p

        def turned(sc, p, n=256, causal=True):
            bk, pt = misc.next(), pts.next()
            if n < 128:
                for i in range(2):
                    t = PE(lambda e, i=i: e.transpose(bk.ap[0:n, i * 128:i * 128 + 128], sc.ap[:, i * n:i * n + n], ident), p, bk.free)
                c = AC(lambda e: e.activation(pt.ap[0:n, 0:256], bk.ap[0:n, 0:256], ACT.Copy), t, pt.free)
                blocks = [(0, 0), (1, 0)]
            else:
                blocks = [(0, 0), (1, 0), (1, 1)] if causal else [(0, 0), (0, 1), (1, 0), (1, 1)]
                for j, (i, k) in enumerate(blocks):
                    t = PE(lambda e, i=i, k=k, j=j: e.transpose(
                        bk.ap[:, j * 128:j * 128 + 128], sc.ap[:, i * 256 + k * 128:i * 256 + k * 128 + 128], ident), p, bk.free)
                w = len(blocks) * 128
                c = AC(lambda e: e.activation(pt.ap[:, 0:w], bk.ap[:, 0:w], ACT.Copy), t, pt.free)
            sc.free = [t]
            bk.free = [c]
            return pt, c, blocks

        def attend(units, out_hi, out_lo, extra):
            bk = misc.next()
            for i in range(2):
                ops = [(pt, j, n, v(k), c) for (pt, c, blocks), v, n in units for j, (ii, k) in enumerate(blocks) if ii == i]
                for a, (pt, j, n, v, c) in enumerate(ops):
                    t = PE(lambda e, i=i, j=j, n=n, v=v, pt=pt, a=a, z=len(ops) - 1: e.matmul(
                        bk.ap[:, i * 128:i * 128 + 128], v, pt.ap[0:n, j * 128:j * 128 + 128], start=a == 0, stop=a == z),
                        c, bk.free, extra)
            for (pt, _, _), _, _ in units:
                pt.free = [t]
            if out_lo is None:
                r = AC(lambda e: e.activation(out_hi, bk.ap[:, 0:256], ACT.Copy), t)
                bk.free = [r]
                got.setdefault("whole", []).append(r)
                return
            h = AC(lambda e: e.activation(out_hi, bk.ap[:, 0:256], ACT.Copy), t, in_done)
            r = DV(lambda e: e.tensor_tensor(out_lo, bk.ap[:, 0:256], out_hi.bitcast(F32), ALU.subtract), h, t, in_done)
            bk.free = [r]
            got.setdefault("mix", []).append(r)

        def dilated():
            held = None
            for h in range(5):
                new = None
                if h < 4:
                    new = scores(QKB[:, h * 256:h * 256 + 256], QKB[:, 1024 + h * 256:1024 + h * 256 + 256], ca("dil"), None, got["qkb"])
                    yield
                if held is not None:
                    tr = turned(*held)
                    attend([(tr, lambda k, h=h: VB[:, k * 512 + (h - 1) * 128:k * 512 + h * 128], 128)],
                           QKB[:, (h - 1) * S:h * S], None, got["vb"])
                    yield
                held = new

        B1 = VSW[:, 0:960]

        def compress():
            for kv in range(2):
                w_name = ("ck", "cv")[kv]
                hid = misc.next()
                vb = B1.rearrange("p (g n j) -> p g n j", g=2, n=15)
                ov = CKV[:, kv * 512:kv * 512 + 512].rearrange("p (g n j) -> p g n j", g=2, n=16)
                po = ca("pos").rearrange("p (h j) -> p h j", h=2)
                for h in range(2):
                    a = DV(lambda e, h=h: e.tensor_tensor(
                        vb[:, :, :, h * 16:h * 16 + 16], ov[:, :, h:h + 15, :],
                        po[:, h, :].unsqueeze(1).unsqueeze(1).to_broadcast([P, 2, 15, 16]), ALU.add),
                        got["ckv"], l_ca, got.get("b1free"))
                t = None
                for c in range(2):
                    w, wt, rel = take_plain(w_name, c)
                    for j in range(16):
                        jj = 16 * c + j
                        t = PE(lambda e, w=w, j=j, jj=jj: e.matmul(
                            hid.ap[:, 0:30], w[:, j * 128:j * 128 + 128], vb[:, :, :, jj], start=jj == 0, stop=jj == 31),
                            wt, a, hid.free, mark=j == 15) or t
                    rel(t)
                    yield
                got["b1free"] = [t]
                h_sb = sms8.next()
                b = AC(lambda e: e.activation(h_sb.ap[:, 0:30], hid.ap[:, 0:30], ACT.Gelu_apprx_tanh), t, h_sb.free)
                hid.free = [b]
                o = misc.next()
                if kv == 0:
                    t = PE(lambda e: e.matmul(o.ap[:, 0:30], ca("ckw2"), h_sb.ap[:, 0:30], start=True, stop=True), b, o.free)
                    r = DV(lambda e: e.tensor_copy(KC[:, 0:30], o.ap[:, 0:30]), t)
                    got["kc"] = [r]
                else:
                    for q in range(2):
                        t = PE(lambda e, q=q: e.matmul(o.ap[0:15, q * 128:q * 128 + 128], h_sb.ap[:, q * 15:q * 15 + 15],
                                                       ca("cvw2"), start=True, stop=True), b, o.free)
                    r = DV(lambda e: e.tensor_copy(VC[0:15, :], o.ap[0:15, 0:256]), t)
                    got["vc"] = [r]
                o.free = [r]
                h_sb.free = [t]
                yield

        sms8 = Ring([Place(SM[:, 64 + 32 * i:64 + 32 * i + 32]) for i in range(2)])
        def take_plain(name, i):
            j = len(found)
            found.append((name, i))
            if order is None:
                return RW[:, 0:CH], None, lambda t: None
            assert order[j] == (name, i)
            while prepared[0] < j:
                prepare()
            assert prepared[0] == j
            prepared[0] += 1
            k = j % NW
            return RW[:, k * CH:(k + 1) * CH], loaded[j], lambda t: send(j + NW, t)

        def nsa():
            held = None
            for h in range(9):
                new = None
                if held is not None:
                    tc = turned(*held[0], n=15)
                if h < 8:
                    q, gq = QC[:, h * 256:h * 256 + 256], h // 4
                    gate = lambda i: GN.rearrange("p (i c) -> p i c", i=2)[:, :, h * 3 + i]
                    sc, p = scores(q, KC[:, gq * 15:gq * 15 + 15], ca("bcmp")[:, 0:30], gate(0), [got["qc"], got["kc"]], n=15)
                    p = DV(lambda e: e.tensor_tensor(sc.ap[:, 0:30], sc.ap[:, 0:30], ca("vcmp")[:, 0:30], ALU.mult), p)
                    yield
                    if held is not None:
                        t1 = turned(*held[1])
                        yield
                    s1 = scores(q, KSW[:, gq * 256:gq * 256 + 256], ca("cau"), gate(1), [got["qc"], got["ksw"]])
                    yield
                    if held is not None:
                        t2 = turned(*held[2])
                        yield
                    s2 = scores(q, KSW[:, 512 + gq * 256:512 + gq * 256 + 256], ca("cau"), gate(2), [got["qc"], got["ksw"]])
                    yield
                    new = ((sc, p), s1, s2)
                elif held is not None:
                    t1, t2 = turned(*held[1]), turned(*held[2])
                if held is not None:
                    gq, o = (h - 1) // 4, (8 + h - 1) * S
                    attend([(t1, lambda k: VSW[:, k * 512 + gq * 128:k * 512 + gq * 128 + 128], 128),
                            (t2, lambda k: VSW[:, k * 512 + 256 + gq * 128:k * 512 + 256 + gq * 128 + 128], 128),
                            (tc, lambda k: VC[0:15, gq * 128:gq * 128 + 128], 15)],
                           AH[:, o:o + S], AL[:, o:o + S], [got["vsw"], got["vc"]])
                    yield
                held = new

        def early():
            yield from compress()
            yield from gmlp()
            yield from dilated()

        got["b1free"] = []
        run(early(), w_in("qc", "ksw", "gates", "vsw"))
        in_done = [(PE.sem, PE.n)]
        got["mix_ab"] = []
        for i in range(4):
            src = (UA if i < 2 else QKB)[:, (i % 2) * 512:(i % 2) * 512 + 512]
            d = slice(512 * i, 512 * i + 512)
            got["mix_ab"].append(split(AH[:, d], AL[:, d], src, got["whole"], in_done))
        dbg("mixh", AH[:, :].bitcast(F32))

        MEM = G[:, 24 * S:24 * S + 4096]
        z_free = now()
        l_m = [load(f"mem{i}", MEM[:, 1024 * i:1024 * i + 1024], io["mem_t"][:, 1024 * i:1024 * i + 1024], [z_free]) for i in range(4)]
        rm = []
        m_bufs = [Place(ca(n)) for n in ("ln_g", "ln_b", "b_s")]
        for b_ in m_bufs:
            b_.free = list(z_free)

        def memory():
            nonlocal R, RCt
            sums = Sums(m_bufs[0], Ring(m_bufs[1:3]))
            for i in range(4):
                for kt in (4 * i, 4 * i + 2):
                    sums.square(MEM[:, kt * S:kt * S + 512], l_m[i])
                    for k in (kt, kt + 1):
                        d2 = slice(k * S, k * S + S)
                        h = AC(lambda e: e.activation(HH[:, d2], MEM[:, d2], ACT.Copy, scale=par("norm_mem", k)), l_m[i], z_free)
                        t = DV(lambda e: e.scalar_tensor_tensor(HL[:, d2], MEM[:, d2], par("norm_mem", k), HH[:, d2].bitcast(F32),
                                                                ALU.mult, ALU.subtract), h, l_m[i], sums.t, z_free)
                    yield
                rm.append(t)
            R = rstd(sums)
            RCt = rstd_columns(R)

        hM, lM = ap_of(HH), ap_of(HL)

        got["x"] = []

        def add_x(b, bb, t):
            for i in range(2):
                x = X[:, b * 1024 + i * 512:b * 1024 + i * 512 + 512]
                r = DV(lambda e: e.tensor_tensor(x, bb[i].ap[:, :], x, ALU.add), t, got["x"])
                bb[i].free = [r]
            got["x"] = [r]

        def beside_nsa():
            yield from both(gemm("outa", 0, 4, 2, hA, lA, [got["mix_ab"]] * 2, "T", add_x), after(4, memory()))
            yield from gemm("xkv", 0, 1, 4, hM, lM, rm, "T", to(XK, "xk"))
            yield from gemm("xkv", 1, 1, 4, hM, lM, rm, "N", to_n(XV, "xv"))

        got["mix"] = []
        run(nsa(), slow(beside_nsa(), 1.2))

        def add_feed(sums, gain, wait_from, fed):
            def evac(b, bb, t):
                for i in range(2):
                    kt = 4 * b + 2 * i
                    x = X[:, kt * S:kt * S + 512]
                    r = DV(lambda e: e.tensor_tensor(x, bb[i].ap[:, :], x, ALU.add), t, got["x"])
                    bb[i].free = [r]
                    if wait_from[0] <= kt < wait_from[1]:
                        fed.append((kt, r))
                    else:
                        fed.append((kt, feed(X, kt, gain, AH, AL, r, wait_from[2])))
                    sums.square(x, r)
            return evac

        def fed_tiles(fed, wait_from, gain):
            free = [(PE.sem, PE.n)]
            out = [[] for _ in range(4)]
            for kt, r in fed:
                if wait_from[0] <= kt < wait_from[1]:
                    r = feed(X, kt, gain, AH, AL, r, free)
                out[kt // 4].append(r)
            return out

        base = now()
        for b_ in bufs:
            b_.free = list(base)
        sums = Sums(bufs[0], Ring(bufs[1:3]))
        fed, held_back = [], (8, 16, base)
        run(gemm("outb", 0, 4, 2, ap_of(AH, 8), ap_of(AL, 8), [got["mix"]] * 2, "T", add_feed(sums, "norm_xattn", held_back, fed)))
        rx = fed_tiles(fed, held_back, "norm_xattn")
        dbg("x1", X[:, :])

        XQ = G[:, 0:1024]
        got["xq"] = []
        rstd_later(sums)
        run(gemm("xq", 0, 1, 4, hA, lA, rx, "T", to(XQ, "xq")))
        scr, pts = Ring(bufs[0:4]), Ring(bufs[4:7])
        in_done = [(PE.sem, PE.n)]
        got["mix"] = []

        def cross():
            held = None
            for h in range(5):
                new = None
                if h < 4:
                    new = scores(XQ[:, h * 256:h * 256 + 256], XK[:, h * 256:h * 256 + 256], None, None, [got["xq"], got["xk"]])
                    yield
                if held is not None:
                    tr = turned(*held, causal=False)
                    o = (h - 1) * S
                    attend([(tr, lambda k, h=h: XV[:, k * 512 + (h - 1) * 128:k * 512 + h * 128], 128)],
                           AH[:, o:o + S], AL[:, o:o + S], got["xv"])
                    yield
                held = new

        run(cross())
        base = now()
        for b_ in bufs:
            b_.free = list(base)
        run(gemm("xo", 0, 4, 1, hA, lA, [got["mix"]], "T", add_x))
        rm, x2_t, x2_free = [[] for _ in range(4)], got["x"], [(PE.sem, PE.n)]
        dbg("x2", X[:, :])

        tmps = Ring([Place(G[:, E0 + 4096 + 512 * i:E0 + 4608 + 512 * i]) for i in range(3)])
        base = now()
        for s_ in tmps.places:
            s_.free = list(base)
        s_bufs = [Place(G[:, 4096 + 512 * i:4608 + 512 * i]) for i in range(3)]
        slots = [Place(G[:, E0 + 5632 + 2048 * i:E0 + 7680 + 2048 * i]) for i in range(2)]
        for s_ in s_bufs + slots:
            s_.free = list(base)
        sums_x2 = Sums(s_bufs[0], Ring(s_bufs[1:]))
        late_acc = [Place(G[:, E0:E0 + 2048]), Place(G[:, E0 + 2048:E0 + 4096])]
        for s_ in late_acc:
            s_.free = list(base)
        ada_at["acc"][0] = ada_at["acc"][1] = ada_at["acc"][4] = late_acc
        hid_free = [base] * 24
        hid_ready = [None] * 24

        def up(qn, b0, nb):
            def evac(b, bb, t):
                held = []
                for i in range(2):
                    tm = tmps.next()
                    r = DV(lambda e: e.scalar_tensor_tensor(pair2(tm.ap), pair2(bb[i].ap[:, :]), 0.0, R2, ALU.max, ALU.mult), t, R, tm.free)
                    bb[i].free = [r]
                    held.append((i, tm, AC(lambda e, tm=tm: e.activation(tm.ap, tm.ap, ACT.Square), r)))

                def parts():
                    for i, tm, r2 in held:
                        kt = (16 * qn + 4 * (b0 + b) + 2 * i) % 24
                        d = slice(kt * S, kt * S + 512)
                        z = split(HH[:, d], HL[:, d], tm.ap, r2, hid_free[kt])
                        tm.free = [z]
                        hid_ready[kt] = hid_ready[kt + 1] = z
                return [parts]
            yield from gemm("up", 4 * qn + b0, nb, 4, hA, lA, rm, "T", evac)

        def ring24(t, qn):
            return lambda kt: t[:, ((16 * qn + kt) % 24) * S:((16 * qn + kt) % 24 + 1) * S]

        def down(qn):
            ready = [[hid_ready[(16 * qn + 4 * c + k) % 24] for k in range(4)] for c in range(4)]
            yield from gemm("down", 4 * qn, 4, 4, ring24(HH, qn), ring24(HL, qn), ready, "T", add_x)
            for k in range(16):
                hid_free[(16 * qn + k) % 24] = [(PE.sem, PE.n)]

        CTX, l_ctx = G[:, E0 + 5632:E0 + 9728], []

        def ctx_loads():
            for i in range(4):
                d = slice(1024 * i, 1024 * i + 1024)
                l_ctx.append(load(f"ctx{i}", CTX[:, d], io["ctx_t"][:, d], now()))
                for _ in range(8):
                    yield

        def mlp():
            for qn in range(3):
                yield from up(qn + 1, 0, 2)
                yield from down(qn)
                yield from up(qn + 1, 2, 2)

        rstd_later(sums_x2)
        beside = chain(ada_apart((0, 1, 4), (2.4, 2.4, 1.6), slots), ctx_loads())
        run(feeding(sums_x2, "norm_mlp", rm, lambda kt: x2_t, x2_free), up(0, 0, 4), beside=beside)
        for k in range(16, 24):
            hid_free[k] = now()
        run(mlp(), beside=beside)
        for _ in beside:
            pass
        state["rs"] = [(DV.sem, DV.n)]
        one = []
        for a in (16, 64, 96 + 16):
            one.append(DV(lambda e: e.tensor_scalar(MODT[:, a:a + 16], MODT[:, a:a + 16], 1.0, None, ALU.add), got["mod"]))

        base = now()
        l_cg = load("cg", G[:, E0:E0 + NCG], io["c_gla"], [base])
        bufs = [Place(G[:, E0 + 2048 + 512 * i:E0 + 2560 + 512 * i]) for i in range(4)]
        for b_ in bufs:
            b_.free = list(base)

        def cg(name):
            a, b = CG[name]
            return G[:, E0 + a:E0 + b]

        def modulate(src, sh, sc, tms, ready, free, out):
            for kt in range(0, 16, 2):
                tm = tms.next()
                for k in range(2):
                    t = DV(lambda e: e.tensor_scalar(tm.ap[:, k * 256:k * 256 + 256], src[:, (kt + k) * S:(kt + k + 1) * S],
                                                     sc(kt + k), sh(kt + k), ALU.mult, ALU.add),
                           ready[kt // 2], one, tm.free)
                d = slice(kt * S, kt * S + 512)
                t2 = split(AH[:, d], AL[:, d], tm.ap, t, free)
                tm.free = [t2]
                out[kt // 4].append(t2)
                yield

        sums = Sums(bufs[0], Ring([bufs[1]]))

        def squared(b, r):
            for i in range(2):
                kt = 4 * b + 2 * i
                sums.square(X[:, kt * S:kt * S + 512], r)

        def last_down():
            ready = [[hid_ready[(48 + 4 * c + k) % 24] for k in range(4)] for c in range(4)]

            def evac(b, bb, t):
                add_x(b, bb, t)
                squared(b, got["x"])
            yield from gemm("down", 12, 4, 4, ring24(HH, 3), ring24(HL, 3), ready, "T", evac)

        rc = [[] for _ in range(4)]
        run(last_down(), after(6, modulate(CTX, lambda kt: cmod(0, kt), lambda kt: cmod(1, kt), Ring(bufs[2:4]), [l_ctx[i // 2] for i in range(8)],
                                  [base], rc)))
        dbg("x3", X[:, :])
        dbg("mod", MODT[:, :])

        R = rstd(sums)
        x_ready = []
        for kt in range(16):
            t = DV(lambda e: e.scalar_tensor_tensor(X[:, kt * S:kt * S + S], X[:, kt * S:kt * S + S], par("final_norm", kt),
                                                    RS[:, 0:256], ALU.mult, ALU.mult), R)
            if kt % 2:
                x_ready.append(t)
        state["rs"] = [t]
        got["x"] = [t]
        dbg("x4", X[:, :])

        base = now()
        K, Q = G[:, 0:2048], G[:, 2048:4096]
        Vr = Ring([Place(G[:, 4096:5120]), Place(G[:, 5120:6144])])
        SS = Place(G[:, 6144:8192])
        Zr = Ring([Place(G[:, 8192:8704]), Place(G[:, E0 + 9472:E0 + 9984])])
        TM = [Place(G[:, 8704:9216]), Place(G[:, 9216:9728])]
        QN, KN, QA, KB, Q4 = (Place(G[:, 9728 + 512 * i:10240 + 512 * i]) for i in range(5))
        T0 = E0 + NCG
        K3, Q3 = Place(G[:, T0:T0 + 256]), Place(G[:, T0 + 256:T0 + 512])
        ATD = [Place(G[:, T0 + 512 + 128 * i:T0 + 640 + 128 * i]) for i in range(2)]
        AT = Place(G[:, T0 + 768:T0 + 1024])
        AT3 = [Place(G[:, T0 + 1024 + 128 * i:T0 + 1152 + 128 * i]) for i in range(2)]
        ON = [Place(G[:, T0 + 1280 + 512 * i:T0 + 1792 + 512 * i]) for i in range(2)]
        OT = G[:, T0 + 2304:T0 + 6400]
        modt = [Place(G[:, T0 + 6400 + 512 * i:T0 + 6912 + 512 * i]) for i in range(2)]
        assert T0 + 7424 <= E0 + 9472
        TD, GB = modt
        ALR = sb("ALR", 256)
        ET = [Place(SM[:, 8 * i:8 * i + 8]) for i in range(2)]
        PX = Place(SM[:, 16:24])
        PXS = (PX, Place(SM[:, 32:40]))
        places = Vr.places + [SS] + Zr.places + TM + [QN, KN, QA, KB, Q4, K3, Q3, AT, PX, PXS[1]] + ATD + AT3 + ON + modt + ET
        for pl in places:
            pl.free = list(base)
        kq = {"k": base, "q": base}
        spill = Load(sem("s_spill"))
        v8 = lambda ap: ap.rearrange("p (c t) -> p c t", c=8)
        k4 = lambda ap: ap.rearrange("p (k c t) -> p k c t", k=2, c=4)

        def bcast(small, n=8):
            return small.unsqueeze(2).to_broadcast([P, n, 64])

        def decay(d, h, alr_t):
            bk, z = misc.next(), Zr.next()
            for k in range(2):
                f = (2 * h + k) * 128
                t = PE(lambda e: e.matmul(bk.ap[:, k * 256:k * 256 + 256], cg("decay")[32 * d:32 * d + 32, f:f + 128],
                                          ALR[32 * d:32 * d + 32, :], start=True, stop=True, tile_position=(32 * d, 0)),
                       alr_t, bk.free, l_cg)
            for k in range(2):
                a = AC(lambda e: e.activation(z.ap[:, k * 256:k * 256 + 256], bk.ap[:, k * 256:k * 256 + 256], ACT.Identity,
                                              bias=par("b_decay", 8 * d + 2 * h + k)), t, z.free)
            bk.free = [a]
            b = DV(lambda e: e.scalar_tensor_tensor(TD.ap, z.ap, -1.0, z.ap, ALU.mult, ALU.min), a, TD.free)
            c = AC(lambda e: e.activation(TD.ap, TD.ap, ACT.Exp), b)
            c = AC(lambda e: e.activation(TD.ap, TD.ap, ACT.Ln, bias=1.0), c)
            a = DV(lambda e: e.scalar_tensor_tensor(z.ap, z.ap, 0.0, TD.ap, ALU.min, ALU.subtract), c)
            TD.free = [a]
            rev = (lambda ap: ap) if d == 0 else (lambda ap: ap[:, ::-1])
            t = DV(lambda e: e.tensor_tensor_scan(rev(z.ap), cg("scan"), rev(z.ap), 0.0, ALU.mult, ALU.add), a)
            return z, t

        def totals(d, z):
            zc = v8(z.ap)
            return zc[:, :, 63:64] if d == 0 else zc[:, :, 0:1]

        def chunk_factors(d, z, zt):
            et = ET[d]
            t = AC(lambda e: e.activation(et.ap, totals(d, z).rearrange("p c t -> p (c t)"), ACT.Exp, scale=1 / 16.0), zt, et.free)
            return et, t

        def products(et, et_t, towards_end, PX):
            e4, p4 = (ap.rearrange("p (k c) -> p k c", k=2) for ap in (et.ap, PX.ap))
            order_ = (3, 2, 1, 0) if towards_end else (0, 1, 2, 3)
            a = DV(lambda e: e.memset(p4[:, :, order_[0]:order_[0] + 1], 1.0), PX.free)
            for was, c in zip(order_, order_[1:]):
                a = DV(lambda e: e.tensor_tensor(p4[:, :, c:c + 1], p4[:, :, was:was + 1], e4[:, :, was:was + 1], ALU.mult), a, et_t)
            return a

        def towards(d, z, zt, src, src_t, out):
            tm = TM[1]
            a = DV(lambda e: e.tensor_tensor(v8(tm.ap), totals(d, z).to_broadcast([P, 8, 64]), v8(z.ap), ALU.subtract), zt, tm.free)
            b = AC(lambda e: e.activation(tm.ap, tm.ap, ACT.Exp, scale=1 / 16.0), a)
            c = DV(lambda e: e.tensor_tensor(out.ap, src, tm.ap, ALU.mult), b, src_t, out.free)
            tm.free = [c]
            return c

        def low_rank(ready, waits):
            bk = misc.next()
            t = small("alr", hA, lA, ready, bk)
            r = DV(lambda e: e.tensor_copy(ALR[:, :], bk.ap[:, 0:256]), t, waits)
            bk.free = [r]
            return r

        def to_k(dst, key, scale=1.0):
            def evac(b, bb, t):
                for i in range(2):
                    o = dst[:, b * 1024 + i * 512:b * 1024 + i * 512 + 512]
                    r = AC(lambda e: e.activation(o, bb[i].ap[:, :], ACT.Copy, scale=scale), t, kq[key])
                    bb[i].free = [r]
                    got.setdefault(key, []).append(r)
            return evac

        def v_block(h):
            v = Vr.next()
            v.ready = []

            def evac(b, bb, t):
                for i in range(2):
                    o = v.ap[:, i * 512:i * 512 + 512]
                    v.ready.append(AC(lambda e: e.activation(o, bb[i].ap[:, :], ACT.Copy), t, v.free))
                    bb[i].free = [v.ready[-1]]
            return v, gemm("v2", h, 1, 4, hA, lA, rc, "N", evac)

        def ctx_head(h, v, alr_t):
            zs = [decay(0, h, alr_t)]
            yield
            zs.append(decay(1, h, alr_t))
            yield
            kn = []
            for d, (z, zt) in enumerate(zs):
                full, norm = CH_BUF[d]
                et, et_t = chunk_factors(d, z, zt)
                p_t = products(et, et_t, d == 0, PXS[d])
                et.free = [p_t]
                ks = towards(d, z, zt, K[:, h * 512:h * 512 + 512], got["k"], full)
                z.free = [ks, et_t]
                ks = DV(lambda e: e.tensor_tensor(v8(norm.ap), v8(full.ap), bcast(PXS[d].ap), ALU.mult), ks, p_t, norm.free)
                PXS[d].free = full.free = [ks]
                kq["used"] = [ks]
                kn.append(ks)
                yield
            for d in range(2):
                full, norm = CH_BUF[d]
                bk = misc.next()
                for i in range(2):
                    for k in range(2):
                        t = PE(lambda e: e.transpose(bk.ap[:, i * 256 + k * 128:i * 256 + k * 128 + 128],
                                                     norm.ap[:, k * 256 + i * 128:k * 256 + i * 128 + 128], ident), kn[d], bk.free)
                norm.free = [t]
                kn[d] = DV(lambda e: e.tensor_copy(full.ap, bk.ap[:, :]), t, full.free)
                bk.free = [kn[d]]
                yield
            for d in range(2):
                full, norm = CH_BUF[d]
                for k in range(2):
                    bk = misc.next()
                    for i in range(2):
                        t = PE(lambda e: e.matmul(bk.ap[:, :], full.ap[:, i * 256 + k * 128:i * 256 + k * 128 + 128],
                                                  v.ap[:, i * 512:i * 512 + 512], start=i == 0, stop=i == 1), kn[d], v.ready, bk.free)
                    c = AC(lambda e: e.activation(SS.ap[:, d * 1024 + k * 512:d * 1024 + k * 512 + 512], bk.ap[:, :], ACT.Copy), t, SS.free)
                    bk.free = [c]
                full.free = [t]
                yield
            z = AC.dma(io["state"][h], SS.ap, spill, c)
            SS.free = [z]
            v.free = [t]

        CH_BUF = ((KB, KN), (QA, QN))
        got["k"], got["q"] = [], []
        ada_at["acc"][2] = [Place(Q)]
        ada_at["acc"][2][0].free = list(base)
        slots = [Place(OT[:, 0:2048]), Place(OT[:, 2048:4096])]
        for s_ in slots:
            s_.free = list(base)
        ada2 = ada_apart((2,), (1.25,), slots)
        alr_t = low_rank(rc, None)
        run(gemm("k2", 0, 2, 4, hA, lA, rc, "T", to_k(K, "k")), beside=ada2)
        v, gen = v_block(0)
        run(gen, beside=ada2)
        for h in range(4):
            if h == 3:
                for _ in ada2:
                    pass
                kq["q"] = now()
                nxt, gen = None, gemm("q2", 0, 2, 4, hA, lA, rl, "T", to_k(Q, "q", 1.0 / 16.0))
            else:
                nxt, gen = v_block(h + 1)
            run(ctx_head(h, v, alr_t), gen, beside=ada2)
            v = nxt
            if h == 2:
                free, rl = [(PE.sem, PE.n)], [[] for _ in range(4)]
                GB.free = TD.free = list(flat([GB.free, TD.free]))
                for _ in modulate(X, lambda kt: mod(0, kt), lambda kt: mod(1, kt), Ring([ON[0], ON[1]]), x_ready, free, rl):
                    pass

        for i in range(4):
            x = X[:, 1024 * i:1024 * i + 1024]
            a = AC(lambda e: e.activation(x, x, ACT.Copy, scale=ALPHA), rl[i], x_ready)
        got["x"] = [a]

        rc = rl
        alr_t = low_rank(rc, [(PE.sem, PE.n)])
        base = [(PE.sem, PE.n)]
        zs0 = decay(0, 0, alr_t)
        got["k"] = []
        kq["k"] = [kq["used"]]
        run(gemm("k2", 0, 2, 4, hA, lA, rc, "T", to_k(K, "k")))
        zero = [PO(lambda e: e.memset(pl.ap, 0.0), pl.free) for pl in ATD]
        for pl in ATD:
            pl.free = list(zero)
        MK = [sb(f"MK{d}", 64, U32) for d in range(2)]
        l_mk = [load(f"mk{d}", MK[d][:, :], io["masks"][d]) for d in range(2)]
        back = Load(sem("s_back"))
        ob = [banks[4], banks[5]]
        misc = Ring([banks[6], banks[7]])
        got["ot"] = [base]
        ot_free = now()

        def lat_head(h, v, zs):
            AC.wait([spill.all(), SS.free])
            lt = AC.dma(SS.ap, io["state"][h], back)
            PE.wait([ob[0].free, ob[1].free])
            first = [True, True]
            for d in range(2):
                z, zt = zs
                if d == 0:
                    zs = decay(1, h, alr_t)
                elif h < 3:
                    zs = decay(0, h + 1, alr_t)
                yield
                q, kk = Q[:, h * 512:h * 512 + 512], K[:, h * 512:h * 512 + 512]
                ref = v8(z.ap)[:, :, 31:32] if d == 0 else v8(z.ap)[:, :, 32:33]
                t0, t1 = TM
                a = DV(lambda e: e.tensor_tensor(v8(t0.ap), v8(z.ap), ref.to_broadcast([P, 8, 64]), ALU.subtract), zt, t0.free)
                b = AC(lambda e: e.activation(t1.ap, t0.ap, ACT.Exp, scale=1 / 16.0), a, t1.free)
                b2 = AC(lambda e: e.activation(t0.ap, t0.ap, ACT.Exp, scale=-1 / 16.0), a)
                qn = DV(lambda e: e.tensor_tensor(QN.ap, q, t1.ap, ALU.mult), b, got["q"], QN.free)
                t1.free = [qn]
                kn = DV(lambda e: e.tensor_tensor(KN.ap, kk, t0.ap, ALU.mult), b2, got["k"], KN.free)
                t0.free = [kn]
                et, et_t = chunk_factors(d, z, zt)
                yield
                a = AC(lambda e: e.activation(t0.ap, z.ap, ACT.Exp, scale=1 / 16.0), zt, t0.free)
                qa = DV(lambda e: e.tensor_tensor(QA.ap, q, t0.ap, ALU.mult), a, got["q"], QA.free)
                t0.free = [qa]
                kb = towards(d, z, zt, kk, got["k"], KB)
                z.free = [kb, et_t, qa]
                yield
                e4 = et.ap.rearrange("p (k c) -> p k c", k=2)
                tk, tq = (0, 1) if d == 0 else (1, 0)
                far = []
                for out, src, tile, src_t in ((K3, KB, tk, kb), (Q3, QA, tq, qa)):
                    o4 = out.ap.rearrange("p (k c t) -> p k c t", k=2, c=2)
                    near_c, far_c, f = (1, 0, 1) if tile == 0 else (2, 3, 2)
                    far.append(DV(lambda e: e.tensor_copy(o4[:, :, near_c % 2, :], k4(src.ap)[:, :, near_c, :]), src_t, out.free))
                    far.append(DV(lambda e: e.tensor_tensor(o4[:, :, far_c % 2, :], k4(src.ap)[:, :, far_c, :],
                                                            e4[:, :, f:f + 1].to_broadcast([P, 2, 64]), ALU.mult), src_t, et_t, out.free))
                p_t = products(et, et_t, d == 1, PX)
                q4 = DV(lambda e: e.tensor_tensor(v8(Q4.ap), v8(QA.ap), bcast(PX.ap), ALU.mult), p_t, qa, Q4.free)
                PX.free = [q4]
                et.free = [q4]
                yield
                bk = misc.next()
                parts = ((0, 0, 64), (32, 32, 32)) if d == 0 else ((32, 0, 64), (0, 0, 32))
                for c in range(4):
                    half = 64 * (c % 2)
                    for j0, i0, ni in parts:
                        for k in range(2):
                            o = k * 256 + c * 64
                            t = PE(lambda e: e.matmul(
                                bk.ap[half + j0:half + j0 + 32, (c // 2) * 64 + i0:(c // 2) * 64 + i0 + ni],
                                KN.ap[:, o + j0:o + j0 + 32], QN.ap[:, o + i0:o + i0 + ni],
                                start=k == 0, stop=k == 1, tile_position=(0, half + j0)), qn, kn, bk.free)
                QN.free = KN.free = [t]
                rk, rq = (0, 64) if d == 0 else (64, 0)
                for tile in range(2):
                    for k in range(2):
                        o = k * 256 + tile * 128
                        t = PE(lambda e: e.matmul(
                            bk.ap[rk:rk + 64, 128 + tile * 64:192 + tile * 64], KB.ap[:, o + rk:o + rk + 64],
                            QA.ap[:, o + rq:o + rq + 64], start=k == 0, stop=k == 1, tile_position=(0, rk)), kb, qa)
                KB.free, QA.free = [t, far], [t, far, q4]
                for k in range(2):
                    t = PE(lambda e: e.matmul(bk.ap[:, 256:384], K3.ap[:, k * 128:k * 128 + 128], Q3.ap[:, k * 128:k * 128 + 128],
                                              start=k == 0, stop=k == 1), far)
                K3.free = Q3.free = [t]
                dd = ATD[d]
                ad = dd.ap.rearrange("p (i t) -> p i t", i=2)
                pd = bk.ap[:, 0:128].rearrange("p (i t) -> p i t", i=2)
                for half in (0, 64):
                    for j0, i0, ni in parts:
                        r, q_ = slice(half + j0, half + j0 + 32), slice(i0, i0 + ni)
                        c = DV(lambda e: e.copy_predicated(ad[r, :, q_], MK[d][r, q_].unsqueeze(1).to_broadcast([32, 2, ni]),
                                                           pd[r, :, q_]), t, l_mk, dd.free)
                at = AT.ap.rearrange("p (i t) -> p i t", i=2)
                c2 = DV(lambda e: e.tensor_copy(at[rk:rk + 64, :, rq:rq + 64],
                                                bk.ap[rk:rk + 64, 128:256].rearrange("p (i t) -> p i t", i=2)), t, AT.free)
                c3 = DV(lambda e: e.tensor_copy(AT3[d].ap, bk.ap[:, 256:384]), t, AT3[d].free)
                bk.free = [c3]
                yield
                for i in range(2):
                    for k in range(2):
                        s_ap = SS.ap[:, d * 1024 + k * 512:d * 1024 + k * 512 + 512]
                        t = PE(lambda e: e.matmul(ob[i].ap[:, :], Q4.ap[:, k * 256 + i * 128:k * 256 + i * 128 + 128], s_ap,
                                                  start=first[i], stop=False, skip_group_check=True), q4, lt)
                        first[i] = False
                Q4.free = [t]
                yield
            SS.free = [t]
            kq["used"] = [kn, kb]
            ds = []
            for r in (slice(0, 64), slice(64, 128)):
                ds.append(DV(lambda e: e.tensor_tensor(at[r, :, r], ATD[0].ap.rearrange("p (i t) -> p i t", i=2)[r, :, :],
                                                       ATD[1].ap.rearrange("p (i t) -> p i t", i=2)[r, :, :], ALU.add), c, AT.free))
            ATD[0].free = ATD[1].free = [ds[-1]]
            for i in range(2):
                t = PE(lambda e: e.matmul(ob[i].ap[:, :], AT.ap[:, i * 128:i * 128 + 128], v.ap[:, i * 512:i * 512 + 512],
                                          start=False, stop=False, skip_group_check=True), ds, c2, c3, v.ready)
                t = PE(lambda e: e.matmul(ob[i].ap[:, :], AT3[1 - i].ap, v.ap[:, (1 - i) * 512:(1 - i) * 512 + 512],
                                          start=False, stop=True, skip_group_check=True), c3)
            AT.free = AT3[0].free = AT3[1].free = [t]
            v.free = [t]
            yield
            ready = []
            for i in range(2):
                o = 24 + 4 * i
                a = AC(lambda e: e.activation(ON[i].ap, ob[i].ap[:, :], ACT.Square, accum_out=SM[:, o:o + 1]), t, ON[i].free)
                b = DV(lambda e: e.tensor_scalar(SM[:, o + 1:o + 2], SM[:, o:o + 1], 1.0 / 512, 1e-6, ALU.mult, ALU.add), a)
                b = AC(lambda e: e.activation(SM[:, o + 2:o + 3], SM[:, o + 1:o + 2], ACT.Sqrt), b)
                b = DV(lambda e: e.reciprocal(SM[:, o + 3:o + 4], SM[:, o + 2:o + 3]), b)
                c = DV(lambda e: e.tensor_scalar(ON[i].ap, ob[i].ap[:, :], SM[:, o + 3:o + 4], None, ALU.mult), b)
                ob[i].free = [c]
                ready.append(c)
            yield
            for j in range(2):
                bk = misc.next()
                for k in range(2):
                    for i in range(2):
                        f = (2 * j + k) * 128
                        t = PE(lambda e: e.transpose(bk.ap[:, k * 256 + i * 128:k * 256 + i * 128 + 128],
                                                     ON[i].ap[:, f:f + 128], ident), ready[i], bk.free)
                for k in range(2):
                    ft = 4 * h + 2 * j + k
                    c = DV(lambda e: e.tensor_scalar(OT[:, ft * 256:ft * 256 + 256], bk.ap[:, k * 256:k * 256 + 256],
                                                     par("gla_gain", ft), None, ALU.mult), t, ot_free)
                bk.free = [c]
                yield
            ON[0].free = ON[1].free = [t]
            got["ot"] = [c]
            got["next"] = zs

        kept = Load(sem("s_kept"))

        def gates_kept(b0, nb):
            def evac(b, bb, t):
                for i in range(2):
                    a = AC(lambda e: e.activation(GB.ap, bb[i].ap[:, :], ACT.Sigmoid), t, GB.free)
                    bb[i].free = [a]
                    GB.free = [AC.dma(io["gate"][b0 + b][:, i * 512:i * 512 + 512], GB.ap, kept, a)]
            yield from gemm("bg2", b0, nb, 4, hA, lA, rc, "T", evac)

        v, gen = v_block(0)
        run(gen)
        zs = zs0
        for h in range(4):
            nxt, gen = (None, iter(())) if h == 3 else v_block(h + 1)

            def beside(gen=gen, h=h):
                yield from gen
                yield from gates_kept(2 * h, 2)
            run(slow(lat_head(h, v, zs), 1.25 if h == 3 else 1.85), beside())
            zs, v = got["next"], nxt
        dbg("ot", OT)
        misc = Ring(banks[4:8])

        base = now()

        def BG(i, n):
            b = (16 if i < 8 else 24 + 16) * S + (i % 8) * S
            return G[:, b:b + n * S]

        tm2 = Ring([Place(G[:, E0 + 512 * i:E0 + 512 + 512 * i]) for i in range(3)])
        for s in tm2.places:
            s.free = list(base)

        got["y"] = []

        def g_evac(b, bb, t):
            held = []
            for i in range(2):
                tm = tm2.next()
                a = AC(lambda e, tm=tm, s=bb[i]: e.activation(tm.ap, s.ap[:, :], ACT.Silu), t, tm.free)
                bb[i].free = [a]
                d = slice(b * 1024 + i * 512, b * 1024 + i * 512 + 512)
                held.append((d, tm, DV(lambda e, tm=tm, d=d: e.tensor_tensor(tm.ap, tm.ap, OT[:, d], ALU.mult), a, got["ot"])))

            def parts():
                for d, tm, m in held:
                    z = split(HH[:, d], HL[:, d], tm.ap, m, base)
                    tm.free = [z]
                    got["y"].append(z)
            return [parts]

        l_bg = Load(sem("s_l_bg"))
        AC.wait([kept.all(), base])
        for b in range(4):
            AC.dma(BG(4 * b, 4), io["gate"][b], l_bg)
        got["bg"] = [l_bg.all()]
        run(gemm("g2", 0, 4, 4, hA, lA, rc, "T", g_evac))
        PN = G[:, E0 + 1536:E0 + 1536 + 2048]
        PM = G[:, E0 + 3584:E0 + 5632].rearrange("p (w i t) -> p w i t", w=4, i=2)
        PG = G[:, E0 + 5632:E0 + 7680].rearrange("p (k w n) -> p k w n", k=2, w=4)
        l_cp, cp_free = [], [got["y"]]

        def cp_loads():
            for i in range(4):
                d = slice(1024 * i, 1024 * i + 1024)
                l_cp.append(load(f"cp{i}", G[:, E0 + 3584:E0 + 7680][:, d], io["c_pool"][:, d], [cp_free, (PE.sem, PE.n)]))
                for _ in range(3):
                    yield

        ada_at["acc"][3] = [Place(G[:, E0 + 7680:E0 + 9728])]
        ada_at["acc"][3][0].free = now()

        def y_evac(b, bb, t):
            for i in range(2):
                o = BG(4 * b + 2 * i, 2)
                r = DV(lambda e, o=o, s=bb[i]: e.tensor_tensor(o, s.ap[:, :], o, ALU.mult), t, got["bg"])
                bb[i].free = [r]
            got["yg"] = [r]

        got["pn"] = []

        def pn_evac(b, bb, t):
            for i in range(2):
                o = PN[:, i * 1024 + b * 512:i * 1024 + b * 512 + 512]
                r = DV(lambda e, o=o, s=bb[i]: e.tensor_copy(o, s.ap[:, :]), t)
                bb[i].free = [r]
                got["pn"].append(r)

        def BP(i, n):
            return G[:, E0 + 3584 + i * S:E0 + 3584 + (i + n) * S]

        got["pp"] = []
        l_bp = Load(sem("s_l_bp"))

        def pool():
            for w in range(4):
                bk = misc.next()
                for k in range(2):
                    for i in range(2):
                        t = PE(lambda e, w=w, k=k, i=i, bk=bk: e.matmul(
                            bk.ap[:, k * 256:k * 256 + 256], PN[:, i * 1024 + (2 * w + k) * 128:i * 1024 + (2 * w + k) * 128 + 128],
                            PM[:, w, i, :], start=i == 0, stop=i == 1), got["pn"], l_cp, bk.free)
                tm = tm2.next()
                a = AC(lambda e, tm=tm, bk=bk: e.activation(tm.ap, bk.ap[:, :], ACT.Copy), t, tm.free)
                bk.free = [a]
                yield
                bk = misc.next()
                for m in range(2):
                    for k in range(2):
                        t = PE(lambda e, w=w, k=k, m=m, bk=bk, tm=tm: e.matmul(
                            bk.ap[:, m * 256:m * 256 + 256], PG[:, k, w, m * 128:m * 128 + 128], tm.ap[:, k * 256:k * 256 + 256],
                            start=k == 0, stop=k == 1), a, bk.free)
                tm.free = [t]
                tm = tm2.next()
                for m in range(2):
                    b = DV(lambda e, m=m, w=w, tm=tm, bk=bk: e.tensor_scalar(tm.ap[:, m * 256:m * 256 + 256], bk.ap[:, m * 256:m * 256 + 256],
                                                                            par("pool_scale", 2 * w + m), None, ALU.mult), t, tm.free)
                bk.free = [b]
                d = slice(w * 512, w * 512 + 512)
                z = split(AH[:, d], AL[:, d], tm.ap, b, got["p_done"])
                tm.free = [z]
                got["pp"].append(z)
                yield
            AC.wait([(PE.sem, PE.n)])
            for b in range(4):
                AC.dma(BP(4 * b, 4), io["gate"][4 + b], l_bp)
            got["bp"] = [l_bp.all()]

        got["m"] = []

        def merge_evac(b, bb, t):
            held = []
            for i in range(2):
                tm = tm2.next()
                r = DV(lambda e, tm=tm, s=bb[i], o=BP(4 * b + 2 * i, 2): e.tensor_tensor(tm.ap, s.ap[:, :], o, ALU.mult), t, got["bp"], tm.free)
                bb[i].free = [r]
                r = DV(lambda e, tm=tm, o=BG(4 * b + 2 * i, 2): e.tensor_tensor(tm.ap, tm.ap, o, ALU.add), r, got["yg"])
                held.append((slice(b * 1024 + i * 512, b * 1024 + i * 512 + 512), tm, r))

            def parts():
                for d, tm, r in held:
                    z = split(HH[:, d], HL[:, d], tm.ap, r, got["y_done"])
                    tm.free = [z]
                    got["m"].append(z)
            return [parts]

        def merge():
            yield from gemm("p2", 0, 2, 4, hA, lA, rc, "N", pn_evac)
            got["p_done"] = [(PE.sem, PE.n)]
            yield from both(pool(), gemm("gout", 0, 4, 4, ap_of(HH), ap_of(HL), [got["y"][2 * c:2 * c + 2] for c in range(4)], "T", y_evac))
            got["y_done"] = [(PE.sem, PE.n), got["yg"]]
            yield from gemm("pout", 0, 4, 2, hA, lA, [got["pp"][0:2], got["pp"][2:4]], "T", merge_evac)

        slots = [Place(AF[:, a:a + 2048]) for a in (2048, 6144)]

        def beside_merge():
            while "p_done" not in got:
                yield
            for s_ in slots:
                s_.free = list(got["p_done"])
            yield from ada_apart((3,), (2.0,), slots)

        ada3 = beside_merge()
        run(merge(), cp_loads(), beside=ada3)

        class Norm:

            def __init__(self):
                self.sums, self.squares = Sums(bufs[0], None), Sums(bufs[3], Ring(bufs[1:3]))

            def shift(self):
                bk, t = self.sums.over_partitions()
                self.m0 = AC(lambda e: e.activation(RS[:, 0:256], bk.ap[:, 0:256], ACT.Copy, scale=1.0 / 1536), t, state["rs"])
                bk.free = [self.m0]

            def shifted(self, kts):
                out = []
                for kt, t in kts:
                    x = X[:, kt * S:kt * S + 512]
                    out.append((x, DV(lambda e: e.tensor_tensor(pair2(x), pair2(x), R2, ALU.subtract), self.m0, t)))
                return out

            def squared(self, kts):
                for x, t in self.shifted(kts):
                    self.squares.square(x, t)

            def added(self, b, kts):
                if b < 3:
                    for kt, t in kts:
                        self.sums.plain(X[:, kt * S:kt * S + 512], t)
                    self.kts = (self.kts if b else []) + kts
                    if b == 2:
                        return [self.shift] + [lambda p=p: self.squared(self.kts[p:p + 2]) for p in (0, 2, 4)]
                else:
                    self.rest = [(x, t, tm, AC(lambda e: e.activation(tm.ap, x, ACT.Square), t, tm.free))
                                 for (x, t), tm in zip(self.shifted(kts), self.squares.tmps.places)]
                return []

            def finish(self):
                bk = misc.next()
                for i, (x, t, _, _) in enumerate(self.rest):
                    for k in range(2):
                        t = PE(lambda e: e.matmul(bk.ap[:, 0:256], ones, x[:, k * S:k * S + S], start=i == k == 0, stop=i == k == 1),
                               t, bk.free)
                b2 = misc.next()
                parts = [(self.squares.acc.ap, self.squares.t)] + [(tm.ap, a) for _, _, tm, a in self.rest]
                for i, (x, a) in enumerate(parts):
                    for k in range(2):
                        t2 = PE(lambda e: e.matmul(b2.ap[:, 0:256], ones, x[:, k * S:k * S + S], start=i == k == 0, stop=i == 2 and k == 1),
                                a, b2.free)
                self.squares.acc.free = [t2]
                for _, _, tm, _ in self.rest:
                    tm.free = [t2]
                d_, w = RS[:, 256:512], RS[:, 512:768]
                d = DV(lambda e: e.tensor_scalar(d_, bk.ap[:, 0:256], 1.0 / D, None, ALU.mult), t, state["rs"])
                bk.free = [d]
                r = DV(lambda e: e.tensor_tensor(w, d_, d_, ALU.mult), d)
                tm = self.sums.acc
                q = DV(lambda e: e.tensor_scalar(tm.ap[:, 0:256], b2.ap[:, 0:256], 1.0 / D, 1e-5, ALU.mult, ALU.add), t2, tm.free)
                b2.free = [q]
                r = DV(lambda e: e.tensor_tensor(w, tm.ap[:, 0:256], w, ALU.subtract), q, r)
                r = AC(lambda e: e.activation(w, w, ACT.Sqrt), r)
                r = DV(lambda e: e.reciprocal(RS[:, 0:256], w), r)
                D2 = d_.unsqueeze(1).to_broadcast([P, 2, 256])
                for kt in range(0, 16, 2):
                    x = X[:, kt * S:kt * S + 512]
                    t = DV(lambda e: e.tensor_tensor(pair2(x), pair2(x), D2, ALU.subtract), r)
                    t = DV(lambda e: e.tensor_tensor(pair2(x), pair2(x), R2, ALU.mult), t)
                    state["rs"] = [t]
                    yield kt, t

        def gated_x(which):
            def evac(b, bb, t):
                kts = []
                for i in range(2):
                    for m in range(2):
                        kt = 4 * b + 2 * i + m
                        x = X[:, kt * S:kt * S + S]
                        r = DV(lambda e, x=x, kt=kt, m=m, s=bb[i]: e.scalar_tensor_tensor(
                            x, s.ap[:, m * 256:m * 256 + 256], mod(which, kt), x, ALU.mult, ALU.add), t, got["x"], got["mod"])
                    bb[i].free = [r]
                    kts.append((kt - 1, r))
                return norm.added(b, kts)
            return evac

        bufs = [Place(G[:, E0 + 4608 + 512 * i:E0 + 5120 + 512 * i]) for i in range(6)]
        base = now()
        for b_ in bufs:
            b_.free = list(base)
        norm = Norm()
        run(gemm("out2", 0, 4, 4, ap_of(HH), ap_of(HL), [got["m"][2 * c:2 * c + 2] for c in range(4)], "T", gated_x(2)), beside=ada3)
        for _ in ada3:
            pass

        GS, BS, GA, BA = (SM[:, 64 + 16 * i:80 + 16 * i] for i in range(4))
        c1 = DV(lambda e: e.tensor_tensor(GS, par("lnm_g"), MODT[:, 64:80], ALU.mult), got["mod"], one)
        c2 = DV(lambda e: e.tensor_tensor(BS, par("lnm_b"), MODT[:, 64:80], ALU.mult), got["mod"], one)
        c2 = DV(lambda e: e.tensor_tensor(BS, BS, MODT[:, 48:64], ALU.add), c2, got["mod"])
        c3 = DV(lambda e: e.tensor_scalar(GA, par("lnm_g"), ALPHA, None, ALU.mult))
        c4 = DV(lambda e: e.tensor_scalar(BA, par("lnm_b"), ALPHA, None, ALU.mult))
        rf, tms, free = [[] for _ in range(4)], Ring(bufs[4:6]), [(PE.sem, PE.n)]
        got["x"] = []

        def modulated(norm):
            marks = []
            for kt, t in norm.finish():
                tm = tms.next()
                for k in range(2):
                    a = DV(lambda e: e.tensor_scalar(tm.ap[:, k * S:k * S + S], X[:, (kt + k) * S:(kt + k + 1) * S],
                                                     GS[:, kt + k:kt + k + 1], BS[:, kt + k:kt + k + 1], ALU.mult, ALU.add),
                           t, tm.free, c1, c2)
                d = slice(kt * S, kt * S + 512)
                z = split(AH[:, d], AL[:, d], tm.ap, a, free)
                tm.free = [z]
                rf[kt // 4].append(z)
                marks.append(a)
                yield
            for kt in range(16):
                x = X[:, kt * S:kt * S + S]
                a = DV(lambda e: e.tensor_scalar(x, x, GA[:, kt:kt + 1], BA[:, kt:kt + 1], ALU.mult, ALU.add), marks[kt // 2], c3, c4)
                got["x"] = [a]
                if kt % 2:
                    yield

        hid_free = [now()] * 24
        silu_tm = Ring([Place(G[:, E0 + 512 * i:E0 + 512 + 512 * i]) for i in range(3)])
        for s_ in silu_tm.places:
            s_.free = now()

        def ffn_up(b0, nb):
            def evac(b, bb, t):
                kt = (2 * (b0 + b)) % 24
                tm = silu_tm.next()
                a = AC(lambda e, tm=tm: e.activation(tm.ap, bb[0].ap[:, :], ACT.Silu), t, tm.free)
                bb[0].free = [a]
                m = DV(lambda e, tm=tm: e.tensor_tensor(tm.ap, bb[1].ap[:, :], tm.ap, ALU.mult), a, t)
                bb[1].free = [m]

                def parts():
                    d = slice(kt * S, kt * S + 512)
                    z = split(HH[:, d], HL[:, d], tm.ap, m, hid_free[kt])
                    tm.free = [z]
                    hid_ready[kt] = hid_ready[kt + 1] = z
                return [parts]
            yield from gemm("fin", b0, nb, 4, hA, lA, rf, "T", evac)

        PARTS = [(0, 16), (16, 16), (32, 12)]

        def ffn_down(part):
            a, n = PARTS[part]

            def evac(b, bb, t):
                kts = []
                for i in range(2):
                    for m in range(2):
                        kt = 4 * b + 2 * i + m
                        x = X[:, kt * S:kt * S + S]
                        r = DV(lambda e, x=x, kt=kt, m=m, s=bb[i]: e.scalar_tensor_tensor(
                            x, s.ap[:, m * 256:m * 256 + 256], mod(5, kt), x, ALU.mult, ALU.add), t, got["x"], got["mod"])
                    bb[i].free = [r]
                    kts.append((kt - 1, r))
                return norm.added(b, kts) if part == 2 else None
            ready = [[hid_ready[(a + 4 * c + k) % 24] for k in range(4)] for c in range(n // 4)]
            yield from gemm(f"fout{part}", 0, 4, n // 4, lambda kt: HH[:, ((a + kt) % 24) * S:((a + kt) % 24 + 1) * S],
                            lambda kt: HL[:, ((a + kt) % 24) * S:((a + kt) % 24 + 1) * S], ready, "T", evac)
            got["x"] = [(DV.sem, DV.n)]
            for k in range(n):
                hid_free[(a + k) % 24] = [(PE.sem, PE.n)]

        def ffn():
            yield from ffn_up(0, 8)
            yield from ffn_up(8, 4)
            yield from ffn_down(0)
            yield from ffn_up(12, 4)
            yield from ffn_up(16, 4)
            yield from ffn_down(1)
            yield from ffn_up(20, 2)
            for b_ in bufs[0:4]:
                b_.free = now()
            yield from ffn_down(2)

        first, norm = norm, Norm()
        ada_at["acc"][5] = [Place(G[:, E0 + 7680:E0 + 9728])]
        ada_at["acc"][5][0].free = now()
        slots = [Place(G[:, E0 + 1536 + 2048 * i:E0 + 3584 + 2048 * i]) for i in range(2)]

        def ada5():
            for _ in range(10):
                yield
            for s_ in slots:
                s_.free = now()
            yield from ada_apart((5,), (2.2,), slots)
        run(modulated(first), ffn(), ada5())
        dbg("x7", X[:, :])
        o = Load(sem("s_out"))
        for kt, t in norm.finish():
            for k in (kt, kt + 1):
                x = X[:, k * S:k * S + S]
                t = AC(lambda e: e.activation(x, x, ACT.Identity, scale=par("lnf_g", k), bias=par("lnf_b", k)), t)
            if kt % 4:
                d = slice((kt - 2) * S, (kt + 2) * S)
                SP.dma(io["out"][:, d], X[:, d], o, t)
        SP.wait([o.all(), spill.all(), kept.all()])
        if debug:
            PO.wait([dbg_load.all()])

        if order is None:
            return found
        assert found == order
    return found


def blocks(w, kt=4, width=512):
    k, n = w.shape
    v = w.reshape(k // (P * kt), kt, P, n // width, width)
    return np.ascontiguousarray(v.transpose(3, 0, 2, 1, 4)).reshape(-1, P, kt * width)


def columns(v):
    return v.reshape(-1, P).T


def tokens(x):
    return np.ascontiguousarray(x.reshape(S, -1, P).transpose(2, 1, 0)).reshape(P, -1)


def constants():
    t = np.arange(S)
    dist = t[:, None] - t[None, :]
    count = (((dist >= 0) & (dist <= 128)).astype(np.float64) + ((dist >= 0) & (dist % 4 == 0) & (dist // 4 <= 128))
             + ((dist >= 0) & (dist % 16 == 0) & (dist // 16 <= 128)))
    dil = np.where(count > 0, np.log(np.maximum(count, 1)), NEG).astype(np.float32)
    cau = np.where(dist >= 0, 0.0, NEG).astype(np.float32)
    end = np.arange(15) * 16 + 31
    valid = end[None, :] <= t[:, None]
    bcmp = np.where(valid, 0.0, NEG).astype(np.float32)
    rows = lambda a: a.reshape(2, P, -1).transpose(1, 0, 2).reshape(P, -1)
    pad = lambda a: np.pad(a, ((0, 0), (0, 32 - a.shape[1])))
    tri = (np.arange(P)[:, None] <= np.arange(P)[None, :]).astype(np.float32)
    mean = np.zeros((4, S, S))
    for i, w in enumerate((2, 4, 8, 16)):
        def axis(n):
            m = np.zeros((n, n))
            for a in range(n):
                lo, hi = max(a - w // 2, 0), min(a + w - w // 2, n)
                m[a, lo:hi] = 1.0 / (hi - lo)
            return m
        mean[i] = np.kron(axis(4), axis(64)) - np.eye(S)
    pm = mean.transpose(2, 0, 1).reshape(2, P, 4, S).transpose(1, 2, 0, 3).reshape(P, -1).astype(np.float32)
    scan = np.ones(512, np.float32)
    scan[::64] = 0
    scan_all = np.ones(512, np.float32)
    scan_all[::256] = 0
    j, i = np.arange(64)[:, None], np.arange(64)[None, :]
    masks = np.stack([np.tile((j <= i).astype(np.uint32), (2, 1)), np.tile((j >= i).astype(np.uint32), (2, 1))])
    return dict(dil=rows(dil), cau=rows(cau), bcmp=pad(rows(bcmp)), vcmp=pad(rows(valid.astype(np.float32))), tri=tri,
                pm=pm, scan=np.tile(scan, (P, 1)), scan_all=np.tile(scan_all, (P, 1)), masks=masks)


def layout(a):
    k = constants()
    wi, w2 = a["w_in"][0], a["w_in_2"][0]
    cat = np.concatenate
    cols = cat([wi[:, 0:1024], wi[:, 3584:4096], wi[:, 1024:2048], wi[:, 2048:2560], wi[:, 2560:3584],
                wi[:, 4096:4352], wi[:, 4608:4864], wi[:, 4352:4608], wi[:, 4864:5120]], axis=1)
    gates = np.zeros((D, 128), np.float32)
    gates[:, 0:24] = wi[:, 5120:5144]
    alr = np.zeros((D, 128), np.float32)
    alr[:, 0:16] = w2[:, 6144:6160]
    alr[:, 32:48] = w2[:, 6160:6176]
    dn = a["w_down"][0]
    fi, fo = a["w_ffn_in_2"][0], a["w_ffn_out_2"][0]
    pair = cat([x for b in range(22) for x in (fi[:, 256 * b:256 * b + 256], fi[:, 5632 + 256 * b:5632 + 256 * b + 256])], axis=1)
    ada = a["w_ada_2"][0].reshape(16, P, 6, CH).transpose(2, 0, 1, 3).reshape(96, P, CH)
    out = {
        "w_in": blocks(cols), "w_gates": blocks(gates, 16, 128), "w_alr": blocks(alr, 16, 128),
        "w_ck": blocks(a["cmp_k_w1"][0], 16, 128), "w_cv": blocks(a["cmp_v_w1"][0], 16, 128),
        "w_outa": blocks(a["w_out"][0][0:1024]), "w_outb": blocks(a["w_out"][0][1024:2048]), "w_xkv": blocks(a["xattn_wkv"][0]), "w_xq": blocks(a["xattn_wq"][0]),
        "w_xo": blocks(a["xattn_wo"][0]), "w_up": blocks(a["w_up"][0]),
        "w_down": cat([blocks(dn[2048 * q:2048 * q + 2048]) for q in range(4)]),
        "w_ada": np.ascontiguousarray(ada),
        "w_q2": blocks(w2[:, 0:1024]), "w_k2": blocks(w2[:, 1024:2048]), "w_v2": blocks(w2[:, 2048:4096]),
        "w_g2": blocks(w2[:, 4096:6144]), "w_p2": blocks(w2[:, 6176:7200]), "w_bg2": blocks(w2[:, 7200:11296]),
        "w_gout": blocks(a["w_gla_out_2"][0]), "w_pout": blocks(a["w_pool_out_2"][0]), "w_out2": blocks(a["w_out_2"][0]),
        "w_fin": blocks(pair), "w_fout0": blocks(fo[0:2048]), "w_fout1": blocks(fo[2048:4096]), "w_fout2": blocks(fo[4096:5632]),
    }
    small = cat([columns(np.asarray(x).reshape(-1)) for x in (
        a["norm_mix"], a["norm_xattn"], a["norm_mem"], a["norm_mlp"], a["final_norm"], a["b_ada_2"], a["gla_norm_gain_2"],
        a["pool_scale_2"], a["ln_mix_gain_2"], a["ln_mix_bias_2"], a["ln_ffn_gain_2"], a["ln_ffn_bias_2"], a["b_decay_up_2"],
        a["c_2"], a["c_ctx_2"])], axis=1)
    out["c_base"] = cat([np.eye(P, dtype=np.float32), np.ones((P, P), np.float32), small], axis=1)
    row = lambda v: np.tile(np.asarray(v).reshape(1, -1), (P, 1))
    ws = a["gmlp_w_s"][0].transpose(2, 0, 1).reshape(P, -1)
    out["c_attn"] = cat([k["dil"], k["cau"], k["bcmp"], k["vcmp"], row(a["gmlp_ln_g"]), row(a["gmlp_ln_b"]), row(a["gmlp_b_s"]), ws,
                         k["tri"], a["cmp_pos"][0].T, a["cmp_k_w2"][0], a["cmp_v_w2"][0]], axis=1)
    dec = np.zeros((P, 1024), np.float32)
    dec[0:16] = a["w_decay_up_2"][0, 0]
    dec[32:48] = a["w_decay_up_2"][0, 1]
    out["c_gla"] = cat([k["scan"], k["scan_all"], dec], axis=1)
    pg = a["w_pool_group_2"][0].reshape(4, 2, P, 256).transpose(2, 1, 0, 3).reshape(P, -1)
    out["c_pool"] = cat([k["pm"], pg], axis=1)
    out["masks"] = k["masks"]
    out["x_t"], out["mem_t"], out["ctx_t"] = tokens(a["x"][0]), tokens(a["mem"][0]), tokens(a["ctx_2"][0])
    return {n: np.ascontiguousarray(v) for n, v in out.items()}


def build(nc, shapes, debug=()):
    dts = {"float32": F32, "uint32": U32}
    io = {n: nc.dram_tensor(f"in_{n}", list(s), dts[d], kind="ExternalInput").ap() for n, (s, d) in shapes.items()}
    io["out"] = nc.dram_tensor("out_0", [P, KT * S], F32, kind="ExternalOutput").ap()
    io["state"] = nc.dram_tensor("state", [4, P, 2048], F32).ap()
    io["gate"] = nc.dram_tensor("gate", [8, P, 1024], F32).ap()
    dbg = {n: nc.dram_tensor("dbg_" + n, [P, w], F32, kind="ExternalOutput").ap() for n, w in debug}
    return io, dbg


def kernel(**inputs):
    from concourse import bacc
    from concourse.bass_utils import run_bass_kernel_spmd

    arrays = layout({n: np.asarray(v) for n, v in inputs.items()})
    shapes = {n: (v.shape, v.dtype.name) for n, v in arrays.items()}
    dry = bacc.Bacc("TRN2", target_bir_lowering=False, num_devices=1)
    order = program(dry, build(dry, shapes)[0], None)
    nc = bacc.Bacc("TRN2", target_bir_lowering=False, num_devices=1)
    program(nc, build(nc, shapes)[0], order)
    r = run_bass_kernel_spmd(nc, [{f"in_{n}": v for n, v in arrays.items()}], core_ids=[0])
    got = r.results[0]["out_0"]
    return np.ascontiguousarray(got.reshape(P, KT, S).transpose(2, 1, 0)).reshape(1, S, D)
```
